# Optimizing a Trainium2 kernel written in Bass

```python
import math
import jax, jax.numpy as jnp
from jax import lax
import numpy as np

D_MODEL = 1024
BATCH = 1
SEQ = 1024
DEPTH = 1

ATTN_Q_HEADS = 8
ATTN_KV_HEADS = 2
HEAD_DIM = 64
ATTN_WIDTH = ATTN_Q_HEADS * HEAD_DIM
KV_WIDTH = ATTN_KV_HEADS * HEAD_DIM
WINDOW = 128
ATTN_BLOCK = 128
N_REL_BUCKETS = 32
REL_MAX_DISTANCE = 128

SSM_HEADS = 8
SSM_HEAD_DIM = 64
SSM_WIDTH = SSM_HEADS * SSM_HEAD_DIM
SSM_STATE = 128
SSM_GROUPS = 2
SSM_BC = SSM_GROUPS * SSM_STATE
SSM_CONV = 4
SSM_CHUNK = 256

MIX_WIDTH = ATTN_WIDTH + SSM_WIDTH
IN_SPLITS = (ATTN_WIDTH, KV_WIDTH, KV_WIDTH, SSM_WIDTH, SSM_WIDTH, SSM_BC, SSM_BC, SSM_HEADS)
IN_PROJ_WIDTH = sum(IN_SPLITS)

D_FF = 2816
FFN_CONV = 3

NORM_EPS = 1e-6
N_MOD = 6

kernel_name = "hymba_swa_sink_ssd_convffn_adaln"

def _split_last(t, sizes):
    points = np.cumsum(sizes)[:-1].tolist()
    return jnp.split(t, points, axis=-1)

def rms_norm(x, w):
    xf = x.astype(jnp.float32)
    y = xf * lax.rsqrt(jnp.mean(xf * xf, axis=-1, keepdims=True) + NORM_EPS)
    return (y * w.astype(jnp.float32)).astype(x.dtype)

def causal_dwconv(x, w, b):
    k = w.shape[0]
    y = lax.conv_general_dilated(
        x, w[:, None, :].astype(x.dtype), window_strides=(1,), padding=[(k - 1, 0)],
        dimension_numbers=("NWC", "WIO", "NWC"), feature_group_count=x.shape[-1])
    return y + b.astype(x.dtype)

def t5_causal_bucket(dist):
    max_exact = N_REL_BUCKETS // 2
    nf = jnp.maximum(dist, 1).astype(jnp.float32)
    large = max_exact + (jnp.log(nf / max_exact) / math.log(REL_MAX_DISTANCE / max_exact)
                         * (N_REL_BUCKETS - max_exact)).astype(jnp.int32)
    large = jnp.minimum(large, N_REL_BUCKETS - 1)
    return jnp.where(dist < max_exact, dist, large)

def sliding_window_attention(q, k, v, rel_bias, sinks):
    bsz, s = q.shape[0], q.shape[1]
    L = ATTN_BLOCK
    nb = s // L
    g = ATTN_Q_HEADS // ATTN_KV_HEADS
    qb = q.reshape(bsz, nb, L, ATTN_KV_HEADS, g, HEAD_DIM)

    def band_keys(t):
        prev = jnp.pad(t, ((0, 0), (L, 0), (0, 0), (0, 0)))[:, :s]
        prev = prev.reshape(bsz, nb, L, ATTN_KV_HEADS, HEAD_DIM)
        cur = t.reshape(bsz, nb, L, ATTN_KV_HEADS, HEAD_DIM)
        return jnp.concatenate([prev, cur], axis=2)

    kb, vb = band_keys(k), band_keys(v)
    qi = jnp.arange(L, dtype=jnp.int32)[:, None] + L
    kj = jnp.arange(2 * L, dtype=jnp.int32)[None, :]
    dist = qi - kj
    band = (dist >= 0) & (dist < WINDOW)
    blk = jnp.arange(nb, dtype=jnp.int32)[:, None, None]
    valid = band[None] & ((blk > 0) | (kj[None] >= L))
    bucket = t5_causal_bucket(jnp.maximum(dist, 0))
    bias = rel_bias.astype(jnp.float32)[bucket]
    bias = bias.transpose(2, 0, 1).reshape(ATTN_KV_HEADS, g, L, 2 * L)

    scale = HEAD_DIM ** -0.5
    sc = jnp.einsum("bnqhgd,bnkhd->bnhgqk", qb, kb).astype(jnp.float32) * scale + bias[None, None]
    sc = jnp.where(valid[None, :, None, None], sc, -1e30)
    sink = sinks.astype(jnp.float32).reshape(ATTN_KV_HEADS, g)[None, None, :, :, None, None]
    m = jnp.maximum(jnp.max(sc, axis=-1, keepdims=True), sink)
    p = jnp.exp(sc - m)
    probs = p / (jnp.sum(p, axis=-1, keepdims=True) + jnp.exp(sink - m))
    o = jnp.einsum("bnhgqk,bnkhd->bnqhgd", probs.astype(v.dtype), vb)
    return o.reshape(bsz, s, ATTN_WIDTH)

def segsum(a):
    t = a.shape[-1]
    cs = jnp.cumsum(a, axis=-1)
    diff = cs[..., :, None] - cs[..., None, :]
    mask = jnp.tril(jnp.ones((t, t), dtype=bool))
    return jnp.where(mask, diff, -jnp.inf)

def ssd_chunked(x, dt, a, bm, cm):
    bsz, s = x.shape[0], x.shape[1]
    pad = (-s) % SSM_CHUNK
    if pad:
        padw = lambda t: jnp.pad(t, [(0, 0), (0, pad)] + [(0, 0)] * (t.ndim - 2))
        x, dt, bm, cm = padw(x), padw(dt), padw(bm), padw(cm)
    sp = s + pad
    nc, L = sp // SSM_CHUNK, SSM_CHUNK
    xc = (x * dt[..., None]).reshape(bsz, nc, L, SSM_HEADS, SSM_HEAD_DIM)
    adt = (dt * a).reshape(bsz, nc, L, SSM_HEADS).transpose(0, 3, 1, 2)
    bc = bm.reshape(bsz, nc, L, SSM_HEADS, SSM_STATE)
    cc = cm.reshape(bsz, nc, L, SSM_HEADS, SSM_STATE)
    a_cum = jnp.cumsum(adt, axis=-1)

    decay = jnp.exp(segsum(adt))
    cb = jnp.einsum("bclhn,bcshn->bhcls", cc, bc)
    y_diag = jnp.einsum("bhcls,bcshp->bclhp", cb * decay, xc)

    to_end = jnp.exp(a_cum[..., -1:] - a_cum).transpose(0, 2, 3, 1)
    states = jnp.einsum("bclhn,bclhp->bchpn", bc * to_end[..., None], xc)

    chunk_decay = jnp.exp(a_cum[..., -1]).transpose(2, 0, 1)

    def step(h, inp):
        dec, st = inp
        return dec[:, :, None, None] * h + st, h

    h0 = jnp.zeros((bsz, SSM_HEADS, SSM_HEAD_DIM, SSM_STATE), jnp.float32)
    _, prev = lax.scan(step, h0, (chunk_decay, states.transpose(1, 0, 2, 3, 4)))
    prev = prev.transpose(1, 0, 2, 3, 4)
    from_start = jnp.exp(a_cum).transpose(0, 2, 3, 1)
    y_off = jnp.einsum("bclhn,bchpn->bclhp", cc * from_start[..., None], prev)
    y = (y_diag + y_off).reshape(bsz, sp, SSM_HEADS, SSM_HEAD_DIM)
    return y[:, :s]

def mamba2_mixer(xs, z, bm, cm, dt_raw, conv_w, conv_b, dt_bias, a_log, d_skip, norm_w):
    bsz, s = xs.shape[0], xs.shape[1]
    xbc = jax.nn.silu(causal_dwconv(jnp.concatenate([xs, bm, cm], axis=-1), conv_w, conv_b))
    xs, bm, cm = _split_last(xbc, (SSM_WIDTH, SSM_BC, SSM_BC))
    rep = SSM_HEADS // SSM_GROUPS
    xh = xs.reshape(bsz, s, SSM_HEADS, SSM_HEAD_DIM).astype(jnp.float32)
    bh = jnp.repeat(bm.reshape(bsz, s, SSM_GROUPS, SSM_STATE), rep, axis=2).astype(jnp.float32)
    ch = jnp.repeat(cm.reshape(bsz, s, SSM_GROUPS, SSM_STATE), rep, axis=2).astype(jnp.float32)
    dt = jax.nn.softplus(dt_raw.astype(jnp.float32) + dt_bias.astype(jnp.float32))
    a = -jnp.exp(a_log.astype(jnp.float32))
    y = ssd_chunked(xh, dt, a, bh, ch) + d_skip.astype(jnp.float32)[:, None] * xh
    y = y.reshape(bsz, s, SSM_WIDTH) * jax.nn.silu(z.astype(jnp.float32))
    yg = y.reshape(bsz, s, SSM_GROUPS, SSM_WIDTH // SSM_GROUPS)
    yg = yg * lax.rsqrt(jnp.mean(yg * yg, axis=-1, keepdims=True) + NORM_EPS)
    y = yg.reshape(bsz, s, SSM_WIDTH) * norm_w.astype(jnp.float32)
    return y.astype(xs.dtype)

def setup_inputs(seed: int = 0) -> dict:
    key = jax.random.key(seed)
    ks = iter(jax.random.split(key, 32))
    f32 = jnp.float32
    nrm = lambda shape, scale: jax.random.normal(next(ks), shape, f32) * scale
    gain = lambda shape: 1.0 + nrm(shape, 0.05)

    x = nrm((BATCH, SEQ, D_MODEL), 1.0)
    c = nrm((BATCH, D_MODEL), 1.0)
    rel_bias = nrm((N_REL_BUCKETS, ATTN_Q_HEADS), 0.5)
    w_ada = nrm((DEPTH, D_MODEL, N_MOD * D_MODEL), D_MODEL ** -0.5)
    b_ada = nrm((DEPTH, N_MOD * D_MODEL), 0.02)
    pre_mix_w = gain((DEPTH, D_MODEL))
    w_in = nrm((DEPTH, D_MODEL, IN_PROJ_WIDTH), D_MODEL ** -0.5)
    attn_sinks = nrm((DEPTH, ATTN_Q_HEADS), 0.5)
    ssm_conv_w = nrm((DEPTH, SSM_CONV, SSM_WIDTH + 2 * SSM_BC), SSM_CONV ** -0.5)
    ssm_conv_b = nrm((DEPTH, SSM_WIDTH + 2 * SSM_BC), 0.02)
    dt0 = jnp.exp(jax.random.uniform(next(ks), (DEPTH, SSM_HEADS), f32,
                                     math.log(1e-3), math.log(1e-1)))
    ssm_dt_bias = dt0 + jnp.log(-jnp.expm1(-dt0))
    ssm_a_log = jnp.log(jax.random.uniform(next(ks), (DEPTH, SSM_HEADS), f32, 1.0, 16.0))
    ssm_d = gain((DEPTH, SSM_HEADS))
    ssm_norm_w = gain((DEPTH, SSM_WIDTH))
    w_out = nrm((DEPTH, MIX_WIDTH, D_MODEL), MIX_WIDTH ** -0.5)
    post_mix_w = gain((DEPTH, D_MODEL))
    pre_ffn_w = gain((DEPTH, D_MODEL))
    w_up = nrm((DEPTH, D_MODEL, 2 * D_FF), D_MODEL ** -0.5)
    ffn_conv_w = nrm((DEPTH, FFN_CONV, 2 * D_FF), FFN_CONV ** -0.5)
    ffn_conv_b = nrm((DEPTH, 2 * D_FF), 0.02)
    w_down = nrm((DEPTH, D_FF, D_MODEL), D_FF ** -0.5)
    post_ffn_w = gain((DEPTH, D_MODEL))
    return {"x": x, "c": c, "rel_bias": rel_bias, "w_ada": w_ada, "b_ada": b_ada,
            "pre_mix_w": pre_mix_w, "w_in": w_in, "attn_sinks": attn_sinks,
            "ssm_conv_w": ssm_conv_w, "ssm_conv_b": ssm_conv_b, "ssm_dt_bias": ssm_dt_bias,
            "ssm_a_log": ssm_a_log, "ssm_d": ssm_d, "ssm_norm_w": ssm_norm_w,
            "w_out": w_out, "post_mix_w": post_mix_w, "pre_ffn_w": pre_ffn_w,
            "w_up": w_up, "ffn_conv_w": ffn_conv_w, "ffn_conv_b": ffn_conv_b,
            "w_down": w_down, "post_ffn_w": post_ffn_w}

def reference(x, c, rel_bias, w_ada, b_ada, pre_mix_w, w_in, attn_sinks, ssm_conv_w,
              ssm_conv_b, ssm_dt_bias, ssm_a_log, ssm_d, ssm_norm_w, w_out, post_mix_w,
              pre_ffn_w, w_up, ffn_conv_w, ffn_conv_b, w_down, post_ffn_w):
    bsz, s = x.shape[0], x.shape[1]
    cond = jax.nn.silu(c)
    for l in range(DEPTH):
        mod = (cond @ w_ada[l] + b_ada[l])[:, None, :]
        shift1, scale1, gate1, shift2, scale2, gate2 = jnp.split(mod, N_MOD, axis=-1)

        h = rms_norm(x, pre_mix_w[l]) * (1.0 + scale1) + shift1
        proj = h @ w_in[l]
        q, k, v, xs, z, bm, cm, dt_raw = _split_last(proj, IN_SPLITS)
        attn = sliding_window_attention(
            q.reshape(bsz, s, ATTN_Q_HEADS, HEAD_DIM),
            k.reshape(bsz, s, ATTN_KV_HEADS, HEAD_DIM),
            v.reshape(bsz, s, ATTN_KV_HEADS, HEAD_DIM),
            rel_bias, attn_sinks[l])
        ssm = mamba2_mixer(xs, z, bm, cm, dt_raw, ssm_conv_w[l], ssm_conv_b[l],
                           ssm_dt_bias[l], ssm_a_log[l], ssm_d[l], ssm_norm_w[l])
        mixed = jnp.concatenate([attn, ssm], axis=-1) @ w_out[l]
        x = x + gate1 * rms_norm(mixed, post_mix_w[l])

        h = rms_norm(x, pre_ffn_w[l]) * (1.0 + scale2) + shift2
        u = causal_dwconv(h @ w_up[l], ffn_conv_w[l], ffn_conv_b[l])
        u_gate, u_val = jnp.split(u, 2, axis=-1)
        f = (jax.nn.gelu(u_gate, approximate=True) * u_val) @ w_down[l]
        x = x + gate2 * rms_norm(f, post_ffn_w[l])
    return x


_drawn_inputs = setup_inputs


def setup_inputs(seed=0):
    import zlib

    import numpy as np

    out = dict(_drawn_inputs(seed))
    spreads = {}
    factors = {'attn_sinks': 8.0,
     'ssm_conv_b': 6.025,
     'ssm_d': 7.838,
     'ssm_norm_w': 2.685,
     'ffn_conv_b': 5.793}
    for name, (base, spread) in spreads.items():
        noise = np.random.default_rng([zlib.crc32(name.encode()), seed]).standard_normal(out[name].shape)
        drawn = base * np.exp(spread * noise) if base else spread * noise
        out[name] = __import__('jax').numpy.asarray(drawn.astype(out[name].dtype))
    for name, factor in factors.items():
        out[name] = (out[name] * factor).astype(out[name].dtype)
    return out
```

```python
import math
from contextlib import ExitStack

import numpy as np
import concourse.bass as bass
from concourse import mybir

D = 1024
T = 1024
P = 128
KT = D // P
NB = T // P
H = 8
HD = 64
NPAIR = H // 2
GROUPS = 2
FF = 2816
FT = FF // P
NBUCKET = 32
EXT = 3 * P
EPS = 1e-6
NEG = -1e30

U_IN, U_DT, U_OUT, U_UP, U_DOWN = 0, 18, 19, 27, 71
U_END = 93
DOWN_UNITS = FT // 2
SSM_W = H * HD
Q, K, V, XS, Z, BB, CC = 0, 4, 5, 6, 10, 14, 16
CONV = [6, 7, 8, 9, 14, 15, 16, 17]
SLOT = [14, 15, 16, 17, 18, 19, 0, 1, 2, 3, 4, 5, 6, 7, 8, 9, 20, 21]
N_SMALL, N_LATE = 10, 10
N_CONV_ROWS = 40
N_FFN_ROWS = 88
N_MOD_ROWS = 64
C_CONV, C_FFN = N_MOD_ROWS, N_MOD_ROWS + N_CONV_ROWS


def shape_constants():
    i = np.arange(P)
    squares = np.concatenate([
        np.eye(P), i[:, None] <= i[None, :], i[:, None] > i[None, :], np.eye(P)[::-1]], axis=1)
    hot = np.zeros((NBUCKET + 1, EXT))
    for u in range(EXT):
        dist = 2 * P - 1 - u
        if 0 <= dist < P:
            half = NBUCKET // 2
            b = dist if dist < half else min(NBUCKET - 1, half + int(
                math.log(dist / half) / math.log(P / half) * (NBUCKET - half)))
            hot[b, u] = 1.0
        else:
            hot[NBUCKET, u] = 1.0
    return squares.astype(np.float32), hot.astype(np.float32)


def hybrid_layer_kernel(nc, x, c, rel_bias, w_ada, b_ada, pre_mix_w, w_in, attn_sinks, ssm_conv_w,
                        ssm_conv_b, ssm_dt_bias, ssm_a_log, ssm_d, ssm_norm_w, w_out, post_mix_w,
                        pre_ffn_w, w_up, ffn_conv_w, ffn_conv_b, w_down, post_ffn_w,
                        squares, hot, out):
    f32 = mybir.dt.float32
    f32r = mybir.dt.float32r
    ALU = mybir.AluOpType
    ACT = mybir.ActivationFunctionType
    AX = mybir.AxisListType

    x2, out2 = x[0], out[0]
    w_in2, w_out2, w_up2, w_down2, w_ada2 = w_in[0], w_out[0], w_up[0], w_down[0], w_ada[0]
    bias_d = nc.dram_tensor("bias_by_distance", (H, EXT), f32).ap()
    x1_d = nc.dram_tensor("residual_after_mixer", (T, D), f32).ap()

    ctx = ExitStack()
    with ctx:
        def sb(name, shape, dt=f32):
            return ctx.enter_context(nc.sbuf_tensor(name, shape, dt))

        def sem(name):
            return ctx.enter_context(nc.semaphore(name))

        big = sb("big", [P, FT, T])
        a_hi = sb("a_hi", [P, KT, T], f32r)
        a_lo = sb("a_lo", [P, KT, T], f32r)
        raw = sb("raw", [P, 2, T])
        w_hi = sb("w_hi", [P, 2, T], f32r)
        w_lo = sb("w_lo", [P, 2, T], f32r)
        scratch = sb("scratch", [P, 4 * T])
        gate_rows = sb("gate_rows", [P, 2, D])
        sq = sb("sq", [P, 3 * P])
        ones = sb("ones", [P, P])
        cols = sb("cols", [P, 280])
        modc = sb("modc", [P, 32])
        ca = sb("ca", [P, 2, KT])
        hv = sb("hv", [P, 8, H])
        dtv = sb("dtv", [P, 5, NB * H])
        st = sb("st", [P, 128])
        normw = sb("normw", [P, SSM_W])
        ident, upper, strict = sq[:, 0:P], sq[:, P:2 * P], sq[:, 2 * P:3 * P]
        flip = scratch[:, 3840:3968]
        raw_dt = scratch[:, 3968:4032].rearrange("p (k h) -> p k h", k=KT)
        ps = ctx.enter_context(nc.psum_tensor("ps", [P, 8 * 512], f32))

        def bank(b, n=1):
            return ps[:, b * 512:(b + n) * 512]

        def ring(t, u):
            return t[:, u % 2, :]

        def flat(tiles):
            return tiles.rearrange("p a b -> p (a b)")

        xnT = big[:, 14:22, :]
        acc = flat(big[:, 8:14, :])
        chunk = [flat(big[:, 4 * s:4 * s + 4, :]).rearrange("p (j n) -> p j n", j=KT) for s in range(2)]

        def proj(n):
            return big[:, SLOT[n], :]

        def blk(n, i, w=1):
            return big[:, SLOT[n], i * P:(i + w) * P]

        def four(n, i):
            return big[:, SLOT[n]:SLOT[n] + 4, i * P:(i + 1) * P]

        def heads(ap):
            return ap.rearrange("p (h d) -> p h d", h=H)

        def per_head(ap):
            return ap.unsqueeze(2).to_broadcast([P, H, HD])

        work = flat(big[:, 10:14, :])
        prob = work[:, 0:1024].rearrange("p (s e k) -> p s e k", s=2, e=2)
        probT = work[:, 1024:2048].rearrange("p (s n) -> p s n", s=2)
        xc, xc_end = work[:, 2048:2560], work[:, 2560:3072]
        yy, state = work[:, 3072:3584], work[:, 3584:4096]
        dt_rows = work[0:16, 0:1024]
        dt_tmp = work[:, 1152:1344].rearrange("p (v n) -> p v n", v=3)
        dt_nat = work[:, 1024:1152].rearrange("p (b n) -> p b n", b=NB)
        bias = scratch[:, 0:2048].rearrange("p (j e k) -> p j e k", j=NPAIR, e=2)
        decay = scratch[:, 2048:3072].rearrange("p (g n) -> p g n", g=2)
        cbm = scratch[:, 3072:3328].rearrange("p (g l) -> p g l", g=2)
        bn = scratch[:, 3328:3584].rearrange("p (g n) -> p g n", g=2)
        vb = scratch[:, 3584:3840].rearrange("p (s n) -> p s n", s=2)
        rows = scratch[:, 2048:2560].rearrange("p (t n) -> p t n", t=4)
        post_bc = scratch[:, 0:2048].rearrange("p (t n) -> p t n", t=2)
        hot_sb = scratch[0:NBUCKET + 1, 2560:2560 + EXT]
        rb_sb = scratch[0:NBUCKET + 1, 2944:2944 + H]
        ext_sb = scratch[0:H, 2960:2960 + EXT]
        xr = big[:, 0:8, :]
        mixed0 = flat(big[:, 8:12, :]).rearrange("p (b n) -> p b n", b=NB)
        xn2 = scratch[:, 0:2048].rearrange("p (s n) -> p s n", s=2)
        mixed_t = scratch[:, 2048:2560]
        junk = scratch[:, 2560:3584]
        gate_t = scratch[:, 0:2048].rearrange("p (s n) -> p s n", s=2)
        half0 = scratch[:, 0:4096].rearrange("p (b n) -> p b n", b=NB)
        junk_r = a_lo[:, 2, 0:512]

        SINK, NSINK, DTB, EA, DD, NM, DEN, REC = range(8)
        DT, ADT, FS, TE, CD, T2, T3, T4 = range(8)
        minus_half = st[:, 62:63]

        def dt_slot(v):
            return dtv[:, v, :] if v <= CD else dt_tmp[:, v - T2, :]

        esk = st[:, 64:72]
        mx = st[:, 72:74]

        s_const = sem("c_and_constants_loaded")
        s_small, s_late = sem("early_vectors_loaded"), sem("late_vectors_loaded")
        s_x = [sem(f"x_block_loaded{i}") for i in range(2)]
        s_ada = [sem(f"ada_chunk_loaded{i}") for i in range(2)]
        s_w = [sem(f"w_unit_loaded{i}") for i in range(2)]
        s_bd, s_bl = sem("bias_vectors_stored"), sem("bias_windows_loaded")
        s_xr, s_x1, s_x1l = sem("x_reloaded"), sem("x1_stored"), sem("x1_reloaded")
        s_out = [sem(f"out_stored{i}") for i in range(2)]
        s_pool, s_pc = sem("pool_constants"), sem("pool_chain")
        s_cs = sem("silu_c_ready")
        s_sq, s_rs = sem("x_squares_summed"), sem("x_rstd_ready")
        s_xn, s_xT, s_xe = sem("xn_ready"), sem("xn_transposed"), sem("xnT_evacuated")
        s_acc = sem("ada_chunk_summed")
        s_rT, s_cols = sem("vector_rows_transposed"), sem("columns_ready")
        s_mp, s_mod = sem("mod_sums_in_psum"), sem("mod_ready")
        s_h, s_hhi, s_hlo = sem("h_modulated"), sem("h_hi_ready"), sem("h_lo_ready")
        s_whi, s_wlo, s_wu = sem("w_hi_ready"), sem("w_lo_ready"), sem("w_unit_used")
        s_evA, s_evD = sem("psum_freed_by_act"), sem("psum_freed_by_dve")
        s_c0, s_si = sem("conv_first_tap"), sem("conv_silu_done")
        s_ext, s_exs = sem("bias_vectors_in_psum"), sem("bias_vectors_ready")
        s_flp, s_bias = sem("bias_flipped"), sem("bias_ready")
        s_dtT, s_dtn = sem("dt_evacuated"), sem("dt_transposed")
        s_dt1, s_dtA = sem("dt_steps_of_dve"), sem("dt_steps_of_act")
        s_dte, s_dtc, s_dt2 = sem("dt_a_ready"), sem("dt_a_sums_in_psum"), sem("dt_end_ready")
        s_t1, s_vb = sem("v_b_transposed"), sem("v_b_rows_ready")
        s_xsT, s_xc = sem("xs_transposed"), sem("xc_ready")
        s_cb, s_cbm = sem("cb_in_psum"), sem("cb_masked")
        s_rd, s_D, s_E = sem("decay_terms_ready"), sem("segment_sums_in_psum"), sem("decay_ready")
        s_W = sem("ssd_weights_ready")
        s_yo, s_yd, s_sn = sem("y_off_in_psum"), sem("y_diag_in_psum"), sem("state_in_psum")
        s_ya, s_yb, s_su = sem("y_off_taken"), sem("y_diag_taken"), sem("state_updated")
        s_zT, s_g = sem("z_transposed"), sem("y_gated")
        s_gq, s_gr, s_my = sem("gated_squares"), sem("gated_rstd"), sem("ssm_rows_ready")
        s_S, s_sb = sem("scores_in_psum"), sem("scores_taken")
        s_nm, s_p = sem("neg_max_ready"), sem("probs_ready")
        s_pT, s_pe, s_pv = sem("probs_transposed"), sem("probsT_ready"), sem("pv_done")
        s_nms, s_es, s_o = sem("sink_minus_max"), sem("sink_exp"), sem("attention_rows_ready")
        s_mT, s_mh, s_ml = sem("mixed_rows_transposed"), sem("mixT_hi_ready"), sem("mixT_lo_ready")
        s_mo, s_m0 = sem("out_bank_done"), sem("mixed_half0_evacuated")
        s_mq, s_mr, s_mx = sem("mixed_squares"), sem("mixed_rstd"), sem("x1_ready")
        s_q2, s_r2, s_n2 = sem("x1_squares"), sem("x1_rstd"), sem("x1_normalised")
        s_T2, s_e2 = sem("x1_transposed"), sem("x1T_evacuated")
        s_h2, s_h2h, s_h2l = sem("h2_modulated"), sem("h2_hi_ready"), sem("h2_lo_ready")
        s_u0, s_uc, s_u1 = sem("up_first_tap"), sem("up_second_tap"), sem("up_taps_done")
        s_ge, s_f = sem("gelu_done"), sem("f_ready")
        s_fh, s_fl, s_fu = sem("f_hi_ready"), sem("f_lo_ready"), sem("f_first_tile_used")
        s_dn, s_d0 = sem("down_bank_done"), sem("down_half0_evacuated")
        s_dq, s_dr, s_do = sem("down_squares"), sem("down_rstd"), sem("out_rows_ready")
        s_dv, s_ac = sem("dve_chain"), sem("act_chain")

        block = ctx.enter_context(nc.Block())

        def bank_done(eng, s, half, b, u):
            if b < NB - 1:
                eng.wait_ge(s, (NB - 1) * half + b + 1)
            else:
                eng.wait_ge(s_wu, u + 1)

        def loaded(u):
            if isinstance(u, int) and u < U_DT:
                return 16 * (u // 2 + 1 + min(2, u // 2 + 1))
            return 16 * (u // 2 + 3 - (1 - u % 2))

        @block.sync
        def _(sp):
            sp.dma_start(ca[:, 0, :], c.rearrange("o (p j) -> p (o j)", j=KT)).then_inc(s_const, 16)
            sp.dma_start(sq[:, :], squares[:, 0:3 * P]).then_inc(s_const, 16)
            sp.dma_start(flip, squares[:, 3 * P:]).then_inc(s_const, 16)

            def load_x(b):
                if b >= 2:
                    sp.wait_ge(s_xT, b - 1)
                sp.dma_start(ring(raw, b), x2[b * P:(b + 1) * P, :]).then_inc(s_x[b % 2], 16)

            def load_chunk(n):
                if n >= 2:
                    sp.wait_ge(s_acc, n - 1)
                sp.dma_start(chunk[n % 2], w_ada2[:, n * 512:(n + 1) * 512]
                             .rearrange("(p j) n -> p j n", j=KT)).then_inc(s_ada[n % 2], 16)

            load_x(0)
            load_x(1)
            load_chunk(0)
            load_chunk(1)
            for b in range(2, NB):
                load_x(b)
                if b in (3, 5):
                    load_chunk((b + 1) // 2)

            in_src = w_in2.rearrange("(k p) n -> p k n", p=P)

            def load_in(n):
                dst = ring(raw, n).rearrange("p (k n) -> p k n", k=KT)
                if n < K:
                    for e in range(2):
                        h = n + 4 * e
                        sp.dma_start(dst[:, :, e * HD:(e + 1) * HD],
                                     in_src[:, :, h * HD:(h + 1) * HD]).then_inc(s_w[n % 2], 16)
                else:
                    sp.dma_start(dst, in_src[:, :, n * P:(n + 1) * P]).then_inc(s_w[n % 2], 16)

            for n in range(U_DT):
                if n < 2:
                    sp.wait_ge(s_xT, 7 + n)
                else:
                    sp.wait_ge(s_wlo, n - 1)
                load_in(n)
                if 1 <= n < 5:
                    load_chunk(2 * n + 2)
                    load_chunk(2 * n + 3)

            def load_rows(u, w, half, k0):
                sp.dma_start(ring(raw, u).rearrange("p (k n) -> p k n", k=2),
                             w[bass.ds(k0 * P, 2 * P), half * 512:(half + 1) * 512]
                             .rearrange("(k p) n -> p k n", p=P)).then_inc(s_w[u % 2], 16)

            for t in range(U_UP - U_OUT):
                sp.wait_ge(s_wlo, U_OUT + t - 1)
                load_rows(U_OUT + t, w_out2, t // 4, 2 * (t % 4))
                if t == 1:
                    sp.wait_ge(s_mT, 2 * NB)
                    sp.dma_start(xr, x2.rearrange("(b p) n -> p b n", p=P)).then_inc(s_xr, 16)

            def load_up(i, t):
                u = U_UP + t
                sp.wait_ge(s_wlo, i * 4 + (u - 1))
                col = i * (2 * P) + ((t // 2) * P + (t % 2) * FF)
                sp.dma_start(ring(raw, u).rearrange("p (k n) -> p k n", k=KT),
                             w_up2[:, bass.ds(col, P)].rearrange("(k p) n -> p k n", p=P))\
                    .then_inc(s_w[u % 2], 16)

            for t in range(2):
                load_up(0, t)
            for b in range(NB):
                sp.wait_ge(s_mx, b + 1)
                sp.dma_start(x1_d[b * P:(b + 1) * P, :], xr[:, b, :]).then_inc(s_x1, 16)
            for t in range(2, 4):
                load_up(0, t)
            with sp.Fori(1, FT // 2) as i:
                for t in range(4):
                    load_up(i, t)

            for half in range(2):
                for kk in range(11):
                    u = U_DOWN + 11 * half + kk
                    sp.wait_ge(s_wlo, u - 1)
                    load_rows(u, w_down2, half, 2 * kk)
            sp.wait_ge(s_x1, 16 * NB)
            sp.wait_ge(s_wu, U_DOWN)
            for b in range(NB):
                dst = (a_hi if b < 4 else a_lo)[:, 4 + b % 4, :].bitcast(f32)
                sp.dma_start(dst, x1_d[b * P:(b + 1) * P, :]).then_inc(s_x1l, 16)
            for b in range(NB):
                sp.wait_ge(s_do, b + 1)
                sp.dma_start(out2[b * P:(b + 1) * P, :], ring(raw, b)).then_inc(s_out[b % 2], 16)
            for n in range(2):
                sp.wait_ge(s_out[n], 16 * NB // 2)

        @block.gpsimd
        def _(pool):
            pool.memset(ones[:, :], 1.0).then_inc(s_pool, 1)
            pool.memset(rb_sb, NEG).then_inc(s_pool, 1)
            pool.memset(minus_half, -0.5).then_inc(s_pool, 1)
            for m, (r0, v) in enumerate([(0, b_ada), (48, pre_mix_w), (56, pre_ffn_w)]):
                n = v.shape[1] // P
                pool.dma_start(rows[r0:r0 + n, 0, :], v[0].rearrange("(r n) -> r n", n=P)).then_inc(s_small, 16)
            pool.dma_start(rows[0:32, 1, :], ssm_conv_w[0].rearrange("t (m n) -> (t m) n", n=P)).then_inc(s_small, 16)
            pool.dma_start(rows[32:40, 1, :], ssm_conv_b[0].rearrange("(r n) -> r n", n=P)).then_inc(s_small, 16)
            fw = ffn_conv_w[0].rearrange("t (m n) -> (t m) n", n=P)
            pool.dma_start(rows[0:88, 2, :], fw[0:88, :]).then_inc(s_small, 16)
            pool.dma_start(rows[0:44, 3, :], fw[88:132, :]).then_inc(s_small, 16)
            pool.dma_start(rows[44:88, 3, :], ffn_conv_b[0].rearrange("(r n) -> r n", n=P)).then_inc(s_small, 16)
            pool.dma_start(hot_sb, hot).then_inc(s_small, 16)
            pool.wait_ge(s_pool, 2)
            pool.dma_start(rb_sb[0:NBUCKET, :], rel_bias).then_inc(s_small, 16)
            for dst, row in [(hv[:, SINK, :], attn_sinks), (hv[:, DTB, :], ssm_dt_bias),
                             (hv[:, EA, :], ssm_a_log), (hv[:, DD, :], ssm_d), (normw[:, :], ssm_norm_w),
                             (gate_rows[:, 0, :], b_ada[:, 2 * D:3 * D]),
                             (gate_rows[:, 1, :], b_ada[:, 5 * D:6 * D]),
                             (post_bc[:, 0, :], post_mix_w), (post_bc[:, 1, :], post_ffn_w)]:
                pool.dma_start(dst, row.to_broadcast([P, row.shape[-1]])).then_inc(s_late, 16)
            pool.dma_start(raw_dt[:, :, :], w_in2.rearrange("(k p) n -> p k n", p=P)[:, :, 18 * P:18 * P + H])\
                .then_inc(s_late, 16)

            chain = [0]

            def link(ins):
                chain[0] += 1
                ins.then_inc(s_pc, 1)
                pool.wait_ge(s_pc, chain[0])

            def rstd(dst, src, width, done):
                link(pool.tensor_scalar(src, src, 1.0 / width, EPS, ALU.mult, ALU.add))
                power = minus_half if src.shape[1] == 1 else minus_half.to_broadcast(list(src.shape))
                pool.tensor_tensor(dst, src, power, ALU.pow).then_inc(done, 1)

            pool.wait_ge(s_pool, 3)
            for b in range(NB):
                pool.wait_ge(s_sq, b + 1)
                rstd(st[:, 8 + b:9 + b], st[:, b:b + 1], D, s_rs)

            pool.wait_ge(s_exs, 1)
            pool.dma_start(bias_d, ext_sb).then_inc(s_bd, 16)
            pool.wait_ge(s_bd, 16)
            pool.wait_ge(s_mod, 6)
            for e in range(2):
                src = bass.AP(bias_d.tensor, 4 * e * EXT, [[1, P], [EXT, NPAIR], [1, 2 * P]])
                pool.dma_start(bias[:, :, e, :], src).then_inc(s_bl, 16)

            pool.wait_ge(s_dte, 1)
            link(pool.memset(state, 0.0))
            for i in range(NB):
                if i >= 1:
                    pool.wait_ge(s_yd, i)
                for g in range(GROUPS):
                    adt = dtv[:, ADT, i * H + 4 * g:i * H + 4 * g + 4].unsqueeze(2).to_broadcast([P, 4, P])
                    tri = upper.unsqueeze(1).to_broadcast([P, 4, P])
                    pool.tensor_tensor(decay[:, g, :].rearrange("p (h l) -> p h l", h=4), tri, adt,
                                       ALU.mult).then_inc(s_rd, 1)
                if i >= 1:
                    pool.wait_ge(s_gq, i)
                    rstd(st[:, 58:60], st[:, 56:58], SSM_W // GROUPS, s_gr)
            pool.wait_ge(s_gq, NB)
            rstd(st[:, 58:60], st[:, 56:58], SSM_W // GROUPS, s_gr)

            for b in range(NB + 1):
                if b < NB:
                    pool.wait_ge(s_mq, b + 1)
                    link(pool.tensor_tensor(st[:, 16 + b:17 + b], st[:, 16 + b:17 + b], st[:, 24 + b:25 + b], ALU.add))
                    rstd(st[:, 80 + b:81 + b], st[:, 16 + b:17 + b], D, s_mr)
                if b >= 1:
                    pool.wait_ge(s_q2, b)
                    rstd(st[:, 40 + b - 1:40 + b], st[:, 32 + b - 1:32 + b], D, s_r2)
            for b in range(NB):
                pool.wait_ge(s_dq, b + 1)
                link(pool.tensor_tensor(st[:, 88 + b:89 + b], st[:, 88 + b:89 + b], st[:, 96 + b:97 + b], ALU.add))
                rstd(st[:, 104 + b:105 + b], st[:, 88 + b:89 + b], D, s_dr)

        @block.scalar
        def _(act):
            act.wait_ge(s_const, 48)
            act.activation(ca[:, 1, :], ca[:, 0, :], ACT.Silu).then_inc(s_cs, 1)
            chain = [0]

            def link(ins):
                chain[0] += 1
                ins.then_inc(s_ac, 1)
                act.wait_ge(s_ac, chain[0])

            def x_squares(b):
                act.wait_ge(s_x[b % 2], 16 * (b // 2 + 1))
                if b >= 1:
                    act.wait_ge(s_sq, b)
                act.activation(bank(6, 2), ring(raw, b), ACT.Square, accum_out=st[:, b:b + 1]).then_inc(s_sq, 1)

            def x_evacuate(b):
                act.wait_ge(s_xT, b + 1)
                act.activation(xnT[:, :, b * P:(b + 1) * P],
                               bank(2 * (b % 3), 2).rearrange("p (k t) -> p k t", k=KT), ACT.Copy).then_inc(s_xe, 1)

            for b in range(NB):
                x_squares(b)
                if b >= 1:
                    x_evacuate(b - 1)
            x_evacuate(NB - 1)

            def split_hi(u, du=0):
                slot = u % 2
                act.wait_ge(s_w[slot], du * 8 + loaded(u))
                if u >= 2:
                    act.wait_ge(s_wu, du + (u - 1))
                act.activation(ring(w_hi, u), ring(raw, u), ACT.Copy).then_inc(s_whi, 1)

            split_hi(0)
            for k in range(KT):
                act.wait_ge(s_h, k + 1)
                act.activation(a_hi[:, k, :], xnT[:, k, :], ACT.Copy).then_inc(s_hhi, 1)

            def evacuate(n):
                act.wait_ge(s_wu, n + 1)
                src = bank(2 * (n % 3), 2)
                if n == XS:
                    act.wait_ge(s_mod, 6)
                if n in CONV:
                    m = CONV.index(n)
                    act.activation(proj(n), src, ACT.Identity,
                                   scale=cols[:, C_CONV + 24 + m:C_CONV + 25 + m]).then_inc(s_c0, 1)
                else:
                    act.activation(proj(n), src, ACT.Silu if Z <= n < BB else ACT.Copy).then_inc(s_evA, 1)

            def conv_silu(n):
                if n in CONV:
                    m = CONV.index(n)
                    act.wait_ge(s_evD, m + 1)
                    act.activation(proj(n), proj(n), ACT.Silu,
                                   bias=cols[:, C_CONV + 32 + m:C_CONV + 33 + m]).then_inc(s_si, 1)

            split_hi(1)
            for n in range(1, U_DT):
                if n + 1 < U_DT:
                    split_hi(n + 1)
                evacuate(n - 1)
                if n >= 2:
                    conv_silu(n - 2)
            act.wait_ge(s_late, 16 * N_LATE)
            act.wait_ge(s_wu, U_DT - 1)
            wdt = ring(w_hi, U_DT).rearrange("p (k n) -> p k n", k=KT)
            act.activation(wdt[:, :, 0:H], raw_dt[:, :, :], ACT.Copy).then_inc(s_whi, 1)
            evacuate(U_DT - 1)
            conv_silu(U_DT - 2)
            conv_silu(U_DT - 1)
            act.wait_ge(s_wu, U_DT + 1)
            act.activation(dt_rows, bank(0, 2)[0:16, :], ACT.Copy).then_inc(s_dtT, 1)

            for j in range(NPAIR):
                act.wait_ge(s_flp, j + 1)
                act.activation(bias[:, j], bank(4 + j % 2).rearrange("p (e k) -> p e k", e=2), ACT.Copy)\
                    .then_inc(s_bias, 1)

            act.wait_ge(s_dt1, 1)
            act.activation(dt_slot(T2), dt_slot(T4), ACT.Exp, scale=-1.0).then_inc(s_dtA, 1)
            act.activation(hv[:, EA, :], hv[:, EA, :], ACT.Exp).then_inc(s_dtA, 1)
            act.wait_ge(s_dt1, 2)
            act.activation(dtv[:, FS, :], dt_slot(T4), ACT.Ln).then_inc(s_dtA, 1)
            act.wait_ge(s_dtc, 1)
            act.activation(dtv[:, FS:CD + 1, :], bank(3)[:, 0:192].rearrange("p (v n) -> p v n", v=3),
                           ACT.Exp).then_inc(s_dtA, 1)

            def probs(i, j):
                u = NPAIR * i + j
                act.wait_ge(s_nm, u + 1)
                if j == 0 and i >= 1:
                    act.wait_ge(s_o, i)
                k0 = P if i == 0 else 0
                for e in range(2):
                    h = j + 4 * e
                    ins = act.activation(prob[:, u % 2, e, k0:], prob[:, u % 2, e, k0:], ACT.Exp,
                                         bias=hv[:, NM, h:h + 1], accum_out=hv[:, DEN, h:h + 1])
                ins.then_inc(s_p, 1)

            def probs_evacuate(i, j):
                u = NPAIR * i + j
                act.wait_ge(s_pT, u + 1)
                if u >= 2:
                    act.wait_ge(s_pv, u - 1)
                src = bank(2 + u % 2).rearrange("p (e k q) -> p e k q", e=2, k=2)
                dst = probT[:, u % 2, :].rearrange("p (e k q) -> p e k q", e=2, k=2)
                k0 = 1 if i == 0 else 0
                act.activation(dst[:, :, k0:, :], src[:, :, k0:, :], ACT.Copy).then_inc(s_pe, 1)

            def mix_hi(i, part):
                act.wait_ge(s_mT, 2 * i + (2 if part == 0 else 1))
                act.activation(a_hi[:, 4 * part:4 * part + 4, i * P:(i + 1) * P],
                               bank(6 + part).rearrange("p (k t) -> p k t", k=4), ACT.Copy).then_inc(s_mh, 1)

            for i in range(NB):
                act.wait_ge(s_t1, i + 1)
                if i >= 2:
                    act.wait_ge(s_pv, NPAIR * i)
                act.activation(vb[:, i % 2, :], bank(5)[:, 0:P], ACT.Copy).then_inc(s_vb, 1)
                if i >= 1:
                    act.wait_ge(s_sn, i)
                act.activation(bn, bank(5)[:, P:3 * P].rearrange("p (g n) -> p g n", g=2), ACT.Copy).then_inc(s_vb, 1)
                probs(i, 0)
                for g in range(GROUPS):
                    act.wait_ge(s_D, 2 * i + g + 1)
                    act.activation(decay[:, g, :], bank(5 + 2 * g), ACT.Exp).then_inc(s_E, 1)
                probs_evacuate(i, 0)
                probs(i, 1)
                probs_evacuate(i, 1)
                probs(i, 2)
                probs_evacuate(i, 2)
                act.wait_ge(s_g, i + 1)
                for g in range(GROUPS):
                    ins = act.activation(four(Z, i)[:, 2 * g:2 * g + 2, :],
                                         yy[:, g * 256:(g + 1) * 256].rearrange("p (a b) -> p a b", a=2),
                                         ACT.Square, accum_out=st[:, 56 + g:57 + g])
                ins.then_inc(s_gq, 1)
                probs(i, 3)
                probs_evacuate(i, 3)
                act.wait_ge(s_nms, i + 1)
                act.activation(esk, esk, ACT.Exp).then_inc(s_es, 1)
                mix_hi(i, 1)
                mix_hi(i, 0)

            for t in range(U_UP - U_OUT):
                split_hi(U_OUT + t)
                if t == 4:
                    for b in range(NB):
                        bank_done(act, s_mo, 0, b, U_OUT + 3)
                        act.activation(mixed0[:, b, :], bank(b), ACT.Copy).then_inc(s_m0, 1)
                    for b in range(NB):
                        act.wait_ge(s_m0, b + 1)
                        link(act.activation(junk[:, 0:512], mixed0[:, b, :], ACT.Square,
                                            accum_out=st[:, 16 + b:17 + b]))
            split_hi(U_UP)
            for b in range(NB + 2):
                if b < NB:
                    bank_done(act, s_mo, 1, b, U_UP - 1)
                    if b >= 1:
                        act.wait_ge(s_mq if b == 1 else s_q2, max(1, b - 1))
                    act.activation(junk[:, 0:512], bank(b), ACT.Square, accum_out=st[:, 24 + b:25 + b])\
                        .then_inc(s_mq, 1)
                if 1 <= b <= NB:
                    act.wait_ge(s_mx, b)
                    if b < NB:
                        act.wait_ge(s_mq, b + 1)
                    else:
                        act.wait_ge(s_q2, b - 1)
                    act.activation(junk, xr[:, b - 1, :], ACT.Square, accum_out=st[:, 32 + b - 1:32 + b])\
                        .then_inc(s_q2, 1)
                if b >= 2:
                    act.wait_ge(s_T2, b - 1)
                    act.activation(xnT[:, :, (b - 2) * P:(b - 1) * P],
                                   bank(2 * (b % 2), 2).rearrange("p (k t) -> p k t", k=KT), ACT.Copy)\
                        .then_inc(s_e2, 1)
            for hf in range(2):
                for k in range(KT):
                    act.wait_ge(s_h2, KT * hf + k + 1)
                    act.activation(a_hi[:, k, hf * 512:(hf + 1) * 512], xnT[:, k, hf * 512:(hf + 1) * 512],
                                   ACT.Copy).then_inc(s_h2h, 1)

            def column(base, i, t):
                return cols[:, bass.ds(i * 2 + (base + t // 2 + FT * (t % 2)), 1)]

            def f_tile(k):
                return flat(big[:, bass.ds(k, 1), :])

            def up_first_tap(i, t, first):
                act.wait_ge(s_wu, i * 4 + (U_UP + t + 1))
                if t % 2:
                    dst = f_tile(i * 2 + t // 2)
                    if first:
                        act.wait_ge(s_x1, 16 * NB)
                else:
                    dst = gate_t[:, t // 2, :]
                    if not first:
                        act.wait_ge(s_f, i * 2 + (t // 2 - 1))
                act.activation(dst, bank(2 * t, 2), ACT.Identity, scale=column(C_FFN + 88, i, t),
                               bias=column(C_FFN + 132, i, t)).then_inc(s_u0, 1)

            def up_gelu(i, pr):
                act.wait_ge(s_u1, i * 4 + (2 * pr + 1))
                act.activation(gate_t[:, pr, :], gate_t[:, pr, :], ACT.Gelu_apprx_tanh).then_inc(s_ge, 1)

            def up_body(i, first=False):
                for t in range(4):
                    split_hi(U_UP + t + 1, i * 4)
                    up_first_tap(i, t, first)
                    if t % 2:
                        up_gelu(i, t // 2)

            up_body(0, first=True)
            with act.Fori(1, FT // 2) as i:
                up_body(i)

            def f_split_hi(half, kk, e):
                if isinstance(kk, int) and half == 0 and kk == 0:
                    act.wait_ge(s_wu, U_DOWN)
                    act.wait_ge(s_f, FT)
                elif e == 0:
                    act.wait_ge(s_fu, kk + DOWN_UNITS * half)
                else:
                    act.wait_ge(s_wu, kk + (U_DOWN + DOWN_UNITS * half))
                act.activation(a_hi[:, e, :], f_tile(kk * 2 + e), ACT.Copy).then_inc(s_fh, 1)

            def down_unit(half, kk0, dk, split_next=True):
                for e in range(2):
                    f_split_hi(half, dk + kk0, e)
                if split_next:
                    split_hi(U_DOWN + DOWN_UNITS * half + kk0 + 1, dk)

            for half in range(2):
                down_unit(half, 0, 0)
                with act.Fori(0, 4) as i:
                    down_unit(half, 1, i * 2)
                    down_unit(half, 2, i * 2)
                down_unit(half, 9, 0)
                down_unit(half, 10, 0, split_next=half == 0)
                if half == 0:
                    for b in range(NB):
                        bank_done(act, s_dn, 0, b, U_DOWN + DOWN_UNITS - 1)
                        act.activation(half0[:, b, :], bank(b), ACT.Copy).then_inc(s_d0, 1)
                    for b in range(NB):
                        act.wait_ge(s_d0, b + 1)
                        link(act.activation(junk_r, half0[:, b, :], ACT.Square, accum_out=st[:, 88 + b:89 + b]))
            for b in range(NB):
                bank_done(act, s_dn, 1, b, U_END - 1)
                if b >= 1:
                    act.wait_ge(s_dq, b)
                act.activation(junk_r, bank(b), ACT.Square, accum_out=st[:, 96 + b:97 + b]).then_inc(s_dq, 1)

        @block.vector
        def _(dve):
            chain = [0]

            def link(ins):
                chain[0] += 1
                ins.then_inc(s_dv, 1)
                dve.wait_ge(s_dv, chain[0])

            def normalise(b):
                dve.wait_ge(s_rs, b + 1)
                dve.tensor_scalar(ring(raw, b), ring(raw, b), st[:, 8 + b:9 + b], None, ALU.mult).then_inc(s_xn, 1)

            def sum_chunk(n):
                if n == 0:
                    dve.wait_ge(s_cs, 1)
                dve.wait_ge(s_ada[n % 2], 16 * (n // 2 + 1))
                part = acc[:, n * 512:(n + 1) * 512]
                link(dve.tensor_scalar(part, chunk[n % 2][:, 0, :], ca[:, 1, 0:1], None, ALU.mult))
                for j in range(1, KT):
                    ins = dve.scalar_tensor_tensor(out=part, in0=chunk[n % 2][:, j, :], scalar=ca[:, 1, j:j + 1],
                                                   in1=part, op0=ALU.mult, op1=ALU.add)
                    if j < KT - 1:
                        link(ins)
                ins.then_inc(s_acc, 1)

            for b in range(NB):
                normalise(b)
                if b % 2:
                    sum_chunk(b // 2)

            dve.wait_ge(s_rT, 1)
            dve.tensor_copy(cols[:, :], bank(7)[:, 0:280]).then_inc(s_cols, 1)
            dve.wait_ge(s_ext, 1)
            dve.tensor_copy(ext_sb, bank(6)[0:H, 0:EXT]).then_inc(s_exs, 1)
            dve.wait_ge(s_cols, 1)

            def take_columns(n):
                link(dve.tensor_tensor(modc[:, 16 * n:16 * n + 16], bank(6)[:, EXT + 16 * n:EXT + 16 * n + 16],
                                       cols[:, 24 * n:24 * n + 16], ALU.add))
                dve.scalar_tensor_tensor(out=modc[:, 16 * n + 8:16 * n + 16], in0=modc[:, 16 * n + 8:16 * n + 16],
                                         scalar=1.0, in1=cols[:, 48 + 8 * n:56 + 8 * n],
                                         op0=ALU.add, op1=ALU.mult).then_inc(s_mod, 1)

            def take_gate(n, half):
                part = gate_rows[:, n, half * 512:(half + 1) * 512]
                link(dve.tensor_tensor(part, bank(7), part, ALU.add))
                dve.tensor_tensor(part, part, post_bc[:, n, half * 512:(half + 1) * 512], ALU.mult).then_inc(s_mod, 1)

            dve.wait_ge(s_mp, 1)
            take_columns(0)
            dve.wait_ge(s_mod, 1)
            dve.wait_ge(s_xe, NB)

            def modulate(k, n, c0, w, done):
                part = xnT[:, k, c0:c0 + w]
                dve.tensor_scalar(part, part, modc[:, 16 * n + 8 + k:16 * n + 9 + k],
                                  modc[:, 16 * n + k:16 * n + k + 1], ALU.mult, ALU.add).then_inc(done, 1)

            def h_lo(k, c0, w, done):
                dve.tensor_tensor(a_lo[:, k, c0:c0 + w], xnT[:, k, c0:c0 + w],
                                  a_hi[:, k, c0:c0 + w].bitcast(f32), ALU.subtract).then_inc(done, 1)

            def split_lo(u, du=0):
                dve.wait_ge(s_whi, du + (u + 1))
                dve.tensor_tensor(ring(w_lo, u), ring(raw, u), ring(w_hi, u).bitcast(f32), ALU.subtract)\
                    .then_inc(s_wlo, 1)

            modulate(0, 0, 0, T, s_h)
            split_lo(0)
            for k in range(KT):
                if k + 1 < KT:
                    modulate(k + 1, 0, 0, T, s_h)
                dve.wait_ge(s_hhi, k + 1)
                h_lo(k, 0, T, s_hlo)

            def conv_taps(n):
                m = CONV.index(n)
                dve.wait_ge(s_c0, m + 1)
                src = bank(2 * (n % 3), 2)
                for d in range(1, 4):
                    tap = C_CONV + 8 * (3 - d) + m
                    ins = dve.scalar_tensor_tensor(out=proj(n)[:, d:], in0=src[:, 0:T - d],
                                                   scalar=cols[:, tap:tap + 1], in1=proj(n)[:, d:],
                                                   op0=ALU.mult, op1=ALU.add)
                    if d < 3:
                        link(ins)
                ins.then_inc(s_evD, 1)

            split_lo(1)
            for n in range(U_DT):
                if 1 <= n < U_DT - 1:
                    split_lo(n + 1)
                if n >= 1 and n - 1 in CONV:
                    conv_taps(n - 1)
                if n < 4:
                    sum_chunk(4 + 2 * n)
                    sum_chunk(5 + 2 * n)
                if n == 3:
                    dve.wait_ge(s_late, 16 * N_LATE)
                    for half in range(2):
                        dve.wait_ge(s_mp, 2 + half)
                        take_gate(0, half)
                if n == 5:
                    dve.wait_ge(s_mp, 4)
                    take_columns(1)
                    for half in range(2):
                        dve.wait_ge(s_mp, 5 + half)
                        take_gate(1, half)
            dve.wait_ge(s_whi, U_DT + 1)
            wdt = ring(w_hi, U_DT).rearrange("p (k n) -> p k n", k=KT)
            dve.tensor_tensor(wdt[:, :, H:2 * H], raw_dt[:, :, :], wdt[:, :, 0:H].bitcast(f32), ALU.subtract)\
                .then_inc(s_wlo, 1)
            conv_taps(U_DT - 1)

            def slot(v):
                return dt_slot(v)

            def by_head(v):
                return dt_slot(v).rearrange("p (b h) -> p b h", h=H)

            def head_row(r):
                return hv[:, r, :].unsqueeze(1).to_broadcast([P, NB, H])

            dve.wait_ge(s_dtn, 1)
            link(dve.tensor_copy(dt_nat, bank(2)[:, 0:P].rearrange("p (b n) -> p b n", b=NB)))
            link(dve.tensor_tensor(by_head(T3), dt_nat[:, :, 0:H], dt_nat[:, :, H:2 * H], ALU.add))
            link(dve.tensor_tensor(by_head(T3), by_head(T3), head_row(DTB), ALU.add))
            dve.scalar_tensor_tensor(out=slot(T4), in0=slot(T3), scalar=-1.0, in1=slot(T3),
                                     op0=ALU.mult, op1=ALU.max).then_inc(s_dt1, 1)
            dve.wait_ge(s_dtA, 2)
            dve.tensor_scalar(slot(T4), slot(T2), 1.0, None, ALU.add).then_inc(s_dt1, 1)
            dve.wait_ge(s_dt1, 2)
            link(dve.tensor_scalar(slot(TE), slot(T4), -1.0, None, ALU.add))
            link(dve.tensor_scalar(slot(CD), slot(TE), 0.0, None, ALU.is_equal))
            link(dve.tensor_tensor(slot(TE), slot(TE), slot(CD), ALU.add))
            link(dve.reciprocal(slot(TE), slot(TE)))
            link(dve.tensor_tensor(slot(TE), slot(TE), slot(T2), ALU.mult))
            dve.wait_ge(s_dtA, 3)
            link(dve.tensor_tensor(slot(FS), slot(FS), slot(CD), ALU.add))
            link(dve.tensor_tensor(slot(FS), slot(FS), slot(TE), ALU.mult))
            link(dve.scalar_tensor_tensor(out=slot(DT), in0=slot(T3), scalar=0.0, in1=slot(FS),
                                          op0=ALU.max, op1=ALU.add))
            link(dve.tensor_tensor(by_head(ADT), by_head(DT), head_row(EA), ALU.mult))
            dve.tensor_scalar(slot(ADT), slot(ADT), -1.0, None, ALU.mult).then_inc(s_dte, 1)
            dve.wait_ge(s_dtA, 4)
            link(dve.tensor_tensor(slot(TE), slot(TE), slot(DT), ALU.mult))
            nsink = hv[:, DTB, :]
            link(dve.tensor_scalar(nsink, hv[:, SINK, :], -1.0, None, ALU.mult))

            def scores(i, j):
                u = NPAIR * i + j
                k0 = P if i == 0 else 0
                s2 = bank(0, 2).rearrange("p (e k) -> p e k", e=2)
                dst = prob[:, u % 2, :, k0:]
                dve.wait_ge(s_S, u + 1)
                if u >= 2:
                    dve.wait_ge(s_pT, u - 1)
                if u == 0:
                    dve.wait_ge(s_bias, NPAIR)
                dve.scalar_tensor_tensor(out=dst, in0=s2[:, :, k0:2 * P], scalar=HD ** -0.5, in1=bias[:, j, :, k0:],
                                         op0=ALU.mult, op1=ALU.add).then_inc(s_sb, 1)
                dve.wait_ge(s_sb, u + 1)
                link(dve.tensor_reduce(mx, dst, AX.X, ALU.max))
                dve.scalar_tensor_tensor(out=hv[:, NM, j::NPAIR], in0=mx, scalar=-1.0, in1=nsink[:, j::NPAIR],
                                         op0=ALU.mult, op1=ALU.min).then_inc(s_nm, 1)

            def at(v, i):
                return per_head(dtv[:, v, i * H:(i + 1) * H])

            def mix_lo(i, part):
                dve.wait_ge(s_mh, 2 * i + (2 if part == 0 else 1))
                dst = (slice(None), slice(4 * part, 4 * part + 4), slice(i * P, (i + 1) * P))
                dve.tensor_tensor(a_lo[dst], bank(6 + part).rearrange("p (k t) -> p k t", k=4),
                                  a_hi[dst].bitcast(f32), ALU.subtract).then_inc(s_ml, 1)

            for i in range(NB):
                dve.wait_ge(s_xsT, i + 1)
                dve.tensor_tensor(heads(xc), heads(bank(6)), at(DT, i), ALU.mult)
                dve.tensor_tensor(heads(xc_end), heads(bank(6)), at(TE, i), ALU.mult)
                xd = four(XS, i).rearrange("p t (e d) -> p t e d", e=2)
                dve.tensor_tensor(xd, bank(6).rearrange("p (t e d) -> p t e d", t=4, e=2),
                                  hv[:, DD, :].rearrange("p (t e) -> p t e", e=2).unsqueeze(3)
                                  .to_broadcast([P, 4, 2, HD]), ALU.mult).then_inc(s_xc, 1)
                dve.wait_ge(s_cb, i + 1)
                dve.tensor_tensor(cbm, bank(7)[:, 0:256].rearrange("p (g l) -> p g l", g=2),
                                  upper.unsqueeze(1).to_broadcast([P, 2, P]), ALU.mult).then_inc(s_cbm, 1)
                scores(i, 0)
                scores(i, 1)
                dve.wait_ge(s_cbm, i + 1)
                for g in range(GROUPS):
                    dve.wait_ge(s_E, 2 * i + g + 1)
                    dg = decay[:, g, :].rearrange("p (h l) -> p h l", h=4)
                    dve.tensor_tensor(dg, dg, cbm[:, g, :].unsqueeze(1).to_broadcast([P, 4, P]),
                                      ALU.mult).then_inc(s_W, 1)
                scores(i, 2)
                dve.wait_ge(s_yo, i + 1)
                dve.tensor_tensor(heads(yy), heads(bank(5)), at(FS, i), ALU.mult).then_inc(s_ya, 1)
                dve.wait_ge(s_ya, i + 1)
                dve.wait_ge(s_yd, i + 1)
                dve.tensor_tensor(yy, yy, bank(6), ALU.add).then_inc(s_yb, 1)
                link(dve.tensor_tensor(heads(state), heads(state), at(CD, i), ALU.mult))
                dve.wait_ge(s_sn, i + 1)
                dve.tensor_tensor(state, state, bank(7), ALU.add).then_inc(s_su, 1)
                dve.wait_ge(s_yb, i + 1)
                y4 = yy.rearrange("p (t n) -> p t n", t=4)
                link(dve.tensor_tensor(y4, y4, four(XS, i), ALU.add))
                dve.wait_ge(s_zT, i + 1)
                dve.tensor_tensor(yy, yy, bank(5), ALU.mult).then_inc(s_g, 1)
                scores(i, 3)
                dve.wait_ge(s_gr, i + 1)
                for g in range(GROUPS):
                    ins = dve.scalar_tensor_tensor(
                        out=four(Z, i)[:, 2 * g:2 * g + 2, :], in0=y4[:, 2 * g:2 * g + 2, :],
                        scalar=st[:, 58 + g:59 + g],
                        in1=normw[:, g * 256:(g + 1) * 256].rearrange("p (a b) -> p a b", a=2),
                        op0=ALU.mult, op1=ALU.mult)
                ins.then_inc(s_my, 1)
                if i >= 1:
                    dve.wait_ge(s_es, i)
                dve.wait_ge(s_nm, NPAIR * (i + 1))
                dve.tensor_tensor(esk, hv[:, NM, :], hv[:, SINK, :], ALU.add).then_inc(s_nms, 1)
                dve.wait_ge(s_es, i + 1)
                link(dve.tensor_tensor(hv[:, DEN, :], hv[:, DEN, :], esk, ALU.add))
                link(dve.reciprocal(hv[:, REC, :], hv[:, DEN, :]))
                dve.wait_ge(s_pv, NPAIR * (i + 1))
                dve.tensor_tensor(four(Q, i).rearrange("p t (e d) -> p t e d", e=2),
                                  bank(4).rearrange("p (t e d) -> p t e d", t=4, e=2),
                                  hv[:, REC, :].rearrange("p (t e) -> p t e", e=2).unsqueeze(3)
                                  .to_broadcast([P, 4, 2, HD]), ALU.mult).then_inc(s_o, 1)
                mix_lo(i, 1)
                mix_lo(i, 0)

            for t in range(U_UP - U_OUT):
                split_lo(U_OUT + t)
            split_lo(U_UP)
            dve.wait_ge(s_xr, 16)
            for b in range(NB + 1):
                if b < NB:
                    dve.wait_ge(s_mr, b + 1)
                    if b >= 1:
                        dve.wait_ge(s_mx, b)
                    for half in range(2):
                        part = xr[:, b, half * 512:(half + 1) * 512]
                        link(dve.scalar_tensor_tensor(
                            out=mixed_t, in0=bank(b) if half else mixed0[:, b, :], scalar=st[:, 80 + b:81 + b],
                            in1=gate_rows[:, 0, half * 512:(half + 1) * 512], op0=ALU.mult, op1=ALU.mult))
                        ins = dve.tensor_tensor(part, part, mixed_t, ALU.add)
                        if half == 0:
                            link(ins)
                    ins.then_inc(s_mx, 1)
                if b >= 1:
                    dve.wait_ge(s_r2, b)
                    if b >= 3:
                        dve.wait_ge(s_T2, b - 2)
                    dve.tensor_scalar(xn2[:, (b - 1) % 2, :], xr[:, b - 1, :], st[:, 40 + b - 1:40 + b], None,
                                      ALU.mult).then_inc(s_n2, 1)
            for hf in range(2):
                dve.wait_ge(s_e2, 4 * (hf + 1))
                modulate(0, 1, hf * 512, 512, s_h2)
                for k in range(KT):
                    if k + 1 < KT:
                        modulate(k + 1, 1, hf * 512, 512, s_h2)
                    dve.wait_ge(s_h2h, KT * hf + k + 1)
                    h_lo(k, hf * 512, 512, s_h2l)

            def column(base, i, t):
                return cols[:, bass.ds(i * 2 + (base + t // 2 + FT * (t % 2)), 1)]

            def f_tile(k):
                return flat(big[:, bass.ds(k, 1), :])

            def up_taps(i, t):
                dst = f_tile(i * 2 + t // 2) if t % 2 else gate_t[:, t // 2, :]
                src = bank(2 * t, 2)
                dve.wait_ge(s_u0, i * 4 + (t + 1))
                dve.scalar_tensor_tensor(out=dst[:, 1:], in0=src[:, 0:T - 1], scalar=column(C_FFN + 44, i, t),
                                         in1=dst[:, 1:], op0=ALU.mult, op1=ALU.add).then_inc(s_uc, 1)
                dve.wait_ge(s_uc, i * 4 + (t + 1))
                dve.scalar_tensor_tensor(out=dst[:, 2:], in0=src[:, 0:T - 2], scalar=column(C_FFN, i, t),
                                         in1=dst[:, 2:], op0=ALU.mult, op1=ALU.add).then_inc(s_u1, 1)

            def up_gate(i, pr):
                dst = f_tile(i * 2 + pr)
                dve.wait_ge(s_ge, i * 2 + (pr + 1))
                dve.wait_ge(s_u1, i * 4 + (2 * pr + 2))
                dve.tensor_tensor(dst, dst, gate_t[:, pr, :], ALU.mult).then_inc(s_f, 1)

            def up_body(i):
                for t in range(4):
                    split_lo(U_UP + t + 1, i * 4)
                    up_taps(i, t)
                    if t % 2:
                        up_gate(i, t // 2)

            up_body(0)
            with dve.Fori(1, FT // 2) as i:
                up_body(i)

            def f_split_lo(half, kk, e):
                dve.wait_ge(s_fh, kk * 2 + (FT * half + e + 1))
                dve.tensor_tensor(a_lo[:, e, :], f_tile(kk * 2 + e), a_hi[:, e, :].bitcast(f32),
                                  ALU.subtract).then_inc(s_fl, 1)

            def down_unit(half, kk0, dk, split_next=True):
                for e in range(2):
                    f_split_lo(half, dk + kk0, e)
                if split_next:
                    split_lo(U_DOWN + DOWN_UNITS * half + kk0 + 1, dk)

            for half in range(2):
                down_unit(half, 0, 0)
                with dve.Fori(0, 4) as i:
                    down_unit(half, 1, i * 2)
                    down_unit(half, 2, i * 2)
                down_unit(half, 9, 0)
                down_unit(half, 10, 0, split_next=half == 0)

            dve.wait_ge(s_x1l, 16 * NB)
            for b in range(NB):
                row = ring(raw, b)
                dve.wait_ge(s_dr, b + 1)
                if b >= 2:
                    dve.wait_ge(s_out[b % 2], 16 * (b // 2))
                for half in range(2):
                    ins = dve.scalar_tensor_tensor(
                        out=row[:, half * 512:(half + 1) * 512], in0=bank(b) if half else half0[:, b, :],
                        scalar=st[:, 104 + b:105 + b], in1=gate_rows[:, 1, half * 512:(half + 1) * 512],
                        op0=ALU.mult, op1=ALU.mult)
                link(ins)
                x1 = (a_hi if b < 4 else a_lo)[:, 4 + b % 4, :].bitcast(f32)
                dve.tensor_tensor(row, row, x1, ALU.add).then_inc(s_do, 1)

        @block.tensor
        def _(pe):
            pe.wait_ge(s_const, 48)
            pe.wait_ge(s_small, 16 * N_SMALL)
            for b in range(NB):
                pe.wait_ge(s_xn, b + 1)
                if b >= 3:
                    pe.wait_ge(s_xe, b - 2)
                for k in range(KT):
                    mm = pe.transpose(bank(2 * (b % 3), 2)[:, k * P:(k + 1) * P],
                                      ring(raw, b)[:, k * P:(k + 1) * P], ident)
                mm.then_inc(s_xT, 1)

            pe.wait_ge(s_sq, NB)
            c0 = 0
            for m, n in enumerate([N_MOD_ROWS, N_CONV_ROWS, N_FFN_ROWS, N_FFN_ROWS]):
                mm = pe.transpose(bank(7)[:, c0:c0 + n], rows[0:n, m, :], ident[0:n, 0:n])
                c0 += n
            mm.then_inc(s_rT, 1)
            pe.matmul(bank(6)[0:H, 0:EXT], rb_sb, hot_sb, start=True, stop=True).then_inc(s_ext, 1)

            def sum_columns(first, col):
                for f in range(16):
                    src = first * 512 + f * P
                    mm = pe.matmul(bank(6)[:, col + f:col + f + 1], acc[:, src:src + P], ones[:, 0:1],
                                   start=True, stop=True)
                mm.then_inc(s_mp, 1)

            def sum_gate(n):
                pe.matmul(bank(7), ones[:, :], acc[:, n * 512:(n + 1) * 512], start=True, stop=True)\
                    .then_inc(s_mp, 1)

            pe.wait_ge(s_pool, 1)
            pe.wait_ge(s_acc, 4)
            pe.wait_ge(s_exs, 1)
            sum_columns(0, EXT)

            def split_products(out, lhs_of, rhs_of, start, stop):
                pe.matmul(out, lhs_of[0], rhs_of[0], start=start, stop=False)
                pe.matmul(out, lhs_of[0], rhs_of[1], start=False, stop=False)
                return pe.matmul(out, lhs_of[1], rhs_of[0], start=False, stop=stop)

            def features(n, u, waits=None):
                out = bank(n, 2)
                for k in range(KT):
                    if waits:
                        waits(k)
                    cs = slice(k * P, (k + 1) * P)
                    wh, wl = ring(w_hi, u)[:, cs], ring(w_lo, u)[:, cs]
                    for stationary, moving, first, last in ((wh, a_hi, k == 0, False), (wh, a_lo, False, False),
                                                            (wl, a_hi, False, k == KT - 1)):
                        for hf in range(2):
                            mm = pe.matmul(out[:, hf * 512:(hf + 1) * 512], stationary,
                                           moving[:, k, hf * 512:(hf + 1) * 512], start=first, stop=last)
                return mm

            def bank_free(n):
                m = n - 3
                if m in CONV:
                    pe.wait_ge(s_evD, CONV.index(m) + 1)
                elif m >= 0:
                    pe.wait_ge(s_evA, len([v for v in range(m + 1) if v not in CONV]))

            for n in range(U_DT):
                pe.wait_ge(s_wlo, n + 1)
                if n == 0:
                    pe.wait_ge(s_xe, NB)
                bank_free(n)
                features(2 * (n % 3), n, (lambda k: pe.wait_ge(s_hlo, k + 1)) if n == 0 else None)\
                    .then_inc(s_wu, 1)
                if n == 2:
                    pe.wait_ge(s_acc, 6)
                    pe.wait_ge(s_cols, 1)
                    sum_gate(4)
                    pe.wait_ge(s_mod, 2)
                    sum_gate(5)
                if n == 4:
                    pe.wait_ge(s_acc, 12)
                    pe.wait_ge(s_mod, 1)
                    sum_columns(6, EXT + 16)
                    pe.wait_ge(s_mod, 3)
                    sum_gate(10)
                    pe.wait_ge(s_mod, 5)
                    sum_gate(11)

            pe.wait_ge(s_wlo, U_DT + 1)
            bank_free(U_DT)
            for k in range(KT):
                w = ring(w_hi, U_DT)[:, k * P:(k + 1) * P]
                for m, moving in enumerate((a_hi, a_lo)):
                    for hf in range(2):
                        mm = pe.matmul(bank(hf), w, moving[:, k, hf * 512:(hf + 1) * 512],
                                       start=(k == 0 and m == 0), stop=(k == KT - 1 and m == 1))
            mm.then_inc(s_wu, 1)

            bank_free(U_DT + 2)
            pe.wait_ge(s_bl, 32)
            for j in range(NPAIR):
                if j >= 2:
                    pe.wait_ge(s_bias, j - 1)
                pe.matmul(bank(4 + j % 2), flip, bias[:, j], start=True, stop=True).then_inc(s_flp, 1)

            pe.wait_ge(s_dtT, 1)
            bank_free(U_DT + 1)
            for b in range(NB):
                mm = pe.transpose(bank(2)[:, 16 * b:16 * b + 16], dt_rows[:, b * P:(b + 1) * P], ident[0:16, 0:16])
            mm.then_inc(s_dtn, 1)
            pe.wait_ge(s_dte, 1)
            for v, m in enumerate((upper, strict, ones[:, :])):
                mm = pe.matmul(bank(3)[:, 64 * v:64 * v + 64], m, dtv[:, ADT, :], start=True, stop=True)
            mm.then_inc(s_dtc, 1)

            def score(i, j):
                u = NPAIR * i + j
                if u >= 1:
                    pe.wait_ge(s_sb, u)
                k0, w = (P, 1) if i == 0 else (0, 2)
                for e in range(2):
                    rs = slice(e * HD, (e + 1) * HD)
                    mm = pe.matmul(bank(e)[:, k0:2 * P], blk(Q + j, i)[rs],
                                   blk(K, i + 1 - w, w)[rs], start=True, stop=True)
                mm.then_inc(s_S, 1)

            def probs_transpose(i, j):
                u = NPAIR * i + j
                pe.wait_ge(s_p, u + 1)
                if u >= 2:
                    pe.wait_ge(s_pe, u - 1)
                else:
                    pe.wait_ge(s_dtA, 4)
                for e in range(2):
                    for kb in range(1 if i == 0 else 0, 2):
                        at = (2 * e + kb) * P
                        mm = pe.transpose(bank(2 + u % 2)[:, at:at + P],
                                          prob[:, u % 2, e, kb * P:(kb + 1) * P], ident)
                mm.then_inc(s_pT, 1)

            def values(i, j):
                u = NPAIR * i + j
                pe.wait_ge(s_pe, u + 1)
                if j == 0:
                    pe.wait_ge(s_vb, 2 * i + 1)
                    if i >= 1:
                        pe.wait_ge(s_o, i)
                for e in range(2):
                    h = j + 4 * e
                    k0 = 1 if i == 0 else 0
                    for kb in range(k0, 2):
                        at = (2 * e + kb) * P
                        mm = pe.matmul(bank(4)[:, h * HD:(h + 1) * HD], probT[:, u % 2, at:at + P],
                                       vb[:, (i + 1 - kb) % 2 if kb == 0 else i % 2, e * HD:(e + 1) * HD],
                                       start=(kb == k0), stop=(kb == 1))
                mm.then_inc(s_pv, 1)

            def transpose_four(dst, src):
                for t in range(4):
                    mm = pe.transpose(bank(dst)[:, t * P:(t + 1) * P], src[:, t, :], ident)
                return mm

            pe.wait_ge(s_bias, NPAIR)
            pe.wait_ge(s_si, len(CONV))
            for i in range(NB):
                if i >= 1:
                    pe.wait_ge(s_g, i)
                pe.transpose(bank(5)[:, 0:P], blk(V, i), ident)
                for g in range(GROUPS):
                    mm = pe.transpose(bank(5)[:, (g + 1) * P:(g + 2) * P], blk(BB + g, i), ident)
                mm.then_inc(s_t1, 1)
                if i >= 1:
                    pe.wait_ge(s_ml, 2 * i)
                transpose_four(6, four(XS, i)).then_inc(s_xsT, 1)
                for g in range(GROUPS):
                    mm = pe.matmul(bank(7)[:, g * P:(g + 1) * P], blk(BB + g, i), blk(CC + g, i),
                                   start=True, stop=True)
                mm.then_inc(s_cb, 1)
                score(i, 0)
                pe.wait_ge(s_vb, 2 * i + 2)
                pe.wait_ge(s_rd, 2 * i + 1)
                pe.matmul(bank(5), strict, decay[:, 0, :], start=True, stop=True).then_inc(s_D, 1)
                pe.wait_ge(s_cbm, i + 1)
                pe.wait_ge(s_rd, 2 * i + 2)
                pe.matmul(bank(7), strict, decay[:, 1, :], start=True, stop=True).then_inc(s_D, 1)
                score(i, 1)
                probs_transpose(i, 0)
                score(i, 2)
                probs_transpose(i, 1)
                values(i, 0)
                pe.wait_ge(s_E, 2 * i + 1)
                if i >= 1:
                    pe.wait_ge(s_su, i)
                for g in range(GROUPS):
                    mm = pe.matmul(bank(5)[:, g * 256:(g + 1) * 256], blk(CC + g, i),
                                   state[:, g * 256:(g + 1) * 256], start=True, stop=True)
                mm.then_inc(s_yo, 1)
                pe.wait_ge(s_xc, i + 1)
                pe.wait_ge(s_W, 2 * i + 2)
                for h in range(H):
                    mm = pe.matmul(bank(6)[:, h * HD:(h + 1) * HD], decay[:, h // 4, (h % 4) * P:(h % 4 + 1) * P],
                                   xc[:, h * HD:(h + 1) * HD], start=True, stop=True)
                mm.then_inc(s_yd, 1)
                for g in range(GROUPS):
                    mm = pe.matmul(bank(7)[:, g * 256:(g + 1) * 256], bn[:, g, :],
                                   xc_end[:, g * 256:(g + 1) * 256], start=True, stop=True)
                mm.then_inc(s_sn, 1)
                score(i, 3)
                probs_transpose(i, 2)
                values(i, 1)
                pe.wait_ge(s_ya, i + 1)
                transpose_four(5, four(Z, i)).then_inc(s_zT, 1)
                probs_transpose(i, 3)
                values(i, 2)
                values(i, 3)
                pe.wait_ge(s_my, i + 1)
                transpose_four(7, four(Z, i)).then_inc(s_mT, 1)
                pe.wait_ge(s_o, i + 1)
                transpose_four(6, four(Q, i)).then_inc(s_mT, 1)

            def row_products(u, e, slot, first, last, per_bank=None, done=None):
                ws = slice(e * 512, (e + 1) * 512)
                for b in range(NB):
                    if per_bank:
                        per_bank(b)
                    ts = slice(b * P, (b + 1) * P)
                    mm = split_products(bank(b), (a_hi[:, slot, ts], a_lo[:, slot, ts]),
                                        (ring(w_hi, u)[:, ws], ring(w_lo, u)[:, ws]), first, last)
                    if done is not None and b < NB - 1:
                        mm.then_inc(done, 1)
                return mm

            pe.wait_ge(s_ml, 2 * NB)
            for t in range(U_UP - U_OUT):
                pe.wait_ge(s_wlo, U_OUT + t + 1)
                for e in range(2):
                    k = 2 * (t % 4) + e
                    mm = row_products(U_OUT + t, e, k, k == 0, k == KT - 1,
                                      (lambda b: pe.wait_ge(s_m0, b + 1)) if t == 4 and e == 0 else None,
                                      s_mo if k == KT - 1 else None)
                mm.then_inc(s_wu, 1)

            for b in range(NB):
                pe.wait_ge(s_n2, b + 1)
                pe.wait_ge(s_mx, 2 * (b % 2) + 2)
                if b >= 2:
                    pe.wait_ge(s_e2, b - 1)
                for k in range(KT):
                    mm = pe.transpose(bank(2 * (b % 2), 2)[:, k * P:(k + 1) * P],
                                      xn2[:, b % 2, k * P:(k + 1) * P], ident)
                mm.then_inc(s_T2, 1)

            def up_tile(i, t, first):
                pe.wait_ge(s_wlo, i * 4 + (U_UP + t + 1))
                if first:
                    pe.wait_ge(s_e2, NB)
                else:
                    pe.wait_ge(s_u1, i * 4 + (t - 3))
                if first and t == 0:
                    pe.wait_ge(s_h2l, 2 * KT)
                features(2 * t, U_UP + t).then_inc(s_wu, 1)

            for t in range(4):
                up_tile(0, t, True)
            with pe.Fori(1, FT // 2) as i:
                for t in range(4):
                    up_tile(i, t, False)

            def down_unit(half, kk0, dk):
                u = U_DOWN + DOWN_UNITS * half + kk0
                pe.wait_ge(s_wlo, dk + (u + 1))
                for e in range(2):
                    q = FT * half + 2 * kk0 + e
                    pe.wait_ge(s_fl, dk * 2 + (q + 1))
                    first, last = kk0 == 0 and e == 0, kk0 == DOWN_UNITS - 1 and e == 1
                    bank_ready = None
                    if first and half == 0:
                        pe.wait_ge(s_u1, 2 * FT)
                    if first and half == 1:
                        def bank_ready(b):
                            pe.wait_ge(s_d0, b + 1)
                    mm = row_products(u, e, e, first, last, bank_ready, s_dn if last else None)
                    if e == 0:
                        mm.then_inc(s_fu, 1)
                mm.then_inc(s_wu, 1)

            for half in range(2):
                down_unit(half, 0, 0)
                with pe.Fori(0, 4) as i:
                    down_unit(half, 1, i * 2)
                    down_unit(half, 2, i * 2)
                down_unit(half, 9, 0)
                down_unit(half, 10, 0)


_INS = ["x", "c", "rel_bias", "w_ada", "b_ada", "pre_mix_w", "w_in", "attn_sinks", "ssm_conv_w", "ssm_conv_b",
        "ssm_dt_bias", "ssm_a_log", "ssm_d", "ssm_norm_w", "w_out", "post_mix_w", "pre_ffn_w", "w_up",
        "ffn_conv_w", "ffn_conv_b", "w_down", "post_ffn_w"]


def kernel(**inputs):
    import concourse.bacc as _bacc
    from concourse.bass_utils import run_bass_kernel_spmd as _run

    nc = _bacc.Bacc("TRN2", target_bir_lowering=False, num_devices=1)
    arrays, args = {}, []
    named = [(name, np.ascontiguousarray(inputs[name])) for name in _INS]
    named += list(zip(("squares", "hot"), shape_constants()))
    for name, a in named:
        arrays[f"in_{name}_dram"] = a
        args.append(nc.dram_tensor(f"in_{name}_dram", a.shape, mybir.dt.from_np(a.dtype), kind="ExternalInput").ap())
    args.append(nc.dram_tensor("out_dram", (1, T, D), mybir.dt.float32, kind="ExternalOutput").ap())
    hybrid_layer_kernel(nc, *args)
    r = _run(nc, [arrays], core_ids=[0])
    return r.results[0]["out_dram"]
```

```python
import math
from contextlib import ExitStack

import numpy as np
import concourse.bass as bass
from concourse import mybir

D = 1024
T = 1024
P = 128
KT = D // P
NB = T // P
H = 8
HD = 64
NPAIR = H // 2
GROUPS = 2
FF = 2816
FT = FF // P
NBUCKET = 32
EXT = 3 * P
EPS = 1e-6
NEG = -1e30

U_IN, U_DT, U_OUT, U_UP, U_DOWN = 0, 14, 19, 27, 71
U_END = 93
DOWN_UNITS = FT // 2
SSM_W = H * HD
Q, K, V, CC, XS, BB, Z = 0, 4, 5, 6, 8, 12, 15
COLUMN = [0, 1, 2, 3, 4, 5, 16, 17, 6, 7, 8, 9, 14, 15, 18, 10, 11, 12, 13]
SLOT = [14, 15, 16, 17, 18, 19, 20, 21, 0, 1, 2, 3, 8, 9, None, 4, 5, 6, 7]
CONV = [8, 9, 10, 11, 12, 13, 6, 7]
CONV_BY_TIME = sorted(CONV)
SILU = CONV_BY_TIME + [15, 16, 17, 18]
BY_ACT = [n for n in range(U_OUT) if n not in CONV]
A0 = 7
N_PAIRS = NB * NPAIR
GATE_BANKS = [4, 5, 7, 4]
N_SMALL, N_LATE = 10, 10
N_CONV_ROWS = 40
N_FFN_ROWS = 88
N_MOD_ROWS = 64
C_CONV, C_FFN = N_MOD_ROWS, N_MOD_ROWS + N_CONV_ROWS


def shape_constants():
    i = np.arange(P)
    squares = np.concatenate([
        np.eye(P), i[:, None] <= i[None, :], i[:, None] > i[None, :], np.eye(P)[::-1]], axis=1)
    hot = np.zeros((NBUCKET + 1, EXT))
    for u in range(EXT):
        dist = 2 * P - 1 - u
        if 0 <= dist < P:
            half = NBUCKET // 2
            b = dist if dist < half else min(NBUCKET - 1, half + int(
                math.log(dist / half) / math.log(P / half) * (NBUCKET - half)))
            hot[b, u] = 1.0
        else:
            hot[NBUCKET, u] = 1.0
    return squares.astype(np.float32), hot.astype(np.float32)


def hybrid_layer_kernel(nc, x, c, rel_bias, w_ada, b_ada, pre_mix_w, w_in, attn_sinks, ssm_conv_w,
                        ssm_conv_b, ssm_dt_bias, ssm_a_log, ssm_d, ssm_norm_w, w_out, post_mix_w,
                        pre_ffn_w, w_up, ffn_conv_w, ffn_conv_b, w_down, post_ffn_w,
                        squares, hot, out):
    f32 = mybir.dt.float32
    f32r = mybir.dt.float32r
    ALU = mybir.AluOpType
    ACT = mybir.ActivationFunctionType
    AX = mybir.AxisListType

    x2, out2 = x[0], out[0]
    w_in2, w_out2, w_up2, w_down2, w_ada2 = w_in[0], w_out[0], w_up[0], w_down[0], w_ada[0]
    bias_d = nc.dram_tensor("bias_by_distance", (H, EXT), f32).ap()
    x1_d = nc.dram_tensor("residual_after_mixer", (T, D), f32).ap()

    ctx = ExitStack()
    with ctx:
        def sb(name, shape, dt=f32):
            return ctx.enter_context(nc.sbuf_tensor(name, shape, dt))

        def sem(name):
            return ctx.enter_context(nc.semaphore(name))

        big = sb("big", [P, FT, T])
        a_hi = sb("a_hi", [P, KT, T], f32r)
        a_lo = sb("a_lo", [P, KT, T], f32r)
        raw = sb("raw", [P, 2, T])
        w_hi = sb("w_hi", [P, 2, T], f32r)
        w_lo = sb("w_lo", [P, 2, T], f32r)
        scratch = sb("scratch", [P, 4 * T])
        gate_rows = sb("gate_rows", [P, 2, D])
        sq = sb("sq", [P, 3 * P])
        ones = sb("ones", [P, P])
        cols = sb("cols", [P, 280])
        modc = sb("modc", [P, 32])
        ca = sb("ca", [P, 2, KT])
        hv = sb("hv", [P, 8, H])
        dtv = sb("dtv", [P, 5, NB * H])
        st = sb("st", [P, 128])
        normw = sb("normw", [P, SSM_W])
        ident, upper, strict = sq[:, 0:P], sq[:, P:2 * P], sq[:, 2 * P:3 * P]
        flip = scratch[:, 3840:3968]
        raw_dt = scratch[:, 3968:4032].rearrange("p (k h) -> p k h", k=KT)
        ps = ctx.enter_context(nc.psum_tensor("ps", [P, 8 * 512], f32))

        def bank(b, n=1):
            return ps[:, b * 512:(b + n) * 512]

        def ring(t, u):
            return t[:, u % 2, :]

        def flat(tiles):
            return tiles.rearrange("p a b -> p (a b)")

        xnT = big[:, 14:22, :]
        acc = flat(big[:, 8:14, :])
        chunk = [flat(big[:, 4 * s:4 * s + 4, :]).rearrange("p (j n) -> p j n", j=KT) for s in range(2)]

        x1nT = big[:, 0:8, :]

        def proj(n):
            return big[:, SLOT[n], :]

        def blk(n, i, w=1):
            return big[:, SLOT[n], i * P:(i + w) * P]

        def four(n, i):
            return big[:, SLOT[n]:SLOT[n] + 4, i * P:(i + 1) * P]

        def heads(ap):
            return ap.rearrange("p (h d) -> p h d", h=H)

        def per_head(ap):
            return ap.unsqueeze(2).to_broadcast([P, H, HD])

        work = flat(big[:, 10:14, :])
        prob = work[:, 0:1024].rearrange("p (s e k) -> p s e k", s=2, e=2)
        probT = work[:, 1024:2048]
        tanh_t = work[:, 2048:4096].rearrange("p (s n) -> p s n", s=2)
        dt_rows = big[0:16, SLOT[Z + 3], :]
        dt_nat = big[:, SLOT[Z + 2], 0:128].rearrange("p (b n) -> p b n", b=NB)
        dt_tmp = big[:, SLOT[Z + 2], 128:320].rearrange("p (v n) -> p v n", v=3)
        bias = scratch[:, 0:2048].rearrange("p (j e k) -> p j e k", j=NPAIR, e=2)
        xr = work[:, 0:2048].rearrange("p (s n) -> p s n", s=2)
        xc, xc_end = work[:, 2048:2560], work[:, 2560:3072]
        yy, state = work[:, 3072:3584], work[:, 3584:4096]
        xn2 = scratch[:, 0:2048].rearrange("p (s n) -> p s n", s=2)
        decay = scratch[:, 2048:3072].rearrange("p (g n) -> p g n", g=2)
        cbm = scratch[:, 3072:3328].rearrange("p (g l) -> p g l", g=2)
        bn = scratch[:, 3328:3584].rearrange("p (g n) -> p g n", g=2)
        junk = [big[:, SLOT[n], :] for n in (K, V)]
        rows = scratch[:, 2048:2560].rearrange("p (t n) -> p t n", t=4)
        post_bc = scratch[:, 0:2048].rearrange("p (t n) -> p t n", t=2)
        hot_sb = scratch[0:NBUCKET + 1, 2560:2560 + EXT]
        rb_sb = scratch[0:NBUCKET + 1, 2944:2944 + H]
        ext_sb = scratch[0:H, 2960:2960 + EXT]
        gate_t = scratch[:, 0:2048].rearrange("p (s n) -> p s n", s=2)
        half0 = scratch[:, 0:4096].rearrange("p (b n) -> p b n", b=NB)
        junk_r = a_lo[:, 2, 0:512]

        SINK, DTB, EA, DD, NM, DEN, DEN_ODD, REC = range(8)
        DT, ADT, FS, TE, CD, T2, T3, T4 = range(8)
        minus_half = st[:, 62:63]

        def dt_slot(v):
            return dtv[:, v, :] if v <= CD else dt_tmp[:, v - T2, :]

        esk = [st[:, 64:72], st[:, 72:80]]
        mx = st[:, 112:114]
        nsink = st[:, 114:122]

        def den(i):
            return hv[:, DEN + i % 2, :]

        def out_bank(b):
            return 0 if b < NB - 1 else 6

        s_const = sem("c_and_constants_loaded")
        s_small, s_late = sem("early_vectors_loaded"), sem("late_vectors_loaded")
        s_x = [sem(f"x_block_loaded{i}") for i in range(2)]
        s_ada = [sem(f"ada_chunk_loaded{i}") for i in range(2)]
        s_w = [sem(f"w_unit_loaded{i}") for i in range(2)]
        s_bd, s_bl = sem("bias_vectors_stored"), sem("bias_windows_loaded")
        s_xr = [sem(f"x_reloaded{i}") for i in range(2)]
        s_x1 = [sem(f"x1_stored{i}") for i in range(2)]
        s_x1l = sem("x1_reloaded")
        s_out = [sem(f"out_stored{i}") for i in range(2)]
        s_pool, s_pc = sem("pool_constants"), sem("pool_chain")
        s_cs = sem("silu_c_ready")
        s_sq, s_rs = sem("x_squares_summed"), sem("x_rstd_ready")
        s_xn, s_xT, s_xe = sem("xn_ready"), sem("xn_transposed"), sem("xnT_evacuated")
        s_acc = sem("ada_chunk_summed")
        s_rT, s_cols = sem("vector_rows_transposed"), sem("columns_ready")
        s_mp, s_mod = sem("mod_sums_in_psum"), sem("mod_ready")
        s_h, s_hhi, s_hlo = sem("h_modulated"), sem("h_hi_ready"), sem("h_lo_ready")
        s_whi, s_wlo, s_wu = sem("w_hi_ready"), sem("w_lo_ready"), sem("w_unit_used")
        s_evA, s_evD = sem("psum_freed_by_act"), sem("psum_freed_by_dve")
        s_c0, s_th, s_si = sem("conv_first_tap"), sem("tanh_done"), sem("silu_done")
        s_ext, s_exs = sem("bias_vectors_in_psum"), sem("bias_vectors_ready")
        s_flp, s_bias = sem("bias_flipped"), sem("bias_ready")
        s_dtT, s_dtn = sem("dt_evacuated"), sem("dt_transposed")
        s_dt1, s_dtA = sem("dt_steps_of_dve"), sem("dt_steps_of_act")
        s_dte, s_dtc, s_dt2 = sem("dt_a_ready"), sem("dt_a_sums_in_psum"), sem("dt_a_sums_taken")
        s_vT, s_v = sem("v_transposed"), sem("v_rows_ready")
        s_t1, s_bn = sem("b_transposed"), sem("b_rows_ready")
        s_xsT, s_xc = sem("xs_transposed"), sem("xc_ready")
        s_cb, s_cbm = sem("cb_in_psum"), sem("cb_masked")
        s_rd, s_D, s_E = sem("decay_terms_ready"), sem("segment_sums_in_psum"), sem("decay_ready")
        s_W = sem("ssd_weights_ready")
        s_yo, s_yd, s_sn = sem("y_off_in_psum"), sem("y_diag_in_psum"), sem("state_in_psum")
        s_ya, s_yb, s_su = sem("y_off_taken"), sem("y_diag_taken"), sem("state_updated")
        s_zT, s_g = sem("z_transposed"), sem("y_gated")
        s_gq, s_gr, s_my = sem("gated_squares"), sem("gated_rstd"), sem("ssm_rows_ready")
        s_S, s_sb = sem("scores_in_psum"), sem("scores_taken")
        s_nm, s_p = sem("neg_max_ready"), sem("probs_ready")
        s_pT, s_pe, s_pv = sem("probs_transposed"), sem("probsT_ready"), sem("pv_done")
        s_nms, s_es, s_o = sem("sink_minus_max"), sem("sink_exp"), sem("attention_rows_ready")
        s_mT, s_mh, s_ml = sem("mixed_rows_transposed"), sem("mixT_hi_ready"), sem("mixT_lo_ready")
        s_mq, s_mr, s_mx = sem("mixed_squares"), sem("mixed_rstd"), sem("x1_ready")
        s_q2, s_r2, s_n2 = sem("x1_squares"), sem("x1_rstd"), sem("x1_normalised")
        s_T2, s_e2 = sem("x1_transposed"), sem("x1T_evacuated")
        s_h2, s_h2h, s_h2l = sem("h2_modulated"), sem("h2_hi_ready"), sem("h2_lo_ready")
        s_ah, s_z0 = sem("h2_tile_used_up"), sem("z_halved")
        s_u0, s_uc, s_u1 = sem("up_first_tap"), sem("up_second_tap"), sem("up_taps_done")
        s_ge, s_f = sem("gelu_done"), sem("f_ready")
        s_fh, s_fl, s_fu = sem("f_hi_ready"), sem("f_lo_ready"), sem("f_first_tile_used")
        s_dn, s_d0 = sem("down_bank_done"), sem("down_half0_evacuated")
        s_dq, s_dr, s_do = sem("down_squares"), sem("down_rstd"), sem("out_rows_ready")
        s_dv, s_ac = sem("dve_chain"), sem("act_chain")

        block = ctx.enter_context(nc.Block())

        def bank_done(eng, s, half, b, u):
            if b < NB - 1:
                eng.wait_ge(s, (NB - 1) * half + b + 1)
            else:
                eng.wait_ge(s_wu, u + 1)

        def loaded(u):
            return 16 * (u // 2 + 1 + min(2, u // 2 + 1) - (u > U_DT and u % 2 == U_DT % 2))

        @block.sync
        def _(sp):
            sp.dma_start(ca[:, 0, :], c.rearrange("o (p j) -> p (o j)", j=KT)).then_inc(s_const, 16)
            sp.dma_start(sq[:, :], squares[:, 0:3 * P]).then_inc(s_const, 16)
            sp.dma_start(flip, squares[:, 3 * P:]).then_inc(s_const, 16)

            for m, (r0, v) in enumerate([(0, b_ada), (48, pre_mix_w), (56, pre_ffn_w)]):
                n = v.shape[1] // P
                sp.dma_start(rows[r0:r0 + n, 0, :], v[0].rearrange("(r n) -> r n", n=P)).then_inc(s_small, 16)
            sp.dma_start(rows[0:32, 1, :], ssm_conv_w[0].rearrange("t (m n) -> (t m) n", n=P)).then_inc(s_small, 16)
            sp.dma_start(rows[32:40, 1, :], ssm_conv_b[0].rearrange("(r n) -> r n", n=P)).then_inc(s_small, 16)

            def load_x(b):
                if b >= 2:
                    sp.wait_ge(s_xT, b - 1)
                sp.dma_start(ring(raw, b), x2[b * P:(b + 1) * P, :]).then_inc(s_x[b % 2], 16)

            def load_chunk(n):
                if n >= 2:
                    sp.wait_ge(s_acc, n - 1)
                sp.dma_start(chunk[n % 2], w_ada2[:, n * 512:(n + 1) * 512]
                             .rearrange("(p j) n -> p j n", j=KT)).then_inc(s_ada[n % 2], 16)

            load_x(0)
            load_x(1)
            load_chunk(0)
            fw = ffn_conv_w[0].rearrange("t (m n) -> (t m) n", n=P)
            sp.dma_start(rows[0:88, 2, :], fw[0:88, :]).then_inc(s_small, 16)
            sp.dma_start(rows[0:44, 3, :], fw[88:132, :]).then_inc(s_small, 16)
            sp.dma_start(rows[44:88, 3, :], ffn_conv_b[0].rearrange("(r n) -> r n", n=P)).then_inc(s_small, 16)
            sp.dma_start(hot_sb, hot).then_inc(s_small, 16)
            sp.wait_ge(s_pool, 1)
            sp.dma_start(rb_sb[0:NBUCKET, :], rel_bias).then_inc(s_small, 16)
            load_chunk(1)
            for b in range(2, NB):
                load_x(b)
                if b in (3, 5):
                    load_chunk((b + 1) // 2)

            def load_late():
                for dst, row in [(hv[:, SINK, :], attn_sinks), (hv[:, DTB, :], ssm_dt_bias),
                                 (hv[:, EA, :], ssm_a_log), (hv[:, DD, :], ssm_d), (normw[:, :], ssm_norm_w),
                                 (gate_rows[:, 0, :], b_ada[:, 2 * D:3 * D]),
                                 (gate_rows[:, 1, :], b_ada[:, 5 * D:6 * D]),
                                 (post_bc[:, 0, :], post_mix_w), (post_bc[:, 1, :], post_ffn_w)]:
                    sp.dma_start(dst, row.to_broadcast([P, row.shape[-1]])).then_inc(s_late, 16)
                sp.dma_start(raw_dt[:, :, :], w_in2.rearrange("(k p) n -> p k n", p=P)[:, :, 18 * P:18 * P + H])\
                    .then_inc(s_late, 16)

            in_src = w_in2.rearrange("(k p) n -> p k n", p=P)

            def load_in(n):
                dst = ring(raw, n).rearrange("p (k n) -> p k n", k=KT)
                c0 = COLUMN[n] * P
                if n < K:
                    for e in range(2):
                        h = n + 4 * e
                        sp.dma_start(dst[:, :, e * HD:(e + 1) * HD],
                                     in_src[:, :, h * HD:(h + 1) * HD]).then_inc(s_w[n % 2], 16)
                else:
                    sp.dma_start(dst, in_src[:, :, c0:c0 + P]).then_inc(s_w[n % 2], 16)

            for n in range(U_OUT):
                if n < 2:
                    sp.wait_ge(s_xT, 7 + n)
                else:
                    sp.wait_ge(s_wlo, n - 1)
                if n != U_DT:
                    load_in(n)
                if n == 0:
                    load_late()
                if 1 <= n < 5:
                    load_chunk(2 * n + 2)
                    load_chunk(2 * n + 3)

            def load_xr(b):
                sp.dma_start(xr[:, b % 2, :], x2[b * P:(b + 1) * P, :]).then_inc(s_xr[b % 2], 16)

            for k in range(KT):
                sp.wait_ge(s_wlo, U_OUT + k - 1)
                sp.dma_start(ring(raw, U_OUT + k), w_out2[k * P:(k + 1) * P, :]).then_inc(s_w[(U_OUT + k) % 2], 16)
            sp.wait_ge(s_pv, N_PAIRS)
            load_xr(0)
            load_xr(1)

            def load_rows(u, w, half, k0):
                sp.dma_start(ring(raw, u).rearrange("p (k n) -> p k n", k=2),
                             w[bass.ds(k0 * P, 2 * P), half * 512:(half + 1) * 512]
                             .rearrange("(k p) n -> p k n", p=P)).then_inc(s_w[u % 2], 16)

            def load_up(i, t):
                u = U_UP + t
                sp.wait_ge(s_wlo, i * 4 + (u - 1))
                col = i * (2 * P) + ((t // 2) * P + (t % 2) * FF)
                sp.dma_start(ring(raw, u).rearrange("p (k n) -> p k n", k=KT),
                             w_up2[:, bass.ds(col, P)].rearrange("(k p) n -> p k n", p=P))\
                    .then_inc(s_w[u % 2], 16)

            for t in range(2):
                load_up(0, t)
            for b in range(NB):
                sp.wait_ge(s_mx, b + 1)
                sp.dma_start(x1_d[b * P:(b + 1) * P, :], xr[:, b % 2, :]).then_inc(s_x1[b % 2], 16)
                if b + 2 < NB:
                    sp.wait_ge(s_n2, b + 1)
                    sp.wait_ge(s_x1[b % 2], 16 * (b // 2 + 1))
                    load_xr(b + 2)
            for t in range(2, 4):
                load_up(0, t)
            with sp.Fori(1, FT // 2) as i:
                for t in range(4):
                    load_up(i, t)

            for half in range(2):
                for kk in range(11):
                    u = U_DOWN + 11 * half + kk
                    sp.wait_ge(s_wlo, u - 1)
                    load_rows(u, w_down2, half, 2 * kk)
            for n in range(2):
                sp.wait_ge(s_x1[n], 16 * NB // 2)
            sp.wait_ge(s_wu, U_DOWN)
            for b in range(NB):
                dst = (a_hi if b < 4 else a_lo)[:, 4 + b % 4, :].bitcast(f32)
                sp.dma_start(dst, x1_d[b * P:(b + 1) * P, :]).then_inc(s_x1l, 16)
            for b in range(NB):
                sp.wait_ge(s_do, b + 1)
                sp.dma_start(out2[b * P:(b + 1) * P, :], ring(raw, b)).then_inc(s_out[b % 2], 16)
            for n in range(2):
                sp.wait_ge(s_out[n], 16 * NB // 2)

        @block.gpsimd
        def _(pool):
            pool.memset(rb_sb, NEG).then_inc(s_pool, 1)
            pool.memset(ones[:, :], 1.0).then_inc(s_pool, 1)
            pool.memset(minus_half, -0.5).then_inc(s_pool, 1)

            chain = [0]

            def link(ins):
                chain[0] += 1
                ins.then_inc(s_pc, 1)
                pool.wait_ge(s_pc, chain[0])

            def rstd(dst, src, width, done):
                link(pool.tensor_scalar(src, src, 1.0 / width, EPS, ALU.mult, ALU.add))
                power = minus_half if src.shape[1] == 1 else minus_half.to_broadcast(list(src.shape))
                pool.tensor_tensor(dst, src, power, ALU.pow).then_inc(done, 1)

            pool.wait_ge(s_pool, 3)
            for b in range(NB):
                pool.wait_ge(s_sq, b + 1)
                rstd(st[:, 8 + b:9 + b], st[:, b:b + 1], D, s_rs)

            pool.wait_ge(s_exs, 1)
            pool.dma_start(bias_d, ext_sb).then_inc(s_bd, 16)
            pool.wait_ge(s_bd, 16)
            pool.wait_ge(s_mod, 6)
            for e in range(2):
                src = bass.AP(bias_d.tensor, 4 * e * EXT, [[1, P], [EXT, NPAIR], [1, 2 * P]])
                pool.dma_start(bias[:, :, e, :], src).then_inc(s_bl, 16)

            def decay_terms(i):
                if i >= 1:
                    pool.wait_ge(s_yd, i)
                for g in range(GROUPS):
                    adt = dtv[:, ADT, i * H + 4 * g:i * H + 4 * g + 4].unsqueeze(2).to_broadcast([P, 4, P])
                    tri = upper.unsqueeze(1).to_broadcast([P, 4, P])
                    pool.tensor_tensor(decay[:, g, :].rearrange("p (h l) -> p h l", h=4), tri, adt,
                                       ALU.mult).then_inc(s_rd, 1)

            pool.wait_ge(s_dte, 1)
            decay_terms(0)
            pool.wait_ge(s_si, len(SILU))
            link(pool.memset(state, 0.0))
            for i in range(NB + 2):
                b = i - 2
                if b >= 0:
                    pool.wait_ge(s_mq, b + 1)
                    rstd(st[:, 80 + b:81 + b], st[:, 16 + b:17 + b], D, s_mr)
                    pool.wait_ge(s_q2, b + 1)
                    rstd(st[:, 40 + b:41 + b], st[:, 32 + b:33 + b], D, s_r2)
                if i + 1 < NB:
                    decay_terms(i + 1)
                if i < NB:
                    pool.wait_ge(s_gq, i + 1)
                    rstd(st[:, 58:60], st[:, 56:58], SSM_W // GROUPS, s_gr)
            for b in range(NB):
                pool.wait_ge(s_dq, b + 1)
                link(pool.tensor_tensor(st[:, 88 + b:89 + b], st[:, 88 + b:89 + b], st[:, 96 + b:97 + b], ALU.add))
                rstd(st[:, 104 + b:105 + b], st[:, 88 + b:89 + b], D, s_dr)

        @block.scalar
        def _(act):
            act.wait_ge(s_const, 48)
            act.activation(ca[:, 1, :], ca[:, 0, :], ACT.Silu).then_inc(s_cs, 1)
            chain = [0]

            def link(ins):
                chain[0] += 1
                ins.then_inc(s_ac, 1)
                act.wait_ge(s_ac, chain[0])

            def x_squares(b):
                act.wait_ge(s_x[b % 2], 16 * (b // 2 + 1))
                if b >= 1:
                    act.wait_ge(s_sq, b)
                act.activation(bank(6, 2), ring(raw, b), ACT.Square, accum_out=st[:, b:b + 1]).then_inc(s_sq, 1)

            def x_evacuate(b):
                act.wait_ge(s_xT, b + 1)
                act.activation(xnT[:, :, b * P:(b + 1) * P],
                               bank(2 * (b % 3), 2).rearrange("p (k t) -> p k t", k=KT), ACT.Copy).then_inc(s_xe, 1)

            for b in range(NB):
                x_squares(b)
                if b >= 1:
                    x_evacuate(b - 1)
            x_evacuate(NB - 1)

            def split_hi(u, du=0):
                slot = u % 2
                act.wait_ge(s_w[slot], du * 8 + loaded(u))
                if u >= 2:
                    act.wait_ge(s_wu, du + (u - 1))
                act.activation(ring(w_hi, u), ring(raw, u), ACT.Copy).then_inc(s_whi, 1)

            split_hi(0)
            for k in range(KT):
                act.wait_ge(s_h, k + 1)
                act.activation(a_hi[:, k, :], xnT[:, k, :], ACT.Copy).then_inc(s_hhi, 1)

            def evacuate(n):
                act.wait_ge(s_wu, n + 1)
                src = bank(2 * (n % 2), 2)
                if n == XS:
                    act.wait_ge(s_mod, 6)
                if n == U_DT:
                    act.activation(dt_rows, src[0:16, :], ACT.Copy).then_inc(s_dtT, 1)
                elif n in CONV:
                    m = CONV.index(n)
                    act.activation(proj(n), src, ACT.Identity, scale=cols[:, C_CONV + 24 + m:C_CONV + 25 + m],
                                   bias=cols[:, C_CONV + 32 + m:C_CONV + 33 + m]).then_inc(s_c0, 1)
                elif n >= Z:
                    if n == Z + 2:
                        act.wait_ge(s_dt1, 3)
                    act.activation(proj(n), src, ACT.Copy, scale=0.5).then_inc(s_z0, 1)
                else:
                    act.activation(proj(n), src, ACT.Copy).then_inc(s_evA, 1)

            def tanh(n):
                m = SILU.index(n)
                if m >= 2:
                    act.wait_ge(s_si, m - 1)
                if n in CONV:
                    act.wait_ge(s_evD, CONV_BY_TIME.index(n) + 1)
                else:
                    act.wait_ge(s_z0, n - Z + 1)
                act.activation(tanh_t[:, m % 2, :], proj(n), ACT.Tanh).then_inc(s_th, 1)

            def probs(u):
                i, j = u // NPAIR, u % NPAIR
                act.wait_ge(s_nm, u + 1)
                if j == 0 and i >= 2:
                    act.wait_ge(s_o, i - 1)
                k0 = P if i == 0 else 0
                for e in range(2):
                    h = j + 4 * e
                    ins = act.activation(prob[:, u % 2, e, k0:], prob[:, u % 2, e, k0:], ACT.Exp,
                                         bias=hv[:, NM, h:h + 1], accum_out=den(i)[:, h:h + 1])
                ins.then_inc(s_p, 1)
                if j == NPAIR - 1:
                    act.wait_ge(s_nms, i + 1)
                    act.activation(esk[i % 2], esk[i % 2], ACT.Exp).then_inc(s_es, 1)

            def probs_evacuate(u):
                act.wait_ge(s_pT, u + 1)
                if u >= 2:
                    act.wait_ge(s_pv, u - 1)
                src = bank(6).rearrange("p (e k q) -> p e k q", e=2, k=2)
                dst = probT[:, (u % 2) * 512:(u % 2 + 1) * 512].rearrange("p (e k q) -> p e k q", e=2, k=2)
                k0 = 1 if u < NPAIR else 0
                act.activation(dst[:, :, k0:, :], src[:, :, k0:, :], ACT.Copy).then_inc(s_pe, 1)

            def maybe(step, u):
                if 0 <= u < N_PAIRS:
                    step(u)

            split_hi(1)
            for n in range(1, U_OUT):
                if n + 1 == U_DT:
                    act.wait_ge(s_late, 16 * N_LATE)
                    act.wait_ge(s_wu, n)
                    wdt = ring(w_hi, U_DT).rearrange("p (k n) -> p k n", k=KT)
                    act.activation(wdt[:, :, 0:H], raw_dt[:, :, :], ACT.Copy).then_inc(s_whi, 1)
                elif n + 1 < U_OUT:
                    split_hi(n + 1)
                evacuate(n - 1)
                if n == 6:
                    for j in range(NPAIR):
                        act.wait_ge(s_flp, j + 1)
                        act.activation(bias[:, j], bank(4 + j % 2).rearrange("p (e k) -> p e k", e=2), ACT.Copy)\
                            .then_inc(s_bias, 1)
                    act.wait_ge(s_vT, 1)
                    act.activation(proj(V), bank(6, 2), ACT.Copy).then_inc(s_v, 1)
                u = 3 * (n - A0)
                maybe(probs_evacuate, u - 2)
                maybe(probs, u)
                if n == U_DT + 1:
                    act.wait_ge(s_dt1, 1)
                    act.activation(dt_slot(T2), dt_slot(T4), ACT.Exp, scale=-1.0).then_inc(s_dtA, 1)
                    act.activation(hv[:, EA, :], hv[:, EA, :], ACT.Exp).then_inc(s_dtA, 1)
                if n == U_DT + 2:
                    act.wait_ge(s_dt2, 1)
                    act.activation(dtv[:, FS:CD + 1, :], dtv[:, FS:CD + 1, :], ACT.Exp).then_inc(s_dtA, 1)
                maybe(probs_evacuate, u - 1)
                if n >= A0:
                    maybe(probs_evacuate, u)
                    maybe(probs, u + 1)
                    if n == U_DT + 1:
                        act.wait_ge(s_dt1, 2)
                        act.activation(dtv[:, FS, :], dt_slot(T4), ACT.Ln).then_inc(s_dtA, 1)
                    maybe(probs, u + 2)
                if n - 1 in SILU:
                    tanh(n - 1)
            evacuate(U_OUT - 1)
            tanh(U_OUT - 1)

            def w_out_hi(k):
                u = U_OUT + k
                act.wait_ge(s_w[u % 2], loaded(u))
                if k == 0:
                    act.wait_ge(s_wu, U_OUT)
                act.activation(a_hi[:, k, :], ring(raw, u), ACT.Copy).then_inc(s_whi, 1)

            def mixed_squares(b):
                act.wait_ge(s_wu, U_OUT + b + 1)
                if b >= 1:
                    act.wait_ge(s_mq, b)
                act.activation(junk[0], bank(out_bank(b), 2), ACT.Square, accum_out=st[:, 16 + b:17 + b])\
                    .then_inc(s_mq, 1)

            def x1_squares(b):
                act.wait_ge(s_mx, b + 1)
                if b >= 1:
                    act.wait_ge(s_q2, b)
                act.activation(junk[1], xr[:, b % 2, :], ACT.Square, accum_out=st[:, 32 + b:33 + b]).then_inc(s_q2, 1)

            def x1_evacuate(b):
                act.wait_ge(s_T2, b + 1)
                act.activation(x1nT[:, :, b * P:(b + 1) * P],
                               bank(4 if b == NB - 1 else 2, 2).rearrange("p (k t) -> p k t", k=KT), ACT.Copy)\
                    .then_inc(s_e2, 1)

            def by_tile(ap):
                return ap.rearrange("p (k t) -> p k t", k=KT)

            def decay_exp(i, g):
                act.wait_ge(s_D, 2 * i + g + 1)
                act.activation(decay[:, g, :], bank(5 + 2 * g), ACT.Exp).then_inc(s_E, 1)

            for k in range(4):
                w_out_hi(k)
            for i in range(NB + 1):
                if i >= 2:
                    mixed_squares(i - 2)
                if i < NB:
                    act.wait_ge(s_t1, i + 1)
                    if i >= 1:
                        act.wait_ge(s_sn, i)
                    act.activation(bn, bank(4)[:, 0:2 * P].rearrange("p (g n) -> p g n", g=2), ACT.Copy)\
                        .then_inc(s_bn, 1)
                    decay_exp(i, 0)
                if i >= 2:
                    x1_squares(i - 2)
                if i < NB:
                    decay_exp(i, 1)
                if i == 0:
                    for k in range(4, KT):
                        w_out_hi(k)
                if i >= 1:
                    act.wait_ge(s_mT, i)
                    act.activation(by_tile(ring(w_hi, U_OUT + i - 1)), by_tile(bank(2, 2)), ACT.Copy).then_inc(s_mh, 1)
                if i < NB:
                    act.wait_ge(s_g, i + 1)
                    for g in range(GROUPS):
                        ins = act.activation(four(Z, i)[:, 2 * g:2 * g + 2, :],
                                             yy[:, g * 256:(g + 1) * 256].rearrange("p (a b) -> p a b", a=2),
                                             ACT.Square, accum_out=st[:, 56 + g:57 + g])
                    ins.then_inc(s_gq, 1)
                if i >= 2:
                    x1_evacuate(i - 2)

            def h2_hi(hf, k):
                if hf == 0 and k == 0:
                    act.wait_ge(s_wu, U_UP)
                act.wait_ge(s_h2, KT * hf + k + 1)
                act.activation(a_hi[:, k, hf * 512:(hf + 1) * 512], x1nT[:, k, hf * 512:(hf + 1) * 512],
                               ACT.Copy).then_inc(s_h2h, 1)

            split_hi(U_UP)
            mixed_squares(NB - 1)
            for k in range(4):
                h2_hi(0, k)
            x1_squares(NB - 1)
            for k in range(4, KT):
                h2_hi(0, k)
            split_hi(U_UP + 1)
            x1_evacuate(NB - 1)
            for k in range(KT):
                h2_hi(1, k)

            def column(base, i, t):
                return cols[:, bass.ds(i * 2 + (base + t // 2 + FT * (t % 2)), 1)]

            def f_tile(k):
                return flat(big[:, bass.ds(k, 1), :])

            def up_first_tap(i, t, first):
                act.wait_ge(s_wu, i * 4 + (U_UP + t + 1))
                if t % 2:
                    dst = f_tile(i * 2 + t // 2)
                else:
                    dst = gate_t[:, t // 2, :]
                    if not first:
                        act.wait_ge(s_f, i * 2 + (t // 2 - 1))
                act.activation(dst, bank(2 * t, 2), ACT.Identity, scale=column(C_FFN + 88, i, t),
                               bias=column(C_FFN + 132, i, t)).then_inc(s_u0, 1)

            def up_gelu(i, pr):
                act.wait_ge(s_u1, i * 4 + (2 * pr + 1))
                act.activation(gate_t[:, pr, :], gate_t[:, pr, :], ACT.Gelu_apprx_tanh).then_inc(s_ge, 1)

            def f_split_hi(half, kk, e):
                if isinstance(kk, int) and half == 0 and kk == 0:
                    act.wait_ge(s_ah, e + 1)
                elif e == 0:
                    act.wait_ge(s_fu, kk + DOWN_UNITS * half)
                else:
                    act.wait_ge(s_wu, kk + (U_DOWN + DOWN_UNITS * half))
                act.activation(a_hi[:, e, :], f_tile(kk * 2 + e), ACT.Copy).then_inc(s_fh, 1)

            def up_body(i, first=False, last=False):
                for t in range(4):
                    if not (first and t == 0):
                        split_hi(U_UP + t + 1, i * 4)
                    if last and t == 3:
                        for e in range(2):
                            f_split_hi(0, 0, e)
                    up_first_tap(i, t, first)
                    if t % 2:
                        up_gelu(i, t // 2)

            up_body(0, first=True)
            with act.Fori(1, FT // 2 - 1) as i:
                up_body(i)
            up_body(FT // 2 - 1, last=True)

            def down_unit(half, kk0, dk, split_next=True):
                for e in range(2):
                    f_split_hi(half, dk + kk0, e)
                if split_next:
                    split_hi(U_DOWN + DOWN_UNITS * half + kk0 + 1, dk)

            for half in range(2):
                split_hi(U_DOWN + DOWN_UNITS * half + 1)
                with act.Fori(0, 4) as i:
                    down_unit(half, 1, i * 2)
                    down_unit(half, 2, i * 2)
                if half == 1:
                    for b in range(NB):
                        act.wait_ge(s_d0, b + 1)
                        link(act.activation(junk_r, half0[:, b, :], ACT.Square, accum_out=st[:, 88 + b:89 + b]))
                down_unit(half, 9, 0)
                down_unit(half, 10, 0, split_next=half == 0)
                if half == 0:
                    f_split_hi(1, 0, 0)
                    for b in range(NB):
                        bank_done(act, s_dn, 0, b, U_DOWN + DOWN_UNITS - 1)
                        act.activation(half0[:, b, :], bank(b), ACT.Copy).then_inc(s_d0, 1)
                    f_split_hi(1, 0, 1)
            for b in range(NB):
                bank_done(act, s_dn, 1, b, U_END - 1)
                if b >= 1:
                    act.wait_ge(s_dq, b)
                act.activation(junk_r, bank(b), ACT.Square, accum_out=st[:, 96 + b:97 + b]).then_inc(s_dq, 1)

        @block.vector
        def _(dve):
            chain = [0]

            def link(ins):
                chain[0] += 1
                ins.then_inc(s_dv, 1)
                dve.wait_ge(s_dv, chain[0])

            def normalise(b):
                dve.wait_ge(s_rs, b + 1)
                dve.tensor_scalar(ring(raw, b), ring(raw, b), st[:, 8 + b:9 + b], None, ALU.mult).then_inc(s_xn, 1)

            def sum_chunk(n):
                if n == 0:
                    dve.wait_ge(s_cs, 1)
                dve.wait_ge(s_ada[n % 2], 16 * (n // 2 + 1))
                part = acc[:, n * 512:(n + 1) * 512]
                link(dve.tensor_scalar(part, chunk[n % 2][:, 0, :], ca[:, 1, 0:1], None, ALU.mult))
                for j in range(1, KT):
                    ins = dve.scalar_tensor_tensor(out=part, in0=chunk[n % 2][:, j, :], scalar=ca[:, 1, j:j + 1],
                                                   in1=part, op0=ALU.mult, op1=ALU.add)
                    if j < KT - 1:
                        link(ins)
                ins.then_inc(s_acc, 1)

            for b in range(NB):
                normalise(b)
                if b % 2:
                    sum_chunk(b // 2)

            dve.wait_ge(s_rT, 1)
            link(dve.tensor_copy(cols[:, :], bank(7)[:, 0:280]))
            conv_cols = cols[:, C_CONV:C_CONV + N_CONV_ROWS]
            dve.tensor_scalar(conv_cols, conv_cols, 0.5, None, ALU.mult).then_inc(s_cols, 1)
            dve.wait_ge(s_ext, 1)
            dve.tensor_copy(ext_sb, bank(6)[0:H, 0:EXT]).then_inc(s_exs, 1)
            dve.wait_ge(s_cols, 1)

            def take_columns(n):
                link(dve.tensor_tensor(modc[:, 16 * n:16 * n + 16], bank(6)[:, EXT + 16 * n:EXT + 16 * n + 16],
                                       cols[:, 24 * n:24 * n + 16], ALU.add))
                dve.scalar_tensor_tensor(out=modc[:, 16 * n + 8:16 * n + 16], in0=modc[:, 16 * n + 8:16 * n + 16],
                                         scalar=1.0, in1=cols[:, 48 + 8 * n:56 + 8 * n],
                                         op0=ALU.add, op1=ALU.mult).then_inc(s_mod, 1)

            def take_gate(n, half):
                part = gate_rows[:, n, half * 512:(half + 1) * 512]
                link(dve.tensor_tensor(part, bank(GATE_BANKS[2 * n + half]), part, ALU.add))
                dve.tensor_tensor(part, part, post_bc[:, n, half * 512:(half + 1) * 512], ALU.mult).then_inc(s_mod, 1)

            dve.wait_ge(s_mp, 1)
            take_columns(0)
            dve.wait_ge(s_mod, 1)
            dve.wait_ge(s_xe, NB)

            def modulate(tiles, k, n, c0, w, done):
                part = tiles[:, k, c0:c0 + w]
                dve.tensor_scalar(part, part, modc[:, 16 * n + 8 + k:16 * n + 9 + k],
                                  modc[:, 16 * n + k:16 * n + k + 1], ALU.mult, ALU.add).then_inc(done, 1)

            def h_lo(tiles, k, c0, w, done):
                dve.tensor_tensor(a_lo[:, k, c0:c0 + w], tiles[:, k, c0:c0 + w],
                                  a_hi[:, k, c0:c0 + w].bitcast(f32), ALU.subtract).then_inc(done, 1)

            def split_lo(u, du=0):
                dve.wait_ge(s_whi, du + (u + 1))
                dve.tensor_tensor(ring(w_lo, u), ring(raw, u), ring(w_hi, u).bitcast(f32), ALU.subtract)\
                    .then_inc(s_wlo, 1)

            modulate(xnT, 0, 0, 0, T, s_h)
            split_lo(0)
            for k in range(KT):
                if k + 1 < KT:
                    modulate(xnT, k + 1, 0, 0, T, s_h)
                dve.wait_ge(s_hhi, k + 1)
                h_lo(xnT, k, 0, T, s_hlo)

            def conv_tap(n, d):
                m = CONV.index(n)
                if d == 1:
                    dve.wait_ge(s_c0, CONV_BY_TIME.index(n) + 1)
                tap = C_CONV + 8 * (3 - d) + m
                ins = dve.scalar_tensor_tensor(out=proj(n)[:, d:], in0=bank(2 * (n % 2), 2)[:, 0:T - d],
                                               scalar=cols[:, tap:tap + 1], in1=proj(n)[:, d:],
                                               op0=ALU.mult, op1=ALU.add)
                if d < 3:
                    link(ins)
                else:
                    ins.then_inc(s_evD, 1)

            def silu_multiply(n):
                m = SILU.index(n)
                dve.wait_ge(s_th, m + 1)
                dve.scalar_tensor_tensor(out=proj(n), in0=tanh_t[:, m % 2, :], scalar=1.0, in1=proj(n),
                                         op0=ALU.add, op1=ALU.mult).then_inc(s_si, 1)

            def scores(u):
                i, j = u // NPAIR, u % NPAIR
                k0 = P if i == 0 else 0
                s2 = bank(4, 2).rearrange("p (e k) -> p e k", e=2)
                dst = prob[:, u % 2, :, k0:]
                dve.wait_ge(s_S, u + 1)
                if u >= 2:
                    dve.wait_ge(s_pT, u - 1)
                if j == 0 and i >= 1:
                    dve.wait_ge(s_nms, i)
                dve.scalar_tensor_tensor(out=dst, in0=s2[:, :, k0:2 * P], scalar=HD ** -0.5, in1=bias[:, j, :, k0:],
                                         op0=ALU.mult, op1=ALU.add).then_inc(s_sb, 1)
                dve.wait_ge(s_sb, u + 1)
                link(dve.tensor_reduce(mx, dst, AX.X, ALU.max))
                dve.scalar_tensor_tensor(out=hv[:, NM, j::NPAIR], in0=mx, scalar=-1.0, in1=nsink[:, j::NPAIR],
                                         op0=ALU.mult, op1=ALU.min).then_inc(s_nm, 1)

            def attention_step(u):
                if u < N_PAIRS:
                    scores(u)
                if u < N_PAIRS and u % NPAIR == NPAIR - 1:
                    dve.wait_ge(s_nm, u + 1)
                    dve.tensor_tensor(esk[(u // NPAIR) % 2], hv[:, NM, :], hv[:, SINK, :], ALU.add).then_inc(s_nms, 1)
                if u >= NPAIR + 1 and u % NPAIR == 1:
                    i = u // NPAIR - 1
                    dve.wait_ge(s_es, i + 1)
                    link(dve.tensor_tensor(den(i), den(i), esk[i % 2], ALU.add))
                    link(dve.reciprocal(hv[:, REC, :], den(i)))
                    dve.wait_ge(s_pv, NPAIR * (i + 1))
                    dve.tensor_tensor(four(Q, i).rearrange("p t (e d) -> p t e d", e=2),
                                      bank(7).rearrange("p (t e d) -> p t e d", t=4, e=2),
                                      hv[:, REC, :].rearrange("p (t e) -> p t e", e=2).unsqueeze(3)
                                      .to_broadcast([P, 4, 2, HD]), ALU.mult).then_inc(s_o, 1)

            def slot(v):
                return dt_slot(v)

            def by_head(v):
                return dt_slot(v).rearrange("p (b h) -> p b h", h=H)

            def head_row(r):
                return hv[:, r, :].unsqueeze(1).to_broadcast([P, NB, H])

            def dt_natural():
                dve.wait_ge(s_dtn, 1)
                dve.wait_ge(s_S, 3 * (U_DT + 1 - A0) + 2)
                link(dve.tensor_copy(dt_nat, bank(5)[:, 256:256 + P].rearrange("p (b n) -> p b n", b=NB)))
                link(dve.tensor_tensor(by_head(T3), dt_nat[:, :, 0:H], dt_nat[:, :, H:2 * H], ALU.add))
                link(dve.tensor_tensor(by_head(T3), by_head(T3), head_row(DTB), ALU.add))
                dve.scalar_tensor_tensor(out=slot(T4), in0=slot(T3), scalar=-1.0, in1=slot(T3),
                                         op0=ALU.mult, op1=ALU.max).then_inc(s_dt1, 1)

            def dt_one_plus():
                dve.wait_ge(s_dtA, 2)
                dve.tensor_scalar(slot(T4), slot(T2), 1.0, None, ALU.add).then_inc(s_dt1, 1)
                dve.wait_ge(s_dt1, 2)
                link(dve.tensor_scalar(slot(TE), slot(T4), -1.0, None, ALU.add))
                link(dve.tensor_scalar(slot(CD), slot(TE), 0.0, None, ALU.is_equal))
                link(dve.tensor_tensor(slot(TE), slot(TE), slot(CD), ALU.add))
                link(dve.reciprocal(slot(TE), slot(TE)))
                link(dve.tensor_tensor(slot(TE), slot(TE), slot(T2), ALU.mult))

            def dt_finish():
                dve.wait_ge(s_dtA, 3)
                link(dve.tensor_tensor(slot(FS), slot(FS), slot(CD), ALU.add))
                link(dve.tensor_tensor(slot(FS), slot(FS), slot(TE), ALU.mult))
                dve.scalar_tensor_tensor(out=slot(DT), in0=slot(T3), scalar=0.0, in1=slot(FS),
                                         op0=ALU.max, op1=ALU.add).then_inc(s_dt1, 1)
                dve.wait_ge(s_dt1, 3)
                link(dve.tensor_tensor(by_head(ADT), by_head(DT), head_row(EA), ALU.mult))
                dve.tensor_scalar(slot(ADT), slot(ADT), -1.0, None, ALU.mult).then_inc(s_dte, 1)

            def dt_sums():
                dve.wait_ge(s_dtc, 1)
                dve.wait_ge(s_S, 3 * (U_DT + 2 - A0) + 2)
                dve.tensor_copy(dtv[:, FS:CD + 1, :], bank(5)[:, 256:448].rearrange("p (v n) -> p v n", v=3))\
                    .then_inc(s_dt2, 1)

            split_lo(1)
            for n in range(U_OUT + 2):
                if n - 2 in SILU:
                    silu_multiply(n - 2)
                if n + 1 == U_DT:
                    dve.wait_ge(s_whi, U_DT + 1)
                    wdt = ring(w_hi, U_DT).rearrange("p (k n) -> p k n", k=KT)
                    dve.tensor_tensor(wdt[:, :, H:2 * H], raw_dt[:, :, :], wdt[:, :, 0:H].bitcast(f32),
                                      ALU.subtract).then_inc(s_wlo, 1)
                elif 2 <= n + 1 < U_OUT:
                    split_lo(n + 1)
                if n < 4:
                    sum_chunk(4 + 2 * n)
                    sum_chunk(5 + 2 * n)
                if n == 3:
                    dve.wait_ge(s_late, 16 * N_LATE)
                    dve.tensor_scalar(nsink, hv[:, SINK, :], -1.0, None, ALU.mult)
                    for half in range(2):
                        dve.wait_ge(s_mp, 2 + half)
                        take_gate(0, half)
                if n == 5:
                    dve.wait_ge(s_mp, 4)
                    take_columns(1)
                    for half in range(2):
                        dve.wait_ge(s_mp, 5 + half)
                        take_gate(1, half)
                if n == U_DT + 3:
                    dve.wait_ge(s_dtA, 4)
                    dve.tensor_tensor(slot(TE), slot(TE), slot(DT), ALU.mult)
                for r in range(3):
                    u = 3 * (n - A0) + r
                    if n - 1 in CONV:
                        conv_tap(n - 1, r + 1)
                    if n == U_DT + 1 and r == 1:
                        dt_natural()
                    if n == U_DT + 1 and r == 2:
                        dt_one_plus()
                    if n == U_DT + 2 and r == 1:
                        dt_sums()
                    if u >= 0 and n < U_OUT:
                        attention_step(u)
                if n == U_DT + 1:
                    dt_finish()

            def at(v, i):
                return per_head(dtv[:, v, i * H:(i + 1) * H])

            def by_tile(ap):
                return ap.rearrange("p (k t) -> p k t", k=KT)

            def w_out_lo(k):
                u = U_OUT + k
                dve.wait_ge(s_whi, u + 1)
                dve.tensor_tensor(a_lo[:, k, :], ring(raw, u), a_hi[:, k, :].bitcast(f32), ALU.subtract)\
                    .then_inc(s_wlo, 1)

            def residual(b):
                dve.wait_ge(s_mr, b + 1)
                if b >= 2:
                    dve.wait_ge(s_T2, b - 1)
                link(dve.scalar_tensor_tensor(out=xn2[:, b % 2, :], in0=bank(out_bank(b), 2),
                                              scalar=st[:, 80 + b:81 + b], in1=gate_rows[:, 0, :],
                                              op0=ALU.mult, op1=ALU.mult))
                dve.wait_ge(s_xr[b % 2], 16 * (b // 2 + 1))
                dve.tensor_tensor(xr[:, b % 2, :], xr[:, b % 2, :], xn2[:, b % 2, :], ALU.add).then_inc(s_mx, 1)

            def normalise_x1(b):
                dve.wait_ge(s_r2, b + 1)
                dve.tensor_scalar(xn2[:, b % 2, :], xr[:, b % 2, :], st[:, 40 + b:41 + b], None,
                                  ALU.mult).then_inc(s_n2, 1)

            for k in range(4):
                w_out_lo(k)
            y4 = yy.rearrange("p (t n) -> p t n", t=4)
            for i in range(NB + 1):
                if i < NB:
                    dve.wait_ge(s_xsT, i + 1)
                    dve.tensor_tensor(heads(xc), heads(bank(6)), at(DT, i), ALU.mult)
                    dve.tensor_tensor(heads(xc_end), heads(bank(6)), at(TE, i), ALU.mult)
                    xd = four(XS, i).rearrange("p t (e d) -> p t e d", e=2)
                    dve.tensor_tensor(xd, bank(6).rearrange("p (t e d) -> p t e d", t=4, e=2),
                                      hv[:, DD, :].rearrange("p (t e) -> p t e", e=2).unsqueeze(3)
                                      .to_broadcast([P, 4, 2, HD]), ALU.mult).then_inc(s_xc, 1)
                    dve.wait_ge(s_cb, i + 1)
                    dve.tensor_tensor(cbm, bank(7)[:, 0:256].rearrange("p (g l) -> p g l", g=2),
                                      upper.unsqueeze(1).to_broadcast([P, 2, P]), ALU.mult).then_inc(s_cbm, 1)
                if i >= 2:
                    residual(i - 2)
                if i < NB:
                    dve.wait_ge(s_cbm, i + 1)
                    for g in range(GROUPS):
                        dve.wait_ge(s_E, 2 * i + g + 1)
                        dg = decay[:, g, :].rearrange("p (h l) -> p h l", h=4)
                        dve.tensor_tensor(dg, dg, cbm[:, g, :].unsqueeze(1).to_broadcast([P, 4, P]),
                                          ALU.mult).then_inc(s_W, 1)
                if i == 0:
                    for k in range(4, KT):
                        w_out_lo(k)
                if i >= 1:
                    dve.wait_ge(s_mh, i)
                    u = U_OUT + i - 1
                    dve.tensor_tensor(by_tile(ring(w_lo, u)), by_tile(bank(2, 2)), by_tile(ring(w_hi, u).bitcast(f32)),
                                      ALU.subtract).then_inc(s_ml, 1)
                if i < NB:
                    dve.wait_ge(s_yo, i + 1)
                    dve.tensor_tensor(heads(yy), heads(bank(5)), at(FS, i), ALU.mult).then_inc(s_ya, 1)
                    dve.wait_ge(s_ya, i + 1)
                    dve.wait_ge(s_yd, i + 1)
                    dve.tensor_tensor(yy, yy, bank(6), ALU.add).then_inc(s_yb, 1)
                    link(dve.tensor_tensor(heads(state), heads(state), at(CD, i), ALU.mult))
                    dve.wait_ge(s_sn, i + 1)
                    dve.tensor_tensor(state, state, bank(7), ALU.add).then_inc(s_su, 1)
                    dve.wait_ge(s_yb, i + 1)
                    link(dve.tensor_tensor(y4, y4, four(XS, i), ALU.add))
                    dve.wait_ge(s_zT, i + 1)
                    dve.tensor_tensor(yy, yy, bank(5), ALU.mult).then_inc(s_g, 1)
                if i >= 2:
                    normalise_x1(i - 2)
                if i < NB:
                    dve.wait_ge(s_gr, i + 1)
                    for g in range(GROUPS):
                        ins = dve.scalar_tensor_tensor(
                            out=four(Z, i)[:, 2 * g:2 * g + 2, :], in0=y4[:, 2 * g:2 * g + 2, :],
                            scalar=st[:, 58 + g:59 + g],
                            in1=normw[:, g * 256:(g + 1) * 256].rearrange("p (a b) -> p a b", a=2),
                            op0=ALU.mult, op1=ALU.mult)
                    ins.then_inc(s_my, 1)

            def h2_modulate(hf):
                dve.wait_ge(s_e2, 4 * (hf + 1))
                for k in range(KT):
                    modulate(x1nT, k, 1, hf * 512, 512, s_h2)

            def h2_lo(hf, ks):
                for k in ks:
                    dve.wait_ge(s_h2h, KT * hf + k + 1)
                    h_lo(x1nT, k, hf * 512, 512, s_h2l)

            h2_modulate(0)
            split_lo(U_UP)
            h2_lo(0, range(4))
            residual(NB - 1)
            h2_lo(0, range(4, KT))
            normalise_x1(NB - 1)
            split_lo(U_UP + 1)
            h2_modulate(1)
            h2_lo(1, range(KT))

            def column(base, i, t):
                return cols[:, bass.ds(i * 2 + (base + t // 2 + FT * (t % 2)), 1)]

            def f_tile(k):
                return flat(big[:, bass.ds(k, 1), :])

            def up_taps(i, t):
                dst = f_tile(i * 2 + t // 2) if t % 2 else gate_t[:, t // 2, :]
                src = bank(2 * t, 2)
                dve.wait_ge(s_u0, i * 4 + (t + 1))
                dve.scalar_tensor_tensor(out=dst[:, 1:], in0=src[:, 0:T - 1], scalar=column(C_FFN + 44, i, t),
                                         in1=dst[:, 1:], op0=ALU.mult, op1=ALU.add).then_inc(s_uc, 1)
                dve.wait_ge(s_uc, i * 4 + (t + 1))
                dve.scalar_tensor_tensor(out=dst[:, 2:], in0=src[:, 0:T - 2], scalar=column(C_FFN, i, t),
                                         in1=dst[:, 2:], op0=ALU.mult, op1=ALU.add).then_inc(s_u1, 1)

            def up_gate(i, pr):
                dst = f_tile(i * 2 + pr)
                dve.wait_ge(s_ge, i * 2 + (pr + 1))
                dve.wait_ge(s_u1, i * 4 + (2 * pr + 2))
                dve.tensor_tensor(dst, dst, gate_t[:, pr, :], ALU.mult).then_inc(s_f, 1)

            def f_split_lo(half, kk, e):
                dve.wait_ge(s_fh, kk * 2 + (FT * half + e + 1))
                dve.tensor_tensor(a_lo[:, e, :], f_tile(kk * 2 + e), a_hi[:, e, :].bitcast(f32),
                                  ALU.subtract).then_inc(s_fl, 1)

            def up_body(i, first=False, last=False):
                for t in range(4):
                    if not (first and t == 0):
                        split_lo(U_UP + t + 1, i * 4)
                    if last and t == 3:
                        for e in range(2):
                            f_split_lo(0, 0, e)
                    up_taps(i, t)
                    if t % 2:
                        up_gate(i, t // 2)

            up_body(0, first=True)
            with dve.Fori(1, FT // 2 - 1) as i:
                up_body(i)
            up_body(FT // 2 - 1, last=True)

            def down_unit(half, kk0, dk, split_next=True):
                for e in range(2):
                    f_split_lo(half, dk + kk0, e)
                if split_next:
                    split_lo(U_DOWN + DOWN_UNITS * half + kk0 + 1, dk)

            for half in range(2):
                split_lo(U_DOWN + DOWN_UNITS * half + 1)
                with dve.Fori(0, 4) as i:
                    down_unit(half, 1, i * 2)
                    down_unit(half, 2, i * 2)
                down_unit(half, 9, 0)
                down_unit(half, 10, 0, split_next=half == 0)
                if half == 0:
                    for e in range(2):
                        f_split_lo(1, 0, e)

            dve.wait_ge(s_x1l, 16 * NB)
            for b in range(NB):
                row = ring(raw, b)
                dve.wait_ge(s_dr, b + 1)
                if b >= 2:
                    dve.wait_ge(s_out[b % 2], 16 * (b // 2))
                for half in range(2):
                    ins = dve.scalar_tensor_tensor(
                        out=row[:, half * 512:(half + 1) * 512], in0=bank(b) if half else half0[:, b, :],
                        scalar=st[:, 104 + b:105 + b], in1=gate_rows[:, 1, half * 512:(half + 1) * 512],
                        op0=ALU.mult, op1=ALU.mult)
                link(ins)
                x1 = (a_hi if b < 4 else a_lo)[:, 4 + b % 4, :].bitcast(f32)
                dve.tensor_tensor(row, row, x1, ALU.add).then_inc(s_do, 1)

        @block.tensor
        def _(pe):
            pe.wait_ge(s_const, 48)
            pe.wait_ge(s_small, 16 * N_SMALL)
            for b in range(NB):
                pe.wait_ge(s_xn, b + 1)
                if b >= 3:
                    pe.wait_ge(s_xe, b - 2)
                for k in range(KT):
                    mm = pe.transpose(bank(2 * (b % 3), 2)[:, k * P:(k + 1) * P],
                                      ring(raw, b)[:, k * P:(k + 1) * P], ident)
                mm.then_inc(s_xT, 1)

            pe.wait_ge(s_sq, NB)
            c0 = 0
            for m, n in enumerate([N_MOD_ROWS, N_CONV_ROWS, N_FFN_ROWS, N_FFN_ROWS]):
                mm = pe.transpose(bank(7)[:, c0:c0 + n], rows[0:n, m, :], ident[0:n, 0:n])
                c0 += n
            mm.then_inc(s_rT, 1)
            pe.matmul(bank(6)[0:H, 0:EXT], rb_sb, hot_sb, start=True, stop=True).then_inc(s_ext, 1)

            def sum_columns(first, col):
                for f in range(16):
                    src = first * 512 + f * P
                    mm = pe.matmul(bank(6)[:, col + f:col + f + 1], acc[:, src:src + P], ones[:, 0:1],
                                   start=True, stop=True)
                mm.then_inc(s_mp, 1)

            def sum_gate(n, b):
                pe.matmul(bank(b), ones[:, :], acc[:, n * 512:(n + 1) * 512], start=True, stop=True)\
                    .then_inc(s_mp, 1)

            pe.wait_ge(s_pool, 2)
            pe.wait_ge(s_acc, 4)
            pe.wait_ge(s_exs, 1)
            sum_columns(0, EXT)

            def split_products(outs, lhs_of, rhs_of, first, last):
                for p, (a, b) in enumerate(((0, 0), (0, 1), (1, 0))):
                    for j, out in enumerate(outs):
                        mm = pe.matmul(out, lhs_of[a], rhs_of(b, j), start=first and p == 0, stop=last and p == 2)
                return mm

            def features(banks, u, halves=(0, 1), before=None, after=None):
                for k in range(KT):
                    if before:
                        before(k)
                    cs = slice(k * P, (k + 1) * P)
                    mm = split_products(
                        [bank(banks + hf) for hf in halves], (ring(w_hi, u)[:, cs], ring(w_lo, u)[:, cs]),
                        lambda b, j: (a_hi, a_lo)[b][:, k, halves[j] * 512:(halves[j] + 1) * 512],
                        k == 0, k == KT - 1)
                    if after:
                        after(k, mm)
                return mm

            def bank_free(n):
                m = n - 2
                if m in CONV:
                    pe.wait_ge(s_evD, CONV_BY_TIME.index(m) + 1)
                elif m == U_DT:
                    pe.wait_ge(s_dtT, 1)
                elif m >= Z:
                    pe.wait_ge(s_z0, m - Z + 1)
                elif m >= 0:
                    pe.wait_ge(s_evA, m + 1)

            def score(u):
                i, j = u // NPAIR, u % NPAIR
                if u >= 1:
                    pe.wait_ge(s_sb, u)
                else:
                    pe.wait_ge(s_bias, NPAIR)
                k0, w = (P, 1) if i == 0 else (0, 2)
                for e in range(2):
                    rs = slice(e * HD, (e + 1) * HD)
                    mm = pe.matmul(bank(4 + e)[:, k0:2 * P], blk(Q + j, i)[rs],
                                   blk(K, i + 1 - w, w)[rs], start=True, stop=True)
                mm.then_inc(s_S, 1)

            def probs_transpose(u):
                i = u // NPAIR
                pe.wait_ge(s_p, u + 1)
                if u >= 1:
                    pe.wait_ge(s_pe, u)
                else:
                    pe.wait_ge(s_v, 1)
                for e in range(2):
                    for kb in range(1 if i == 0 else 0, 2):
                        at = (2 * e + kb) * P
                        mm = pe.transpose(bank(6)[:, at:at + P], prob[:, u % 2, e, kb * P:(kb + 1) * P], ident)
                mm.then_inc(s_pT, 1)

            def values(u):
                i, j = u // NPAIR, u % NPAIR
                pe.wait_ge(s_pe, u + 1)
                if j == 0 and i >= 1:
                    pe.wait_ge(s_o, i)
                for e in range(2):
                    h = j + 4 * e
                    k0 = 1 if i == 0 else 0
                    for kb in range(k0, 2):
                        at = (u % 2) * 512 + (2 * e + kb) * P
                        mm = pe.matmul(bank(7)[:, h * HD:(h + 1) * HD], probT[:, at:at + P],
                                       blk(V, i - 1 + kb)[:, e * HD:(e + 1) * HD],
                                       start=(kb == k0), stop=(kb == 1))
                mm.then_inc(s_pv, 1)

            def bias_flip():
                pe.wait_ge(s_bl, 32)
                for j in range(NPAIR):
                    if j < 2:
                        pe.wait_ge(s_mod, 6)
                    else:
                        pe.wait_ge(s_bias, j - 1)
                    pe.matmul(bank(4 + j % 2), flip, bias[:, j], start=True, stop=True).then_inc(s_flp, 1)

            def v_transpose():
                pe.wait_ge(s_evA, V + 1)
                for i in range(NB):
                    mm = pe.transpose(bank(6, 2)[:, i * P:(i + 1) * P], blk(V, i), ident)
                mm.then_inc(s_vT, 1)

            def dt_transpose():
                pe.wait_ge(s_dtT, 1)
                pe.wait_ge(s_sb, 3 * (U_DT + 1 - A0) + 1)
                for b in range(NB):
                    mm = pe.transpose(bank(5)[:, 256 + 16 * b:272 + 16 * b], dt_rows[:, b * P:(b + 1) * P],
                                      ident[0:16, 0:16])
                mm.then_inc(s_dtn, 1)

            def dt_sum():
                pe.wait_ge(s_dte, 1)
                pe.wait_ge(s_sb, 3 * (U_DT + 2 - A0) + 1)
                for v, m in enumerate((upper, strict, ones[:, :])):
                    mm = pe.matmul(bank(5)[:, 256 + 64 * v:320 + 64 * v], m, dtv[:, ADT, :], start=True, stop=True)
                mm.then_inc(s_dtc, 1)

            def beside(n):
                u = 3 * (n - A0)
                steps = {0: [(score, u), (probs_transpose, u - 2)],
                         2: [(values, u - 2)],
                         3: [(score, u + 1), (probs_transpose, u - 1)],
                         5: [(probs_transpose, u), (values, u - 1)],
                         6: [(score, u + 2)],
                         7: [(values, u)]}

                def before(k):
                    if n == 0:
                        pe.wait_ge(s_hlo, k + 1)
                    if n == V + 1 and k == 2:
                        bias_flip()
                    if n == V + 1 and k == 4:
                        v_transpose()
                    if n == U_DT + 1 and k == 3:
                        dt_transpose()
                    if n == U_DT + 2 and k == 3:
                        dt_sum()
                    if n >= A0:
                        for step, v in steps.get(k, []):
                            if 0 <= v < N_PAIRS:
                                step(v)
                return before

            for n in range(U_OUT):
                pe.wait_ge(s_wlo, n + 1)
                if n == 0:
                    pe.wait_ge(s_xe, NB)
                bank_free(n)
                if n == U_DT:
                    before = beside(n)
                    for k in range(KT):
                        before(k)
                        w = ring(w_hi, U_DT)[:, k * P:(k + 1) * P]
                        for m, moving in enumerate((a_hi, a_lo)):
                            for hf in range(2):
                                mm = pe.matmul(bank(hf), w, moving[:, k, hf * 512:(hf + 1) * 512],
                                               start=(k == 0 and m == 0), stop=(k == KT - 1 and m == 1))
                    mm.then_inc(s_wu, 1)
                else:
                    features(2 * (n % 2), n, before=beside(n)).then_inc(s_wu, 1)
                if n == 2:
                    pe.wait_ge(s_acc, 6)
                    for half in range(2):
                        sum_gate(4 + half, GATE_BANKS[half])
                if n == 4:
                    pe.wait_ge(s_acc, 12)
                    pe.wait_ge(s_mod, 1)
                    sum_columns(6, EXT + 16)
                    pe.wait_ge(s_cols, 1)
                    sum_gate(10, GATE_BANKS[2])
                    pe.wait_ge(s_mod, 2)
                    sum_gate(11, GATE_BANKS[3])

            def transpose_four(dst, src):
                for t in range(4):
                    mm = pe.transpose(bank(dst)[:, t * P:(t + 1) * P], src[:, t, :], ident)
                return mm

            def project_out(b, ks):
                u = U_OUT + b
                if ks[0] == 0:
                    pe.wait_ge(s_mh, b + 1)
                    pe.wait_ge(s_ml, b + 1)
                    if b >= 1:
                        pe.wait_ge(s_mx, b)
                for k in ks:
                    if b == 0:
                        pe.wait_ge(s_wlo, U_OUT + k + 1)
                    cs = slice(k * P, (k + 1) * P)
                    mm = split_products([bank(out_bank(b) + hf) for hf in range(2)],
                                        (ring(w_hi, u)[:, cs], ring(w_lo, u)[:, cs]),
                                        lambda s, j: (a_hi, a_lo)[s][:, k, j * 512:(j + 1) * 512],
                                        k == 0, k == KT - 1)
                if ks[-1] == KT - 1:
                    mm.then_inc(s_wu, 1)

            def x1_transpose(b):
                pe.wait_ge(s_n2, b + 1)
                for k in range(KT):
                    mm = pe.transpose(bank(4 if b == NB - 1 else 2, 2)[:, k * P:(k + 1) * P],
                                      xn2[:, b % 2, k * P:(k + 1) * P], ident)
                mm.then_inc(s_T2, 1)

            pe.wait_ge(s_z0, 4)
            for i in range(NB + 1):
                if i < NB:
                    if i == 0:
                        pe.wait_ge(s_si, len(CONV))
                        pe.wait_ge(s_sb, N_PAIRS)
                    else:
                        pe.wait_ge(s_bn, i)
                    for g in range(GROUPS):
                        mm = pe.transpose(bank(4)[:, g * P:(g + 1) * P], blk(BB + g, i), ident)
                    mm.then_inc(s_t1, 1)
                    if i == 0:
                        pe.wait_ge(s_pe, N_PAIRS)
                    else:
                        pe.wait_ge(s_yb, i)
                    transpose_four(6, four(XS, i)).then_inc(s_xsT, 1)
                    if i == 0:
                        pe.wait_ge(s_o, NB)
                    else:
                        pe.wait_ge(s_su, i)
                    for g in range(GROUPS):
                        mm = pe.matmul(bank(7)[:, g * P:(g + 1) * P], blk(BB + g, i), blk(CC + g, i),
                                       start=True, stop=True)
                    mm.then_inc(s_cb, 1)
                    if i >= 1:
                        pe.wait_ge(s_g, i)
                    pe.wait_ge(s_rd, 2 * i + 1)
                    pe.matmul(bank(5), strict, decay[:, 0, :], start=True, stop=True).then_inc(s_D, 1)
                    pe.wait_ge(s_cbm, i + 1)
                    pe.wait_ge(s_rd, 2 * i + 2)
                    pe.matmul(bank(7), strict, decay[:, 1, :], start=True, stop=True).then_inc(s_D, 1)
                if i >= 1:
                    pe.wait_ge(s_my, i)
                    if i >= 3:
                        pe.wait_ge(s_e2, i - 2)
                    transpose_four(2, four(Q, i - 1))
                    transpose_four(3, four(Z, i - 1)).then_inc(s_mT, 1)
                if i < NB:
                    pe.wait_ge(s_E, 2 * i + 1)
                    if i == 0:
                        pe.wait_ge(s_pc, NB + 1)
                    for g in range(GROUPS):
                        mm = pe.matmul(bank(5)[:, g * 256:(g + 1) * 256], blk(CC + g, i),
                                       state[:, g * 256:(g + 1) * 256], start=True, stop=True)
                    mm.then_inc(s_yo, 1)
                    pe.wait_ge(s_xc, i + 1)
                    pe.wait_ge(s_W, 2 * i + 2)
                    for h in range(H):
                        mm = pe.matmul(bank(6)[:, h * HD:(h + 1) * HD], decay[:, h // 4, (h % 4) * P:(h % 4 + 1) * P],
                                       xc[:, h * HD:(h + 1) * HD], start=True, stop=True)
                    mm.then_inc(s_yd, 1)
                if i >= 1:
                    project_out(i - 1, range(0, 2))
                if i < NB:
                    pe.wait_ge(s_bn, i + 1)
                    for g in range(GROUPS):
                        mm = pe.matmul(bank(7)[:, g * 256:(g + 1) * 256], bn[:, g, :],
                                       xc_end[:, g * 256:(g + 1) * 256], start=True, stop=True)
                    mm.then_inc(s_sn, 1)
                if i >= 1:
                    project_out(i - 1, range(2, 4))
                if i < NB:
                    if i == 0:
                        pe.wait_ge(s_si, len(SILU))
                    pe.wait_ge(s_ya, i + 1)
                    transpose_four(5, four(Z, i)).then_inc(s_zT, 1)
                if i >= 1:
                    project_out(i - 1, range(4, KT))
                if i >= 2:
                    x1_transpose(i - 2)

            def up_tile(i, t):
                pe.wait_ge(s_wlo, i * 4 + (U_UP + t + 1))
                pe.wait_ge(s_u1, i * 4 + (t - 3))
                features(2 * t, U_UP + t).then_inc(s_wu, 1)

            def h2_ready(hf):
                return lambda k: pe.wait_ge(s_h2l, KT * hf + k + 1)

            pe.wait_ge(s_mx, NB - 1)
            pe.wait_ge(s_wlo, U_UP + 1)
            features(0, U_UP, (0,), before=h2_ready(0))
            x1_transpose(NB - 1)
            pe.wait_ge(s_wlo, U_UP + 2)
            pe.wait_ge(s_e2, NB - 1)
            features(2, U_UP + 1, (0,))
            features(0, U_UP, (1,), before=h2_ready(1)).then_inc(s_wu, 1)
            features(2, U_UP + 1, (1,)).then_inc(s_wu, 1)
            for t in range(2, 4):
                pe.wait_ge(s_wlo, U_UP + t + 1)
                if t == 2:
                    pe.wait_ge(s_e2, NB)
                else:
                    pe.wait_ge(s_mx, NB)
                features(2 * t, U_UP + t).then_inc(s_wu, 1)
            with pe.Fori(1, FT // 2 - 1) as i:
                for t in range(4):
                    up_tile(i, t)
            for t in range(3):
                up_tile(FT // 2 - 1, t)
            pe.wait_ge(s_wlo, U_DOWN)
            pe.wait_ge(s_u1, 2 * FT - 4)
            features(6, U_DOWN - 1, after=lambda k, mm: mm.then_inc(s_ah, 1) if k < 2 else None).then_inc(s_wu, 1)

            def row_products(u, e, first, last, per_bank=None, done=None):
                ws = slice(e * 512, (e + 1) * 512)
                for b in range(NB):
                    if per_bank:
                        per_bank(b)
                    ts = slice(b * P, (b + 1) * P)
                    mm = split_products([bank(b)], (a_hi[:, e, ts], a_lo[:, e, ts]),
                                        lambda s, j: ring((w_hi, w_lo)[s], u)[:, ws], first, last)
                    if done is not None and b < NB - 1:
                        mm.then_inc(done, 1)
                return mm

            def down_unit(half, kk0, dk):
                u = U_DOWN + DOWN_UNITS * half + kk0
                pe.wait_ge(s_wlo, dk + (u + 1))
                for e in range(2):
                    q = FT * half + 2 * kk0 + e
                    pe.wait_ge(s_fl, dk * 2 + (q + 1))
                    first, last = kk0 == 0 and e == 0, kk0 == DOWN_UNITS - 1 and e == 1
                    bank_ready = None
                    if first and half == 0:
                        def bank_ready(b):
                            pe.wait_ge(s_u1, 2 * FT - 4 + b // 2 + 1)
                    if first and half == 1:
                        def bank_ready(b):
                            pe.wait_ge(s_d0, b + 1)
                    mm = row_products(u, e, first, last, bank_ready, s_dn if last else None)
                    if e == 0:
                        mm.then_inc(s_fu, 1)
                mm.then_inc(s_wu, 1)

            for half in range(2):
                down_unit(half, 0, 0)
                with pe.Fori(0, 4) as i:
                    down_unit(half, 1, i * 2)
                    down_unit(half, 2, i * 2)
                down_unit(half, 9, 0)
                down_unit(half, 10, 0)


_INS = ["x", "c", "rel_bias", "w_ada", "b_ada", "pre_mix_w", "w_in", "attn_sinks", "ssm_conv_w", "ssm_conv_b",
        "ssm_dt_bias", "ssm_a_log", "ssm_d", "ssm_norm_w", "w_out", "post_mix_w", "pre_ffn_w", "w_up",
        "ffn_conv_w", "ffn_conv_b", "w_down", "post_ffn_w"]


def kernel(**inputs):
    import concourse.bacc as _bacc
    from concourse.bass_utils import run_bass_kernel_spmd as _run

    nc = _bacc.Bacc("TRN2", target_bir_lowering=False, num_devices=1)
    arrays, args = {}, []
    named = [(name, np.ascontiguousarray(inputs[name])) for name in _INS]
    named += list(zip(("squares", "hot"), shape_constants()))
    for name, a in named:
        arrays[f"in_{name}_dram"] = a
        args.append(nc.dram_tensor(f"in_{name}_dram", a.shape, mybir.dt.from_np(a.dtype), kind="ExternalInput").ap())
    args.append(nc.dram_tensor("out_dram", (1, T, D), mybir.dt.float32, kind="ExternalOutput").ap())
    hybrid_layer_kernel(nc, *args)
    r = _run(nc, [arrays], core_ids=[0])
    return r.results[0]["out_dram"]
```

```python
import math
from contextlib import ExitStack

import numpy as np
import concourse.bass as bass
from concourse import mybir

D = 1024
T = 1024
P = 128
KT = D // P
NB = T // P
H = 8
HD = 64
NPAIR = H // 2
GROUPS = 2
FF = 2816
FT = FF // P
NBUCKET = 32
EXT = 3 * P
EPS = 1e-6
NEG = -1e30

U_IN, U_DT, U_OUT, U_UP, U_DOWN = 0, 14, 19, 27, 71
U_END = 93
DOWN_UNITS = FT // 2
SSM_W = H * HD
Q, K, V, CC, XS, BB, Z = 0, 4, 5, 6, 8, 12, 15
COLUMN = [0, 1, 2, 3, 4, 5, 16, 17, 6, 7, 8, 9, 14, 15, 18, 10, 11, 12, 13]
SLOT = [14, 15, 16, 17, 18, 19, 20, 21, 0, 1, 2, 3, 8, 9, None, 4, 5, 6, 7]
CONV = [8, 9, 10, 11, 12, 13, 6, 7]
CONV_BY_TIME = sorted(CONV)
SILU = CONV_BY_TIME + [15, 16, 17, 18]
A0 = 7
N_PAIRS = NB * NPAIR
GATE_BANKS = [4, 5, 4, 5]
N_SMALL, N_LATE = 10, 10
N_CONV_ROWS = 40
N_FFN_ROWS = 88
N_MOD_ROWS = 64
C_CONV, C_FFN = N_MOD_ROWS, N_MOD_ROWS + N_CONV_ROWS


def shape_constants():
    i = np.arange(P)
    squares = np.concatenate([
        np.eye(P), i[:, None] <= i[None, :], i[:, None] > i[None, :], np.eye(P)[::-1]], axis=1)
    hot = np.zeros((NBUCKET + 1, EXT))
    for u in range(EXT):
        dist = 2 * P - 1 - u
        if 0 <= dist < P:
            half = NBUCKET // 2
            b = dist if dist < half else min(NBUCKET - 1, half + int(
                math.log(dist / half) / math.log(P / half) * (NBUCKET - half)))
            hot[b, u] = 1.0
        else:
            hot[NBUCKET, u] = 1.0
    return squares.astype(np.float32), hot.astype(np.float32)


def hybrid_layer_kernel(nc, x, c, rel_bias, w_ada, b_ada, pre_mix_w, w_in, attn_sinks, ssm_conv_w,
                        ssm_conv_b, ssm_dt_bias, ssm_a_log, ssm_d, ssm_norm_w, w_out, post_mix_w,
                        pre_ffn_w, w_up, ffn_conv_w, ffn_conv_b, w_down, post_ffn_w,
                        squares, hot, out):
    f32 = mybir.dt.float32
    f32r = mybir.dt.float32r
    ALU = mybir.AluOpType
    ACT = mybir.ActivationFunctionType
    AX = mybir.AxisListType

    x2, out2 = x[0], out[0]
    w_in2, w_out2, w_up2, w_down2, w_ada2 = w_in[0], w_out[0], w_up[0], w_down[0], w_ada[0]
    bias_d = nc.dram_tensor("bias_by_distance", (H, EXT), f32).ap()
    x1_d = nc.dram_tensor("residual_after_mixer", (T, D), f32).ap()

    ctx = ExitStack()
    with ctx:
        def sb(name, shape, dt=f32):
            return ctx.enter_context(nc.sbuf_tensor(name, shape, dt))

        def sem(name):
            return ctx.enter_context(nc.semaphore(name))

        big = sb("big", [P, FT, T])
        a_hi = sb("a_hi", [P, KT, T], f32r)
        a_lo = sb("a_lo", [P, KT, T], f32r)
        raw = sb("raw", [P, 2, T])
        w_hi = sb("w_hi", [P, 2, T], f32r)
        w_lo = sb("w_lo", [P, 2, T], f32r)
        scratch = sb("scratch", [P, 4 * T])
        gate_rows = sb("gate_rows", [P, 2, D])
        sq = sb("sq", [P, 3 * P])
        ones = sb("ones", [P, P])
        cols = sb("cols", [P, 280])
        modc = sb("modc", [P, 32])
        ca = sb("ca", [P, 2, KT])
        hv = sb("hv", [P, 8, H])
        dtv = sb("dtv", [P, 5, NB * H])
        st = sb("st", [P, 128])
        normw = sb("normw", [P, SSM_W])
        ident, upper, strict = sq[:, 0:P], sq[:, P:2 * P], sq[:, 2 * P:3 * P]
        flip = scratch[:, 3840:3968]
        raw_dt = scratch[:, 3968:4032].rearrange("p (k h) -> p k h", k=KT)
        ps = ctx.enter_context(nc.psum_tensor("ps", [P, 8 * 512], f32))

        def bank(b, n=1):
            return ps[:, b * 512:(b + n) * 512]

        def ring(t, u):
            return t[:, u % 2, :]

        def flat(tiles):
            return tiles.rearrange("p a b -> p (a b)")

        xnT = big[:, 14:22, :]
        acc = flat(big[:, 8:14, :])
        chunk = [flat(big[:, 4 * s:4 * s + 4, :]).rearrange("p (j n) -> p j n", j=KT) for s in range(2)]

        x1nT = big[:, 0:8, :]

        def x_in(b):
            return (raw if b % 4 < 2 else gate_rows)[:, b % 2, :]

        def proj(n):
            return big[:, SLOT[n], :]

        def blk(n, i, w=1):
            return big[:, SLOT[n], i * P:(i + w) * P]

        def four(n, i):
            return big[:, SLOT[n]:SLOT[n] + 4, i * P:(i + 1) * P]

        def by_tile(ap):
            return ap.rearrange("p (k t) -> p k t", k=KT)

        def heads(ap):
            return ap.rearrange("p (h d) -> p h d", h=H)

        def per_head(ap):
            return ap.unsqueeze(2).to_broadcast([P, H, HD])

        work = flat(big[:, 10:14, :])
        prob = work[:, 0:1024].rearrange("p (s e k) -> p s e k", s=2, e=2)
        probT = work[:, 1024:2048]
        tanh_t = work[:, 2048:4096].rearrange("p (s n) -> p s n", s=2)
        tanh_late = scratch[:, 0:2048].rearrange("p (s n) -> p s n", s=2)
        dt_rows = big[0:16, SLOT[Z + 3], :]
        dt_nat = big[:, SLOT[Z + 2], 0:128].rearrange("p (b n) -> p b n", b=NB)
        dt_tmp = big[:, SLOT[Z + 2], 128:320].rearrange("p (v n) -> p v n", v=3)
        bias = scratch[:, 0:2048].rearrange("p (j e k) -> p j e k", j=NPAIR, e=2)
        xr = work[:, 0:2048].rearrange("p (s n) -> p s n", s=2)
        xc, xc_end = work[:, 2048:2560], work[:, 2560:3072]
        yy, state = work[:, 3072:3584], work[:, 3584:4096]
        xn2 = scratch[:, 0:2048].rearrange("p (s n) -> p s n", s=2)
        decay = scratch[:, 2048:3072].rearrange("p (g n) -> p g n", g=2)
        cbm = scratch[:, 3072:3328].rearrange("p (g l) -> p g l", g=2)
        bn = scratch[:, 3328:3584].rearrange("p (g n) -> p g n", g=2)
        junk = [big[:, SLOT[n], :] for n in (K, V)]
        rows = scratch[:, 2048:2560].rearrange("p (t n) -> p t n", t=4)
        post_bc = big[:, 20:22, :]
        x_sq = big[:, 12, :]
        hot_sb = scratch[0:NBUCKET + 1, 2560:2560 + EXT]
        rb_sb = scratch[0:NBUCKET + 1, 2944:2944 + H]
        ext_sb = scratch[0:H, 2960:2960 + EXT]
        gate_t = scratch[:, 0:2048].rearrange("p (s n) -> p s n", s=2)
        half0 = scratch[:, 0:4096].rearrange("p (b n) -> p b n", b=NB)
        junk_d = normw[:, :]

        def x1_again(b):
            return (a_hi if b < 4 else a_lo)[:, 4 + b % 4, :].bitcast(f32)

        SINK, DTB, EA, DD, NM, DEN, DEN_ODD, REC = range(8)
        DT, ADT, FS, TE, CD, T2, T3, T4 = range(8)
        minus_half = st[:, 62:63]

        def dt_slot(v):
            return dtv[:, v, :] if v <= CD else dt_tmp[:, v - T2, :]

        esk = [st[:, 64:72], st[:, 72:80]]
        mx = st[:, 112:114]
        nsink = st[:, 114:122]

        def den(i):
            return hv[:, DEN + i % 2, :]

        def tanh_at(m):
            return (tanh_t if m < len(SILU) - 2 else tanh_late)[:, m % 2, :]

        def w_out_at(k):
            return [ring(raw, U_OUT), ring(raw, U_OUT + 1), xr[:, 0, :], xr[:, 1, :], proj(K), proj(V),
                    ring(raw, U_OUT + 6), ring(raw, U_OUT + 7)][k]

        def out_bank(b):
            return 0 if b < NB - 1 else 6

        s_const = sem("c_and_constants_loaded")
        s_small, s_late = sem("early_vectors_loaded"), sem("late_vectors_loaded")
        s_x = [sem(f"x_block_loaded{i}") for i in range(NB)]
        s_ada = [[sem(f"ada_chunk_loaded{i}_half{j}") for j in range(2)] for i in range(2)]
        s_w = [sem(f"w_unit_loaded{i}") for i in range(2)]
        s_wm = [sem(f"middle_w_out_loaded{i}") for i in range(2)]
        s_bd, s_bl = sem("bias_vectors_stored"), sem("bias_windows_loaded")
        s_xr = [sem(f"x_reloaded{i}") for i in range(2)]
        s_x1 = [sem(f"x1_stored{i}") for i in range(2)]
        s_x1l = sem("x1_reloaded")
        s_out = [sem(f"out_stored{i}") for i in range(2)]
        s_pool, s_pc = sem("pool_constants"), sem("pool_chain")
        s_cs = sem("silu_c_ready")
        s_sq, s_rs = sem("x_squares_summed"), sem("x_rstd_ready")
        s_xn, s_xT, s_xe = sem("xn_ready"), sem("xn_transposed"), sem("xnT_evacuated")
        s_acc = sem("ada_chunk_summed")
        s_rT, s_cols = sem("vector_rows_transposed"), sem("columns_ready")
        s_mp, s_mod = sem("mod_sums_in_psum"), sem("mod_ready")
        s_h, s_hA = sem("h_even_tiles_modulated"), sem("h_odd_tiles_modulated")
        s_hhi, s_hlo = sem("h_hi_ready"), sem("h_lo_ready")
        s_whi, s_wlo, s_wu = sem("w_hi_ready"), sem("w_lo_ready"), sem("w_unit_used")
        s_evA, s_evD = sem("psum_freed_by_act"), sem("psum_freed_by_dve")
        s_c0, s_th, s_si = sem("conv_first_tap"), sem("tanh_done"), sem("silu_done")
        s_ext, s_exs = sem("bias_vectors_in_psum"), sem("bias_vectors_ready")
        s_flp, s_bias = sem("bias_flipped"), sem("bias_ready")
        s_dtT, s_dtn = sem("dt_evacuated"), sem("dt_transposed")
        s_dt1, s_dtA = sem("dt_steps_of_dve"), sem("dt_steps_of_act")
        s_dte, s_dtc, s_dt2 = sem("dt_a_ready"), sem("dt_a_sums_in_psum"), sem("dt_a_sums_taken")
        s_vT, s_v = sem("v_transposed"), sem("v_rows_ready")
        s_t1, s_bn = sem("b_transposed"), sem("b_rows_ready")
        s_xsT, s_xc = sem("xs_transposed"), sem("xc_ready")
        s_cb, s_cbm = sem("cb_in_psum"), sem("cb_masked")
        s_rd, s_D, s_E = sem("decay_terms_ready"), sem("segment_sums_in_psum"), sem("decay_ready")
        s_W = sem("ssd_weights_ready")
        s_yo, s_yd, s_sn = sem("y_off_in_psum"), sem("y_diag_in_psum"), sem("state_in_psum")
        s_ya, s_yb, s_su = sem("y_off_taken"), sem("y_diag_taken"), sem("state_updated")
        s_zT, s_g = sem("z_transposed"), sem("y_gated")
        s_gq, s_gr, s_my = sem("gated_squares"), sem("gated_rstd"), sem("ssm_rows_ready")
        s_S, s_sb = sem("scores_in_psum"), sem("scores_taken")
        s_nm, s_p = sem("neg_max_ready"), sem("probs_ready")
        s_pT, s_pe, s_pv = sem("probs_transposed"), sem("probsT_ready"), sem("pv_done")
        s_nms, s_es, s_o = sem("sink_minus_max"), sem("sink_exp"), sem("attention_rows_ready")
        s_wr = sem("w_out_tile_used_up")
        s_mT, s_mh, s_ml = sem("mixed_rows_transposed"), sem("mixT_hi_ready"), sem("mixT_lo_ready")
        s_mq, s_mr, s_mf, s_mx = sem("mixed_squares"), sem("mixed_rstd"), sem("mixed_rows_taken"), sem("x1_ready")
        s_q2, s_r2, s_n2 = sem("x1_squares"), sem("x1_rstd"), sem("x1_normalised")
        s_T2, s_e2 = sem("x1_transposed"), sem("x1T_evacuated")
        s_h2, s_h2h, s_h2l = sem("h2_modulated"), sem("h2_hi_ready"), sem("h2_lo_ready")
        s_ah, s_z0 = sem("h2_tile_used_up"), sem("z_halved")
        s_u0, s_uc, s_u1 = sem("up_first_tap"), sem("up_second_tap"), sem("up_taps_done")
        s_ge, s_f = sem("gelu_done"), sem("f_ready")
        s_fh, s_fl, s_fu = sem("f_hi_ready"), sem("f_lo_ready"), sem("f_first_tile_used")
        s_dn, s_d0 = sem("down_bank_done"), sem("down_half0_evacuated")
        s_hq, s_hg = sem("down_half0_squares"), sem("down_half0_gated")
        s_dq, s_dr, s_do = sem("down_squares"), sem("down_rstd"), sem("out_rows_ready")
        s_dv, s_ac = sem("dve_chain"), sem("act_chain")

        block = ctx.enter_context(nc.Block())

        def bank_done(eng, s, half, b, u):
            if b < NB - 1:
                eng.wait_ge(s, (NB - 1) * half + b + 1)
            else:
                eng.wait_ge(s_wu, u + 1)

        def loaded(u):
            return 16 * (u // 2 + 1 + min(2, u // 2 + 1) - (u > U_DT and u % 2 == U_DT % 2)
                         - 2 * (u >= U_OUT + 6))

        @block.sync
        def _(sp):
            def load_x(b):
                if b >= 4:
                    sp.wait_ge(s_xT, b - 3)
                sp.dma_start(x_in(b), x2[b * P:(b + 1) * P, :]).then_inc(s_x[b], 16)

            def load_chunk(n):
                if n >= 2:
                    sp.wait_ge(s_acc, n - 1)
                for half in range(2):
                    js = slice(half * KT // 2, (half + 1) * KT // 2)
                    sp.dma_start(chunk[n % 2][:, js, :], w_ada2[:, n * 512:(n + 1) * 512]
                                 .rearrange("(p j) n -> p j n", j=KT)[:, js, :]).then_inc(s_ada[n % 2][half], 16)

            load_x(0)
            load_x(1)
            sp.dma_start(ca[:, 0, :], c.rearrange("o (p j) -> p (o j)", j=KT)).then_inc(s_const, 16)
            sp.dma_start(sq[:, :], squares[:, 0:3 * P]).then_inc(s_const, 16)
            sp.dma_start(flip, squares[:, 3 * P:]).then_inc(s_const, 16)
            load_chunk(0)
            load_x(2)
            load_x(3)
            for m, (r0, v) in enumerate([(0, b_ada), (48, pre_mix_w), (56, pre_ffn_w)]):
                n = v.shape[1] // P
                sp.dma_start(rows[r0:r0 + n, 0, :], v[0].rearrange("(r n) -> r n", n=P)).then_inc(s_small, 16)
            sp.dma_start(rows[0:32, 1, :], ssm_conv_w[0].rearrange("t (m n) -> (t m) n", n=P)).then_inc(s_small, 16)
            sp.dma_start(rows[32:40, 1, :], ssm_conv_b[0].rearrange("(r n) -> r n", n=P)).then_inc(s_small, 16)
            fw = ffn_conv_w[0].rearrange("t (m n) -> (t m) n", n=P)
            sp.dma_start(rows[0:88, 2, :], fw[0:88, :]).then_inc(s_small, 16)
            sp.dma_start(rows[0:44, 3, :], fw[88:132, :]).then_inc(s_small, 16)
            sp.dma_start(rows[44:88, 3, :], ffn_conv_b[0].rearrange("(r n) -> r n", n=P)).then_inc(s_small, 16)
            sp.dma_start(hot_sb, hot).then_inc(s_small, 16)
            sp.wait_ge(s_pool, 1)
            sp.dma_start(rb_sb[0:NBUCKET, :], rel_bias).then_inc(s_small, 16)
            load_chunk(1)
            load_x(4)
            load_x(5)
            load_chunk(2)
            load_x(6)
            load_x(7)
            load_chunk(3)

            def load_late():
                for dst, row in [(hv[:, SINK, :], attn_sinks), (hv[:, DTB, :], ssm_dt_bias),
                                 (hv[:, EA, :], ssm_a_log), (hv[:, DD, :], ssm_d), (normw[:, :], ssm_norm_w),
                                 (gate_rows[:, 0, :], b_ada[:, 2 * D:3 * D]),
                                 (gate_rows[:, 1, :], b_ada[:, 5 * D:6 * D]),
                                 (post_bc[:, 0, :], post_mix_w), (post_bc[:, 1, :], post_ffn_w)]:
                    sp.dma_start(dst, row.to_broadcast([P, row.shape[-1]])).then_inc(s_late, 16)
                sp.dma_start(raw_dt[:, :, :], w_in2.rearrange("(k p) n -> p k n", p=P)[:, :, 18 * P:18 * P + H])\
                    .then_inc(s_late, 16)

            in_src = w_in2.rearrange("(k p) n -> p k n", p=P)

            def load_in(n):
                dst = ring(raw, n).rearrange("p (k n) -> p k n", k=KT)
                c0 = COLUMN[n] * P
                if n < K:
                    for e in range(2):
                        h = n + 4 * e
                        sp.dma_start(dst[:, :, e * HD:(e + 1) * HD],
                                     in_src[:, :, h * HD:(h + 1) * HD]).then_inc(s_w[n % 2], 16)
                else:
                    sp.dma_start(dst, in_src[:, :, c0:c0 + P]).then_inc(s_w[n % 2], 16)

            for n in range(U_OUT):
                if n < 2:
                    sp.wait_ge(s_xT, 5 + n)
                else:
                    sp.wait_ge(s_wlo, n - 1)
                if n != U_DT:
                    load_in(n)
                if n == 1:
                    load_chunk(4)
                    load_chunk(5)
                if n == 2:
                    sp.wait_ge(s_hlo, KT)
                    load_late()
                for chunk_no in {2: [6], 3: [7], 4: [8], 5: [9, 10], 6: [11]}.get(n, []):
                    load_chunk(chunk_no)

            def load_xr(b):
                sp.dma_start(xr[:, b % 2, :], x2[b * P:(b + 1) * P, :]).then_inc(s_xr[b % 2], 16)

            def load_out(k, done):
                sp.dma_start(w_out_at(k), w_out2[k * P:(k + 1) * P, :]).then_inc(done, 16)

            for k in range(2):
                sp.wait_ge(s_wlo, U_OUT + k - 1)
                load_out(k, s_w[(U_OUT + k) % 2])
            sp.wait_ge(s_pv, N_PAIRS)
            for k in range(2, 6):
                load_out(k, s_wm[k // 4])
            for k in range(6, KT):
                sp.wait_ge(s_wlo, U_OUT + k - 5)
                load_out(k, s_w[(U_OUT + k) % 2])
            sp.wait_ge(s_wlo, U_OUT + 4)
            load_xr(0)
            load_xr(1)

            def load_rows(u, w, half, k0):
                sp.dma_start(ring(raw, u).rearrange("p (k n) -> p k n", k=2),
                             w[bass.ds(k0 * P, 2 * P), half * 512:(half + 1) * 512]
                             .rearrange("(k p) n -> p k n", p=P)).then_inc(s_w[u % 2], 16)

            def load_up(i, t):
                u = U_UP + t
                sp.wait_ge(s_wlo, i * 4 + (u - 1))
                col = i * (2 * P) + ((t // 2) * P + (t % 2) * FF)
                sp.dma_start(ring(raw, u).rearrange("p (k n) -> p k n", k=KT),
                             w_up2[:, bass.ds(col, P)].rearrange("(k p) n -> p k n", p=P))\
                    .then_inc(s_w[u % 2], 16)

            for t in range(2):
                load_up(0, t)
            for b in range(NB):
                sp.wait_ge(s_mx, b + 1)
                sp.dma_start(x1_d[b * P:(b + 1) * P, :], xr[:, b % 2, :]).then_inc(s_x1[b % 2], 16)
                if b + 2 < NB:
                    sp.wait_ge(s_n2, b + 1)
                    sp.wait_ge(s_x1[b % 2], 16 * (b // 2 + 1))
                    load_xr(b + 2)
            for t in range(2, 4):
                load_up(0, t)
            with sp.Fori(1, FT // 2) as i:
                for t in range(4):
                    load_up(i, t)

            for half in range(2):
                for kk in range(11):
                    u = U_DOWN + 11 * half + kk
                    sp.wait_ge(s_wlo, u - 1)
                    load_rows(u, w_down2, half, 2 * kk)
            for n in range(2):
                sp.wait_ge(s_x1[n], 16 * NB // 2)
            sp.wait_ge(s_wu, U_DOWN)
            for b in range(NB):
                sp.dma_start(x1_again(b), x1_d[b * P:(b + 1) * P, :]).then_inc(s_x1l, 16)
            for b in range(NB):
                sp.wait_ge(s_do, b + 1)
                sp.dma_start(out2[b * P:(b + 1) * P, :], ring(raw, b)).then_inc(s_out[b % 2], 16)
            for n in range(2):
                sp.wait_ge(s_out[n], 16 * NB // 2)

        @block.gpsimd
        def _(pool):
            pool.memset(rb_sb, NEG).then_inc(s_pool, 1)
            pool.memset(ones[:, :], 1.0).then_inc(s_pool, 1)
            pool.memset(minus_half, -0.5).then_inc(s_pool, 1)

            chain = [0]

            def link(ins):
                chain[0] += 1
                ins.then_inc(s_pc, 1)
                pool.wait_ge(s_pc, chain[0])

            def rstd(dst, src, width, done):
                link(pool.tensor_scalar(src, src, 1.0 / width, EPS, ALU.mult, ALU.add))
                power = minus_half if src.shape[1] == 1 else minus_half.to_broadcast(list(src.shape))
                pool.tensor_tensor(dst, src, power, ALU.pow).then_inc(done, 1)

            def x_rstd(b):
                pool.wait_ge(s_sq, b + 1)
                rstd(st[:, 8 + b:9 + b], st[:, b:b + 1], D, s_rs)

            pool.wait_ge(s_pool, 3)
            for b in range(2):
                x_rstd(b)
            pool.wait_ge(s_exs, 1)
            pool.dma_start(bias_d, ext_sb).then_inc(s_bd, 16)
            for b in range(2, NB):
                x_rstd(b)
            pool.wait_ge(s_bd, 16)
            for e in range(2):
                src = bass.AP(bias_d.tensor, 4 * e * EXT, [[1, P], [EXT, NPAIR], [1, 2 * P]])
                pool.dma_start(bias[:, :, e, :], src).then_inc(s_bl, 16)

            def decay_terms(i):
                if i >= 1:
                    pool.wait_ge(s_yd, i)
                for g in range(GROUPS):
                    adt = dtv[:, ADT, i * H + 4 * g:i * H + 4 * g + 4].unsqueeze(2).to_broadcast([P, 4, P])
                    tri = upper.unsqueeze(1).to_broadcast([P, 4, P])
                    pool.tensor_tensor(decay[:, g, :].rearrange("p (h l) -> p h l", h=4), tri, adt,
                                       ALU.mult).then_inc(s_rd, 1)

            pool.wait_ge(s_dte, 1)
            decay_terms(0)
            pool.wait_ge(s_si, len(SILU) - 2)
            link(pool.memset(state, 0.0))
            for i in range(NB + 2):
                b = i - 2
                if b >= 0:
                    pool.wait_ge(s_mq, b + 1)
                    rstd(st[:, 80 + b:81 + b], st[:, 16 + b:17 + b], D, s_mr)
                    pool.wait_ge(s_q2, b + 1)
                    rstd(st[:, 40 + b:41 + b], st[:, 32 + b:33 + b], D, s_r2)
                if i + 1 < NB:
                    decay_terms(i + 1)
                if i < NB:
                    pool.wait_ge(s_gq, i + 1)
                    rstd(st[:, 58:60], st[:, 56:58], SSM_W // GROUPS, s_gr)
            for b in range(NB):
                pool.wait_ge(s_dq, b + 1)
                link(pool.tensor_tensor(st[:, 88 + b:89 + b], st[:, 88 + b:89 + b], st[:, 96 + b:97 + b], ALU.add))
                rstd(st[:, 104 + b:105 + b], st[:, 88 + b:89 + b], D, s_dr)

        @block.scalar
        def _(act):
            act.wait_ge(s_const, 48)
            act.activation(ca[:, 1, :], ca[:, 0, :], ACT.Silu).then_inc(s_cs, 1)
            chain = [0]

            def link(ins):
                chain[0] += 1
                ins.then_inc(s_ac, 1)
                act.wait_ge(s_ac, chain[0])

            def x_squares(b):
                act.wait_ge(s_x[b], 16)
                if b >= 1:
                    act.wait_ge(s_sq, b)
                act.activation(x_sq, x_in(b), ACT.Square, accum_out=st[:, b:b + 1]).then_inc(s_sq, 1)

            def x_evacuate(b):
                act.wait_ge(s_xT, b + 1)
                act.activation(xnT[:, :, b * P:(b + 1) * P],
                               bank(2 * (b % 3), 2).rearrange("p (k t) -> p k t", k=KT), ACT.Copy).then_inc(s_xe, 1)

            def split_hi(u, du=0):
                slot = u % 2
                act.wait_ge(s_w[slot], du * 8 + loaded(u))
                if u >= 2:
                    act.wait_ge(s_wu, du + (u - 1))
                act.activation(ring(w_hi, u), ring(raw, u), ACT.Copy).then_inc(s_whi, 1)

            for b in range(NB):
                x_squares(b)
                if b >= 3:
                    x_evacuate(b - 3)
            x_evacuate(NB - 3)
            x_evacuate(NB - 2)
            split_hi(0)
            x_evacuate(NB - 1)

            def h_modulate(k):
                act.activation(xnT[:, k, :], xnT[:, k, :], ACT.Identity, scale=modc[:, 8 + k:9 + k],
                               bias=modc[:, k:k + 1]).then_inc(s_hA, 1)

            def h_hi(k):
                act.wait_ge(s_hA if k % 2 else s_h, k // 2 + 1)
                act.activation(a_hi[:, k, :], xnT[:, k, :], ACT.Copy).then_inc(s_hhi, 1)

            act.wait_ge(s_mod, 1)
            act.wait_ge(s_xe, NB)
            h_hi(0)
            h_modulate(1)
            for k in range(2, KT, 2):
                h_modulate(k + 1)
                h_hi(k - 1)
                h_hi(k)
            h_hi(KT - 1)

            def evacuate(n):
                act.wait_ge(s_wu, n + 1)
                src = bank(2 * (n % 2), 2)
                if n == V + 1:
                    act.wait_ge(s_mod, 6)
                if n == U_DT:
                    act.activation(dt_rows, src[0:16, :], ACT.Copy).then_inc(s_dtT, 1)
                elif n in CONV:
                    m = CONV.index(n)
                    act.activation(proj(n), src, ACT.Identity, scale=cols[:, C_CONV + 24 + m:C_CONV + 25 + m],
                                   bias=cols[:, C_CONV + 32 + m:C_CONV + 33 + m]).then_inc(s_c0, 1)
                elif n >= Z:
                    if n == Z + 2:
                        act.wait_ge(s_dt1, 3)
                    act.activation(proj(n), src, ACT.Copy, scale=0.5).then_inc(s_z0, 1)
                else:
                    act.activation(proj(n), src, ACT.Copy).then_inc(s_evA, 1)

            def tanh(n):
                m = SILU.index(n)
                if m >= 2:
                    act.wait_ge(s_si, m - 1)
                if n in CONV:
                    act.wait_ge(s_evD, CONV_BY_TIME.index(n) + 1)
                else:
                    act.wait_ge(s_z0, n - Z + 1)
                act.activation(tanh_at(m), proj(n), ACT.Tanh).then_inc(s_th, 1)

            def probs(u):
                i, j = u // NPAIR, u % NPAIR
                act.wait_ge(s_nm, u + 1)
                if j == 0 and i >= 2:
                    act.wait_ge(s_o, i - 1)
                k0 = P if i == 0 else 0
                for e in range(2):
                    h = j + 4 * e
                    ins = act.activation(prob[:, u % 2, e, k0:], prob[:, u % 2, e, k0:], ACT.Exp,
                                         bias=hv[:, NM, h:h + 1], accum_out=den(i)[:, h:h + 1])
                ins.then_inc(s_p, 1)
                if j == NPAIR - 1:
                    act.wait_ge(s_nms, i + 1)
                    act.activation(esk[i % 2], esk[i % 2], ACT.Exp).then_inc(s_es, 1)

            def probs_evacuate(u):
                act.wait_ge(s_pT, u + 1)
                if u >= 2:
                    act.wait_ge(s_pv, u - 1)
                src = bank(6).rearrange("p (e k q) -> p e k q", e=2, k=2)
                dst = probT[:, (u % 2) * 512:(u % 2 + 1) * 512].rearrange("p (e k q) -> p e k q", e=2, k=2)
                k0 = 1 if u < NPAIR else 0
                act.activation(dst[:, :, k0:, :], src[:, :, k0:, :], ACT.Copy).then_inc(s_pe, 1)

            def maybe(step, u):
                if 0 <= u < N_PAIRS:
                    step(u)

            split_hi(1)
            for j in range(NPAIR):
                act.wait_ge(s_flp, j + 1)
                act.activation(bias[:, j], bank(4 + j).rearrange("p (e k) -> p e k", e=2), ACT.Copy)\
                    .then_inc(s_bias, 1)
            for n in range(1, U_OUT):
                if n + 1 == U_DT:
                    act.wait_ge(s_late, 16 * N_LATE)
                    act.wait_ge(s_wu, n)
                    wdt = ring(w_hi, U_DT).rearrange("p (k n) -> p k n", k=KT)
                    act.activation(wdt[:, :, 0:H], raw_dt[:, :, :], ACT.Copy).then_inc(s_whi, 1)
                elif n + 1 < U_OUT:
                    split_hi(n + 1)
                evacuate(n - 1)
                if n == 6:
                    act.wait_ge(s_vT, 1)
                    act.activation(proj(V), bank(6, 2), ACT.Copy).then_inc(s_v, 1)
                u = 3 * (n - A0)
                maybe(probs_evacuate, u - 2)
                maybe(probs, u)
                if n == U_DT + 1:
                    act.wait_ge(s_dt1, 1)
                    act.activation(dt_slot(T2), dt_slot(T4), ACT.Exp, scale=-1.0).then_inc(s_dtA, 1)
                    act.activation(hv[:, EA, :], hv[:, EA, :], ACT.Exp).then_inc(s_dtA, 1)
                if n == U_DT + 2:
                    act.wait_ge(s_dt2, 1)
                    act.activation(dtv[:, FS:CD + 1, :], dtv[:, FS:CD + 1, :], ACT.Exp).then_inc(s_dtA, 1)
                maybe(probs_evacuate, u - 1)
                if n >= A0:
                    maybe(probs_evacuate, u)
                    maybe(probs, u + 1)
                    if n == U_DT + 1:
                        act.wait_ge(s_dt1, 2)
                        act.activation(dtv[:, FS, :], dt_slot(T4), ACT.Ln).then_inc(s_dtA, 1)
                    maybe(probs, u + 2)
                if n - 1 in SILU:
                    tanh(n - 1)
            def w_out_hi(k):
                u = U_OUT + k
                if 2 <= k < 6:
                    act.wait_ge(s_wm[k // 4], 32)
                else:
                    act.wait_ge(s_w[u % 2], loaded(u))
                if k == 0:
                    act.wait_ge(s_wu, U_OUT)
                act.activation(a_hi[:, k, :], w_out_at(k), ACT.Copy).then_inc(s_whi, 1)

            def mixed_squares(b):
                act.wait_ge(s_wu, U_OUT + b + 1)
                if b >= 1:
                    act.wait_ge(s_mq, b)
                act.activation(junk[0], bank(out_bank(b), 2), ACT.Square, accum_out=st[:, 16 + b:17 + b])\
                    .then_inc(s_mq, 1)

            def x1_squares(b):
                act.wait_ge(s_mx, b + 1)
                if b >= 1:
                    act.wait_ge(s_q2, b)
                act.activation(junk[1], xr[:, b % 2, :], ACT.Square, accum_out=st[:, 32 + b:33 + b]).then_inc(s_q2, 1)

            def x1_evacuate(b):
                act.wait_ge(s_T2, b + 1)
                act.activation(x1nT[:, :, b * P:(b + 1) * P],
                               bank(4 if b == NB - 1 else 2, 2).rearrange("p (k t) -> p k t", k=KT), ACT.Copy)\
                    .then_inc(s_e2, 1)

            def decay_exp(i, g):
                act.wait_ge(s_D, 2 * i + g + 1)
                act.activation(decay[:, g, :], bank(5 + 2 * g), ACT.Exp).then_inc(s_E, 1)

            def open_ssd(i):
                act.wait_ge(s_t1, i + 1)
                if i >= 1:
                    act.wait_ge(s_sn, i)
                act.activation(bn, bank(4)[:, 0:2 * P].rearrange("p (g n) -> p g n", g=2), ACT.Copy).then_inc(s_bn, 1)
                decay_exp(i, 0)

            open_ssd(0)
            evacuate(U_OUT - 1)
            decay_exp(0, 1)
            tanh(U_OUT - 1)
            for k in range(2):
                w_out_hi(k)

            for i in range(NB + 1):
                if 1 <= i < NB:
                    open_ssd(i)
                if 2 <= i < NB:
                    mixed_squares(i - 2)
                if 1 <= i < NB:
                    decay_exp(i, 1)
                if i == 0:
                    for k in range(2, 6):
                        w_out_hi(k)
                if i >= 1:
                    act.wait_ge(s_mT, i)
                    act.activation(by_tile(ring(w_hi, U_OUT + i - 1)), by_tile(bank(2, 2)), ACT.Copy).then_inc(s_mh, 1)
                if i == 1:
                    for k in range(6, KT):
                        w_out_hi(k)
                if i == NB:
                    mixed_squares(i - 2)
                if i >= 2:
                    x1_squares(i - 2)
                if i < NB:
                    act.wait_ge(s_g, i + 1)
                    for g in range(GROUPS):
                        ins = act.activation(four(Z, i)[:, 2 * g:2 * g + 2, :],
                                             yy[:, g * 256:(g + 1) * 256].rearrange("p (a b) -> p a b", a=2),
                                             ACT.Square, accum_out=st[:, 56 + g:57 + g])
                    ins.then_inc(s_gq, 1)
                if 2 <= i < NB:
                    x1_evacuate(i - 2)

            def h2_hi(hf, k):
                if hf == 0 and k == KT - 1:
                    act.wait_ge(s_wu, U_UP)
                elif hf == 0:
                    act.wait_ge(s_wr, k + 1)
                act.wait_ge(s_h2, KT * hf + k + 1)
                act.activation(a_hi[:, k, hf * 512:(hf + 1) * 512], x1nT[:, k, hf * 512:(hf + 1) * 512],
                               ACT.Copy).then_inc(s_h2h, 1)

            split_hi(U_UP)
            for k in range(KT - 1):
                if k == 5:
                    x1_evacuate(NB - 2)
                h2_hi(0, k)
            mixed_squares(NB - 1)
            h2_hi(0, KT - 1)
            split_hi(U_UP + 1)
            x1_squares(NB - 1)
            x1_evacuate(NB - 1)
            for k in range(KT):
                h2_hi(1, k)

            def column(base, i, t):
                return cols[:, bass.ds(i * 2 + (base + t // 2 + FT * (t % 2)), 1)]

            def f_tile(k):
                return flat(big[:, bass.ds(k, 1), :])

            def up_first_tap(i, t, first):
                act.wait_ge(s_wu, i * 4 + (U_UP + t + 1))
                if t % 2:
                    dst = f_tile(i * 2 + t // 2)
                else:
                    dst = gate_t[:, t // 2, :]
                    if not first:
                        act.wait_ge(s_f, i * 2 + (t // 2 - 1))
                act.activation(dst, bank(2 * t, 2), ACT.Identity, scale=column(C_FFN + 88, i, t),
                               bias=column(C_FFN + 132, i, t)).then_inc(s_u0, 1)

            def up_gelu(i, pr):
                act.wait_ge(s_u1, i * 4 + (2 * pr + 1))
                act.activation(gate_t[:, pr, :], gate_t[:, pr, :], ACT.Gelu_apprx_tanh).then_inc(s_ge, 1)

            def f_split_hi(half, kk, e, skip=0):
                if isinstance(kk, int) and half == 0 and kk == 0:
                    act.wait_ge(s_ah, e + 1)
                elif e == 0:
                    act.wait_ge(s_fu, kk + (DOWN_UNITS * half - skip))
                else:
                    act.wait_ge(s_wu, kk + (U_DOWN + DOWN_UNITS * half - skip))
                act.activation(a_hi[:, e, :], f_tile(kk * 2 + e), ACT.Copy).then_inc(s_fh, 1)

            def up_body(i, first=False, last=False):
                for t in range(4):
                    if not (first and t == 0):
                        split_hi(U_UP + t + 1, i * 4)
                    if last and t == 3:
                        for e in range(2):
                            f_split_hi(0, 0, e)
                    up_first_tap(i, t, first)
                    if t % 2:
                        up_gelu(i, t // 2)

            up_body(0, first=True)
            with act.Fori(1, FT // 2 - 1) as i:
                up_body(i)
            up_body(FT // 2 - 1, last=True)

            def down_unit(half, kk0, dk, split_next=True):
                for e in range(2):
                    f_split_hi(half, dk + kk0, e)
                if split_next:
                    split_hi(U_DOWN + DOWN_UNITS * half + kk0 + 1, dk)

            for half in range(2):
                split_hi(U_DOWN + DOWN_UNITS * half + 1)
                with act.Fori(0, 4) as i:
                    down_unit(half, 1, i * 2)
                    down_unit(half, 2, i * 2)
                if half == 1:
                    for e in range(2):
                        act.activation(a_hi[:, 2 + e, :], f_tile(FT - 4 + e), ACT.Copy).then_inc(s_fh, 1)
                    for b in range(NB):
                        act.wait_ge(s_d0, b + 1)
                        if b >= 1:
                            act.wait_ge(s_hq, b)
                        act.activation(junk_d, half0[:, b, :], ACT.Square, accum_out=st[:, 88 + b:89 + b])\
                            .then_inc(s_hq, 1)
                if half == 0:
                    down_unit(half, 9, 0)
                    down_unit(half, 10, 0)
                else:
                    f_split_hi(1, DOWN_UNITS - 1, 0, skip=1)
                    split_hi(U_END - 1)
                    f_split_hi(1, DOWN_UNITS - 1, 1, skip=1)
                if half == 0:
                    f_split_hi(1, 0, 0)
                    for b in range(NB):
                        bank_done(act, s_dn, 0, b, U_DOWN + DOWN_UNITS - 1)
                        act.activation(half0[:, b, :], bank(b), ACT.Copy).then_inc(s_d0, 1)
                    f_split_hi(1, 0, 1)
            for b in range(NB):
                bank_done(act, s_dn, 1, b, U_END - 1)
                if b >= 1:
                    act.wait_ge(s_dq, b)
                else:
                    act.wait_ge(s_hq, NB)
                act.activation(junk_d, bank(b), ACT.Square, accum_out=st[:, 96 + b:97 + b]).then_inc(s_dq, 1)

        @block.vector
        def _(dve):
            chain = [0]

            def link(ins):
                chain[0] += 1
                ins.then_inc(s_dv, 1)
                dve.wait_ge(s_dv, chain[0])

            def normalise(b):
                dve.wait_ge(s_rs, b + 1)
                dve.tensor_scalar(x_in(b), x_in(b), st[:, 8 + b:9 + b], None, ALU.mult).then_inc(s_xn, 1)

            def sum_chunk(n):
                if n == 0:
                    dve.wait_ge(s_cs, 1)
                dve.wait_ge(s_ada[n % 2][0], 16 * (n // 2 + 1))
                part = acc[:, n * 512:(n + 1) * 512]
                link(dve.tensor_scalar(part, chunk[n % 2][:, 0, :], ca[:, 1, 0:1], None, ALU.mult))
                for j in range(1, KT):
                    if j == KT // 2:
                        dve.wait_ge(s_ada[n % 2][1], 16 * (n // 2 + 1))
                    ins = dve.scalar_tensor_tensor(out=part, in0=chunk[n % 2][:, j, :], scalar=ca[:, 1, j:j + 1],
                                                   in1=part, op0=ALU.mult, op1=ALU.add)
                    if j < KT - 1:
                        link(ins)
                ins.then_inc(s_acc, 1)

            normalise(0)
            normalise(1)
            sum_chunk(0)

            dve.wait_ge(s_rT, 1)
            link(dve.tensor_copy(cols[:, :], bank(7)[:, 0:280]))
            conv_cols = cols[:, C_CONV:C_CONV + N_CONV_ROWS]
            dve.tensor_scalar(conv_cols, conv_cols, 0.5, None, ALU.mult).then_inc(s_cols, 1)
            dve.wait_ge(s_ext, 1)
            dve.tensor_copy(ext_sb, bank(6)[0:H, 0:EXT]).then_inc(s_exs, 1)

            sum_chunk(1)
            normalise(2)
            normalise(3)
            sum_chunk(2)
            normalise(4)
            normalise(5)
            normalise(6)
            normalise(7)
            sum_chunk(3)
            dve.wait_ge(s_cols, 1)

            def take_columns(n):
                link(dve.tensor_tensor(modc[:, 16 * n:16 * n + 16], bank(6)[:, EXT + 16 * n:EXT + 16 * n + 16],
                                       cols[:, 24 * n:24 * n + 16], ALU.add))
                dve.scalar_tensor_tensor(out=modc[:, 16 * n + 8:16 * n + 16], in0=modc[:, 16 * n + 8:16 * n + 16],
                                         scalar=1.0, in1=cols[:, 48 + 8 * n:56 + 8 * n],
                                         op0=ALU.add, op1=ALU.mult).then_inc(s_mod, 1)

            def take_gate(n, half):
                part = gate_rows[:, n, half * 512:(half + 1) * 512]
                link(dve.tensor_tensor(part, bank(GATE_BANKS[2 * n + half]), part, ALU.add))
                dve.tensor_tensor(part, part, post_bc[:, n, half * 512:(half + 1) * 512], ALU.mult).then_inc(s_mod, 1)

            def split_lo(u, du=0):
                dve.wait_ge(s_whi, du + (u + 1))
                dve.tensor_tensor(ring(w_lo, u), ring(raw, u), ring(w_hi, u).bitcast(f32), ALU.subtract)\
                    .then_inc(s_wlo, 1)

            dve.wait_ge(s_mp, 1)
            take_columns(0)
            dve.wait_ge(s_mod, 1)
            dve.wait_ge(s_xe, NB)

            def modulate(tiles, k, n, c0, w, done):
                part = tiles[:, k, c0:c0 + w]
                dve.tensor_scalar(part, part, modc[:, 16 * n + 8 + k:16 * n + 9 + k],
                                  modc[:, 16 * n + k:16 * n + k + 1], ALU.mult, ALU.add).then_inc(done, 1)

            def h_lo(tiles, k, c0, w, done):
                dve.tensor_tensor(a_lo[:, k, c0:c0 + w], tiles[:, k, c0:c0 + w],
                                  a_hi[:, k, c0:c0 + w].bitcast(f32), ALU.subtract).then_inc(done, 1)

            modulate(xnT, 0, 0, 0, T, s_h)
            split_lo(0)
            for k in range(KT):
                if k % 2 == 0 and k + 2 < KT:
                    modulate(xnT, k + 2, 0, 0, T, s_h)
                dve.wait_ge(s_hhi, k + 1)
                h_lo(xnT, k, 0, T, s_hlo)

            def conv_tap(n, d):
                m = CONV.index(n)
                if d == 1:
                    dve.wait_ge(s_c0, CONV_BY_TIME.index(n) + 1)
                tap = C_CONV + 8 * (3 - d) + m
                ins = dve.scalar_tensor_tensor(out=proj(n)[:, d:], in0=bank(2 * (n % 2), 2)[:, 0:T - d],
                                               scalar=cols[:, tap:tap + 1], in1=proj(n)[:, d:],
                                               op0=ALU.mult, op1=ALU.add)
                if d < 3:
                    link(ins)
                else:
                    ins.then_inc(s_evD, 1)

            def silu_multiply(n):
                m = SILU.index(n)
                dve.wait_ge(s_th, m + 1)
                dve.scalar_tensor_tensor(out=proj(n), in0=tanh_at(m), scalar=1.0, in1=proj(n),
                                         op0=ALU.add, op1=ALU.mult).then_inc(s_si, 1)

            def scores(u):
                i, j = u // NPAIR, u % NPAIR
                k0 = P if i == 0 else 0
                s2 = bank(4, 2).rearrange("p (e k) -> p e k", e=2)
                dst = prob[:, u % 2, :, k0:]
                dve.wait_ge(s_S, u + 1)
                if u >= 2:
                    dve.wait_ge(s_pT, u - 1)
                if j == 0 and i >= 1:
                    dve.wait_ge(s_nms, i)
                dve.scalar_tensor_tensor(out=dst, in0=s2[:, :, k0:2 * P], scalar=HD ** -0.5, in1=bias[:, j, :, k0:],
                                         op0=ALU.mult, op1=ALU.add).then_inc(s_sb, 1)
                dve.wait_ge(s_sb, u + 1)
                link(dve.tensor_reduce(mx, dst, AX.X, ALU.max))
                dve.scalar_tensor_tensor(out=hv[:, NM, j::NPAIR], in0=mx, scalar=-1.0, in1=nsink[:, j::NPAIR],
                                         op0=ALU.mult, op1=ALU.min).then_inc(s_nm, 1)

            def attention_step(u):
                if u < N_PAIRS:
                    scores(u)
                if u < N_PAIRS and u % NPAIR == NPAIR - 1:
                    dve.wait_ge(s_nm, u + 1)
                    dve.tensor_tensor(esk[(u // NPAIR) % 2], hv[:, NM, :], hv[:, SINK, :], ALU.add).then_inc(s_nms, 1)
                if u >= NPAIR + 1 and u % NPAIR == 1:
                    i = u // NPAIR - 1
                    dve.wait_ge(s_es, i + 1)
                    link(dve.tensor_tensor(den(i), den(i), esk[i % 2], ALU.add))
                    link(dve.reciprocal(hv[:, REC, :], den(i)))
                    dve.wait_ge(s_pv, NPAIR * (i + 1))
                    dve.tensor_tensor(four(Q, i).rearrange("p t (e d) -> p t e d", e=2),
                                      bank(7).rearrange("p (t e d) -> p t e d", t=4, e=2),
                                      hv[:, REC, :].rearrange("p (t e) -> p t e", e=2).unsqueeze(3)
                                      .to_broadcast([P, 4, 2, HD]), ALU.mult).then_inc(s_o, 1)

            def by_head(v):
                return dt_slot(v).rearrange("p (b h) -> p b h", h=H)

            def head_row(r):
                return hv[:, r, :].unsqueeze(1).to_broadcast([P, NB, H])

            def dt_natural():
                dve.wait_ge(s_dtn, 1)
                dve.wait_ge(s_S, 3 * (U_DT + 1 - A0) + 2)
                link(dve.tensor_copy(dt_nat, bank(5)[:, 256:256 + P].rearrange("p (b n) -> p b n", b=NB)))
                link(dve.tensor_tensor(by_head(T3), dt_nat[:, :, 0:H], dt_nat[:, :, H:2 * H], ALU.add))
                link(dve.tensor_tensor(by_head(T3), by_head(T3), head_row(DTB), ALU.add))
                dve.scalar_tensor_tensor(out=dt_slot(T4), in0=dt_slot(T3), scalar=-1.0, in1=dt_slot(T3),
                                         op0=ALU.mult, op1=ALU.max).then_inc(s_dt1, 1)

            def dt_one_plus():
                dve.wait_ge(s_dtA, 2)
                dve.tensor_scalar(dt_slot(T4), dt_slot(T2), 1.0, None, ALU.add).then_inc(s_dt1, 1)
                dve.wait_ge(s_dt1, 2)
                link(dve.tensor_scalar(dt_slot(TE), dt_slot(T4), -1.0, None, ALU.add))
                link(dve.tensor_scalar(dt_slot(CD), dt_slot(TE), 0.0, None, ALU.is_equal))
                link(dve.tensor_tensor(dt_slot(TE), dt_slot(TE), dt_slot(CD), ALU.add))
                link(dve.reciprocal(dt_slot(TE), dt_slot(TE)))
                link(dve.tensor_tensor(dt_slot(TE), dt_slot(TE), dt_slot(T2), ALU.mult))

            def dt_finish():
                dve.wait_ge(s_dtA, 3)
                link(dve.tensor_tensor(dt_slot(FS), dt_slot(FS), dt_slot(CD), ALU.add))
                link(dve.tensor_tensor(dt_slot(FS), dt_slot(FS), dt_slot(TE), ALU.mult))
                dve.scalar_tensor_tensor(out=dt_slot(DT), in0=dt_slot(T3), scalar=0.0, in1=dt_slot(FS),
                                         op0=ALU.max, op1=ALU.add).then_inc(s_dt1, 1)
                dve.wait_ge(s_dt1, 3)
                link(dve.tensor_tensor(by_head(ADT), by_head(DT), head_row(EA), ALU.mult))
                dve.tensor_scalar(dt_slot(ADT), dt_slot(ADT), -1.0, None, ALU.mult).then_inc(s_dte, 1)

            def dt_sums():
                dve.wait_ge(s_dtc, 1)
                dve.wait_ge(s_S, 3 * (U_DT + 2 - A0) + 2)
                dve.tensor_copy(dtv[:, FS:CD + 1, :], bank(5)[:, 256:448].rearrange("p (v n) -> p v n", v=3))\
                    .then_inc(s_dt2, 1)

            def at(v, i):
                return per_head(dtv[:, v, i * H:(i + 1) * H])

            def ssd_rows(i):
                dve.wait_ge(s_xsT, i + 1)
                dve.tensor_tensor(heads(xc), heads(bank(6)), at(DT, i), ALU.mult)
                dve.tensor_tensor(heads(xc_end), heads(bank(6)), at(TE, i), ALU.mult)
                xd = four(XS, i).rearrange("p t (e d) -> p t e d", e=2)
                dve.tensor_tensor(xd, bank(6).rearrange("p (t e d) -> p t e d", t=4, e=2),
                                  hv[:, DD, :].rearrange("p (t e) -> p t e", e=2).unsqueeze(3)
                                  .to_broadcast([P, 4, 2, HD]), ALU.mult).then_inc(s_xc, 1)
                dve.wait_ge(s_cb, i + 1)
                dve.tensor_tensor(cbm, bank(7)[:, 0:256].rearrange("p (g l) -> p g l", g=2),
                                  upper.unsqueeze(1).to_broadcast([P, 2, P]), ALU.mult).then_inc(s_cbm, 1)

            def ssd_weights(i):
                dve.wait_ge(s_cbm, i + 1)
                for g in range(GROUPS):
                    dve.wait_ge(s_E, 2 * i + g + 1)
                    dg = decay[:, g, :].rearrange("p (h l) -> p h l", h=4)
                    dve.tensor_tensor(dg, dg, cbm[:, g, :].unsqueeze(1).to_broadcast([P, 4, P]),
                                      ALU.mult).then_inc(s_W, 1)

            split_lo(1)
            for n in range(U_OUT + 2):
                if n == U_OUT + 1:
                    ssd_weights(0)
                if n - 2 in SILU:
                    silu_multiply(n - 2)
                if n + 1 == U_DT:
                    dve.wait_ge(s_whi, U_DT + 1)
                    wdt = ring(w_hi, U_DT).rearrange("p (k n) -> p k n", k=KT)
                    dve.tensor_tensor(wdt[:, :, H:2 * H], raw_dt[:, :, :], wdt[:, :, 0:H].bitcast(f32),
                                      ALU.subtract).then_inc(s_wlo, 1)
                elif 2 <= n + 1 < U_OUT:
                    split_lo(n + 1)
                for chunk_no in {0: [4], 1: [5], 2: [6, 7], 3: [8], 4: [9], 5: [10, 11]}.get(n, []):
                    sum_chunk(chunk_no)
                if n == 4:
                    dve.wait_ge(s_late, 16 * N_LATE)
                    dve.tensor_scalar(nsink, hv[:, SINK, :], -1.0, None, ALU.mult)
                    for half in range(2):
                        dve.wait_ge(s_mp, 2 + half)
                        take_gate(0, half)
                if n == 5:
                    dve.wait_ge(s_mp, 4)
                    take_columns(1)
                if n == V + 1:
                    for half in range(2):
                        dve.wait_ge(s_mp, 5 + half)
                        take_gate(1, half)
                if n == U_DT + 3:
                    dve.wait_ge(s_dtA, 4)
                    dve.tensor_tensor(dt_slot(TE), dt_slot(TE), dt_slot(DT), ALU.mult)
                for r in range(3):
                    u = 3 * (n - A0) + r
                    if n - 1 in CONV:
                        conv_tap(n - 1, r + 1)
                    if n == U_DT + 1 and r == 1:
                        dt_natural()
                    if n == U_DT + 1 and r == 2:
                        dt_one_plus()
                    if n == U_DT + 2 and r == 1:
                        dt_sums()
                    if u >= 0 and n < U_OUT:
                        attention_step(u)
                if n == U_DT + 1:
                    dt_finish()
                if n == U_OUT - 1:
                    ssd_rows(0)

            def w_out_lo(k):
                u = U_OUT + k
                dve.wait_ge(s_whi, u + 1)
                dve.tensor_tensor(a_lo[:, k, :], w_out_at(k), a_hi[:, k, :].bitcast(f32), ALU.subtract)\
                    .then_inc(s_wlo, 1)

            def mixed_norm(b):
                dve.wait_ge(s_mr, b + 1)
                if b >= 2:
                    dve.wait_ge(s_T2, b - 1)
                dve.scalar_tensor_tensor(out=xn2[:, b % 2, :], in0=bank(out_bank(b), 2),
                                         scalar=st[:, 80 + b:81 + b], in1=gate_rows[:, 0, :],
                                         op0=ALU.mult, op1=ALU.mult).then_inc(s_mf, 1)

            def residual(b):
                dve.wait_ge(s_mf, b + 1)
                dve.wait_ge(s_xr[b % 2], 16 * (b // 2 + 1))
                dve.tensor_tensor(xr[:, b % 2, :], xr[:, b % 2, :], xn2[:, b % 2, :], ALU.add).then_inc(s_mx, 1)

            def normalise_x1(b):
                dve.wait_ge(s_r2, b + 1)
                dve.tensor_scalar(xn2[:, b % 2, :], xr[:, b % 2, :], st[:, 40 + b:41 + b], None,
                                  ALU.mult).then_inc(s_n2, 1)

            def h2_modulate(hf):
                dve.wait_ge(s_e2, 4 * (hf + 1))
                for k in range(KT):
                    modulate(x1nT, k, 1, hf * 512, 512, s_h2)

            def h2_lo(hf):
                for k in range(KT):
                    dve.wait_ge(s_h2h, KT * hf + k + 1)
                    h_lo(x1nT, k, hf * 512, 512, s_h2l)

            y4 = yy.rearrange("p (t n) -> p t n", t=4)
            for i in range(NB + 1):
                if i < NB:
                    if i >= 1:
                        ssd_rows(i)
                if i == 1:
                    for k in range(2, 4):
                        w_out_lo(k)
                if 1 <= i < NB:
                    ssd_weights(i)
                if 2 <= i < NB:
                    mixed_norm(i - 2)
                if i >= 1:
                    dve.wait_ge(s_mh, i)
                    u = U_OUT + i - 1
                    dve.tensor_tensor(by_tile(ring(w_lo, u)), by_tile(bank(2, 2)), by_tile(ring(w_hi, u).bitcast(f32)),
                                      ALU.subtract).then_inc(s_ml, 1)
                if i == 1:
                    for k in range(4, KT):
                        w_out_lo(k)
                if i == NB:
                    mixed_norm(i - 2)
                if i >= 2:
                    residual(i - 2)
                if i < NB:
                    dve.wait_ge(s_yo, i + 1)
                    dve.tensor_tensor(heads(yy), heads(bank(5)), at(FS, i), ALU.mult).then_inc(s_ya, 1)
                    dve.wait_ge(s_ya, i + 1)
                    dve.wait_ge(s_yd, i + 1)
                    dve.tensor_tensor(yy, yy, bank(6), ALU.add).then_inc(s_yb, 1)
                    link(dve.tensor_tensor(heads(state), heads(state), at(CD, i), ALU.mult))
                    dve.wait_ge(s_sn, i + 1)
                    dve.tensor_tensor(state, state, bank(7), ALU.add).then_inc(s_su, 1)
                    dve.wait_ge(s_yb, i + 1)
                    link(dve.tensor_tensor(y4, y4, four(XS, i), ALU.add))
                    dve.wait_ge(s_zT, i + 1)
                    dve.tensor_tensor(yy, yy, bank(5), ALU.mult).then_inc(s_g, 1)
                if i == 0:
                    w_out_lo(0)
                    w_out_lo(1)
                if i == NB:
                    split_lo(U_UP)
                if i >= 2:
                    normalise_x1(i - 2)
                if i < NB:
                    dve.wait_ge(s_gr, i + 1)
                    for g in range(GROUPS):
                        ins = dve.scalar_tensor_tensor(
                            out=four(Z, i)[:, 2 * g:2 * g + 2, :], in0=y4[:, 2 * g:2 * g + 2, :],
                            scalar=st[:, 58 + g:59 + g],
                            in1=normw[:, g * 256:(g + 1) * 256].rearrange("p (a b) -> p a b", a=2),
                            op0=ALU.mult, op1=ALU.mult)
                    ins.then_inc(s_my, 1)
                if i == NB - 1:
                    h2_modulate(0)

            h2_lo(0)
            mixed_norm(NB - 1)
            residual(NB - 1)
            split_lo(U_UP + 1)
            normalise_x1(NB - 1)
            h2_modulate(1)
            h2_lo(1)

            def column(base, i, t):
                return cols[:, bass.ds(i * 2 + (base + t // 2 + FT * (t % 2)), 1)]

            def f_tile(k):
                return flat(big[:, bass.ds(k, 1), :])

            def up_taps(i, t):
                dst = f_tile(i * 2 + t // 2) if t % 2 else gate_t[:, t // 2, :]
                src = bank(2 * t, 2)
                dve.wait_ge(s_u0, i * 4 + (t + 1))
                dve.scalar_tensor_tensor(out=dst[:, 1:], in0=src[:, 0:T - 1], scalar=column(C_FFN + 44, i, t),
                                         in1=dst[:, 1:], op0=ALU.mult, op1=ALU.add).then_inc(s_uc, 1)
                dve.wait_ge(s_uc, i * 4 + (t + 1))
                dve.scalar_tensor_tensor(out=dst[:, 2:], in0=src[:, 0:T - 2], scalar=column(C_FFN, i, t),
                                         in1=dst[:, 2:], op0=ALU.mult, op1=ALU.add).then_inc(s_u1, 1)

            def up_gate(i, pr):
                dst = f_tile(i * 2 + pr)
                dve.wait_ge(s_ge, i * 2 + (pr + 1))
                dve.wait_ge(s_u1, i * 4 + (2 * pr + 2))
                dve.tensor_tensor(dst, dst, gate_t[:, pr, :], ALU.mult).then_inc(s_f, 1)

            def f_split_lo(half, kk, e):
                dve.wait_ge(s_fh, kk * 2 + (FT * half + e + 1))
                dve.tensor_tensor(a_lo[:, e, :], f_tile(kk * 2 + e), a_hi[:, e, :].bitcast(f32),
                                  ALU.subtract).then_inc(s_fl, 1)

            def up_body(i, first=False, last=False):
                for t in range(4):
                    if not (first and t == 0):
                        split_lo(U_UP + t + 1, i * 4)
                    if last and t == 3:
                        for e in range(2):
                            f_split_lo(0, 0, e)
                    up_taps(i, t)
                    if t % 2:
                        up_gate(i, t // 2)

            up_body(0, first=True)
            with dve.Fori(1, FT // 2 - 1) as i:
                up_body(i)
            up_body(FT // 2 - 1, last=True)

            def down_unit(half, kk0, dk, split_next=True):
                for e in range(2):
                    f_split_lo(half, dk + kk0, e)
                if split_next:
                    split_lo(U_DOWN + DOWN_UNITS * half + kk0 + 1, dk)

            for half in range(2):
                split_lo(U_DOWN + DOWN_UNITS * half + 1)
                with dve.Fori(0, 4) as i:
                    down_unit(half, 1, i * 2)
                    down_unit(half, 2, i * 2)
                if half == 0:
                    down_unit(half, 9, 0)
                    down_unit(half, 10, 0)
                    for e in range(2):
                        f_split_lo(1, 0, e)
                else:
                    for e in range(2):
                        dve.wait_ge(s_fh, 2 * FT - 3 + e)
                        dve.tensor_tensor(a_lo[:, 2 + e, :], f_tile(FT - 4 + e), a_hi[:, 2 + e, :].bitcast(f32),
                                          ALU.subtract).then_inc(s_fl, 1)
                    for b in range(NB):
                        dve.wait_ge(s_hq, b + 1)
                        dve.tensor_tensor(half0[:, b, :], half0[:, b, :], gate_rows[:, 1, 0:512],
                                          ALU.mult).then_inc(s_hg, 1)
                    f_split_lo(1, DOWN_UNITS - 1, 0)
                    split_lo(U_END - 1)
                    f_split_lo(1, DOWN_UNITS - 1, 1)

            dve.wait_ge(s_x1l, 16 * NB)
            dve.wait_ge(s_hg, NB)
            for b in range(NB):
                left, right = ring(raw, b)[:, 0:512], ring(raw, b)[:, 512:1024]
                dve.wait_ge(s_dq, b + 1)
                if b >= 2:
                    dve.wait_ge(s_out[b % 2], 16 * (b // 2))
                link(dve.tensor_tensor(right, bank(b), gate_rows[:, 1, 512:1024], ALU.mult))
                dve.wait_ge(s_dr, b + 1)
                for part, src, x1 in ((left, half0[:, b, :], x1_again(b)[:, 0:512]),
                                      (right, right, x1_again(b)[:, 512:1024])):
                    ins = dve.scalar_tensor_tensor(out=part, in0=src, scalar=st[:, 104 + b:105 + b], in1=x1,
                                                   op0=ALU.mult, op1=ALU.add)
                ins.then_inc(s_do, 1)

        @block.tensor
        def _(pe):
            pe.wait_ge(s_const, 48)

            def x_transpose(b):
                pe.wait_ge(s_xn, b + 1)
                if b >= 3:
                    pe.wait_ge(s_xe, b - 2)
                for k in range(KT):
                    mm = pe.transpose(bank(2 * (b % 3), 2)[:, k * P:(k + 1) * P],
                                      x_in(b)[:, k * P:(k + 1) * P], ident)
                mm.then_inc(s_xT, 1)

            x_transpose(0)
            x_transpose(1)
            pe.wait_ge(s_small, 16 * N_SMALL)
            c0 = 0
            for m, n in enumerate([N_MOD_ROWS, N_CONV_ROWS, N_FFN_ROWS, N_FFN_ROWS]):
                mm = pe.transpose(bank(7)[:, c0:c0 + n], rows[0:n, m, :], ident[0:n, 0:n])
                c0 += n
            mm.then_inc(s_rT, 1)
            pe.matmul(bank(6)[0:H, 0:EXT], rb_sb, hot_sb, start=True, stop=True).then_inc(s_ext, 1)

            def sum_columns(n, col):
                pe.wait_ge(s_acc, n + 1)
                for f in range(4):
                    src = n * 512 + f * P
                    mm = pe.matmul(bank(6)[:, col + f:col + f + 1], acc[:, src:src + P], ones[:, 0:1],
                                   start=True, stop=True)
                return mm

            def sum_gate(n, b):
                pe.matmul(bank(b), ones[:, :], acc[:, n * 512:(n + 1) * 512], start=True, stop=True)\
                    .then_inc(s_mp, 1)

            x_transpose(2)
            x_transpose(3)
            pe.wait_ge(s_pool, 2)
            pe.wait_ge(s_exs, 1)
            sum_columns(0, EXT)
            sum_columns(1, EXT + 4)
            x_transpose(4)
            sum_columns(2, EXT + 8)
            x_transpose(5)
            x_transpose(6)
            x_transpose(7)
            sum_columns(3, EXT + 12).then_inc(s_mp, 1)

            def split_products(outs, lhs_of, rhs_of, first, last):
                for p, (a, b) in enumerate(((0, 0), (0, 1), (1, 0))):
                    for j, out in enumerate(outs):
                        mm = pe.matmul(out, lhs_of[a], rhs_of(b, j), start=first and p == 0, stop=last and p == 2)
                return mm

            def features(banks, u, halves=(0, 1), before=None, after=None):
                for k in range(KT):
                    if before:
                        before(k)
                    cs = slice(k * P, (k + 1) * P)
                    mm = split_products(
                        [bank(banks + hf) for hf in halves], (ring(w_hi, u)[:, cs], ring(w_lo, u)[:, cs]),
                        lambda b, j: (a_hi, a_lo)[b][:, k, halves[j] * 512:(halves[j] + 1) * 512],
                        k == 0, k == KT - 1)
                    if after:
                        after(k, mm)
                return mm

            def bank_free(n):
                m = n - 2
                if m in CONV:
                    pe.wait_ge(s_evD, CONV_BY_TIME.index(m) + 1)
                elif m == U_DT:
                    pe.wait_ge(s_dtT, 1)
                elif m >= Z:
                    pe.wait_ge(s_z0, m - Z + 1)
                elif m >= 0:
                    pe.wait_ge(s_evA, m + 1)

            def score(u):
                i, j = u // NPAIR, u % NPAIR
                if u >= 1:
                    pe.wait_ge(s_sb, u)
                else:
                    pe.wait_ge(s_mod, 6)
                k0, w = (P, 1) if i == 0 else (0, 2)
                for e in range(2):
                    rs = slice(e * HD, (e + 1) * HD)
                    mm = pe.matmul(bank(4 + e)[:, k0:2 * P], blk(Q + j, i)[rs],
                                   blk(K, i + 1 - w, w)[rs], start=True, stop=True)
                mm.then_inc(s_S, 1)

            def probs_transpose(u):
                i = u // NPAIR
                pe.wait_ge(s_p, u + 1)
                if u >= 1:
                    pe.wait_ge(s_pe, u)
                else:
                    pe.wait_ge(s_v, 1)
                for e in range(2):
                    for kb in range(1 if i == 0 else 0, 2):
                        at = (2 * e + kb) * P
                        mm = pe.transpose(bank(6)[:, at:at + P], prob[:, u % 2, e, kb * P:(kb + 1) * P], ident)
                mm.then_inc(s_pT, 1)

            def values(u):
                i, j = u // NPAIR, u % NPAIR
                pe.wait_ge(s_pe, u + 1)
                if j == 0 and i >= 1:
                    pe.wait_ge(s_o, i)
                for e in range(2):
                    h = j + 4 * e
                    k0 = 1 if i == 0 else 0
                    for kb in range(k0, 2):
                        at = (u % 2) * 512 + (2 * e + kb) * P
                        mm = pe.matmul(bank(7)[:, h * HD:(h + 1) * HD], probT[:, at:at + P],
                                       blk(V, i - 1 + kb)[:, e * HD:(e + 1) * HD],
                                       start=(kb == k0), stop=(kb == 1))
                mm.then_inc(s_pv, 1)

            def bias_flip():
                pe.wait_ge(s_bl, 32)
                pe.wait_ge(s_mod, 1)
                for j in range(NPAIR):
                    pe.matmul(bank(4 + j), flip, bias[:, j], start=True, stop=True).then_inc(s_flp, 1)

            def v_transpose():
                pe.wait_ge(s_evA, V + 1)
                pe.wait_ge(s_mod, 4)
                for i in range(NB):
                    mm = pe.transpose(bank(6, 2)[:, i * P:(i + 1) * P], blk(V, i), ident)
                mm.then_inc(s_vT, 1)

            def dt_transpose():
                pe.wait_ge(s_dtT, 1)
                pe.wait_ge(s_sb, 3 * (U_DT + 1 - A0) + 1)
                for b in range(NB):
                    mm = pe.transpose(bank(5)[:, 256 + 16 * b:272 + 16 * b], dt_rows[:, b * P:(b + 1) * P],
                                      ident[0:16, 0:16])
                mm.then_inc(s_dtn, 1)

            def dt_sum():
                pe.wait_ge(s_dte, 1)
                pe.wait_ge(s_sb, 3 * (U_DT + 2 - A0) + 1)
                for v, m in enumerate((upper, strict, ones[:, :])):
                    mm = pe.matmul(bank(5)[:, 256 + 64 * v:320 + 64 * v], m, dtv[:, ADT, :], start=True, stop=True)
                mm.then_inc(s_dtc, 1)

            def transpose_four(dst, src):
                for t in range(4):
                    mm = pe.transpose(bank(dst)[:, t * P:(t + 1) * P], src[:, t, :], ident)
                return mm

            def rows_and_b(i):
                if i == 0:
                    pe.wait_ge(s_si, len(CONV))
                    pe.wait_ge(s_sb, N_PAIRS)
                else:
                    pe.wait_ge(s_bn, i)
                for g in range(GROUPS):
                    mm = pe.transpose(bank(4)[:, g * P:(g + 1) * P], blk(BB + g, i), ident)
                mm.then_inc(s_t1, 1)
                if i == 0:
                    pe.wait_ge(s_pe, N_PAIRS)
                else:
                    pe.wait_ge(s_yb, i)
                transpose_four(6, four(XS, i)).then_inc(s_xsT, 1)

            def cb_and_first_sums(i):
                if i == 0:
                    pe.wait_ge(s_o, NB)
                else:
                    pe.wait_ge(s_su, i)
                for g in range(GROUPS):
                    mm = pe.matmul(bank(7)[:, g * P:(g + 1) * P], blk(BB + g, i), blk(CC + g, i),
                                   start=True, stop=True)
                mm.then_inc(s_cb, 1)
                if i >= 1:
                    pe.wait_ge(s_g, i)
                pe.wait_ge(s_rd, 2 * i + 1)
                pe.matmul(bank(5), strict, decay[:, 0, :], start=True, stop=True).then_inc(s_D, 1)

            def second_sums(i):
                pe.wait_ge(s_cbm, i + 1)
                pe.wait_ge(s_rd, 2 * i + 2)
                pe.matmul(bank(7), strict, decay[:, 1, :], start=True, stop=True).then_inc(s_D, 1)

            def beside(n):
                u = 3 * (n - A0)
                steps = {0: [(score, u), (probs_transpose, u - 2)],
                         2: [(values, u - 2)],
                         3: [(score, u + 1), (probs_transpose, u - 1)],
                         5: [(probs_transpose, u), (values, u - 1)],
                         6: [(score, u + 2)],
                         7: [(values, u)]}

                def before(k):
                    if n == 0:
                        pe.wait_ge(s_hlo, k + 1)
                    if n == 1 and k == 2:
                        bias_flip()
                    if n == V + 1 and k == 2:
                        pe.wait_ge(s_acc, 12)
                        for half in range(2):
                            sum_gate(10 + half, GATE_BANKS[2 + half])
                    if n == V + 1 and k == 4:
                        v_transpose()
                    if n == U_DT + 1 and k == 3:
                        dt_transpose()
                    if n == U_DT + 2 and k == 3:
                        dt_sum()
                    if n == U_OUT - 1 and k == 4:
                        rows_and_b(0)
                    if n == U_OUT - 1 and k == 6:
                        cb_and_first_sums(0)
                    if n >= A0:
                        for step, v in steps.get(k, []):
                            if 0 <= v < N_PAIRS:
                                step(v)
                return before

            for n in range(U_OUT):
                pe.wait_ge(s_wlo, n + 1)
                if n == 0:
                    pe.wait_ge(s_xe, NB)
                bank_free(n)
                if n == U_DT:
                    before = beside(n)
                    for k in range(KT):
                        before(k)
                        w = ring(w_hi, U_DT)[:, k * P:(k + 1) * P]
                        for m, moving in enumerate((a_hi, a_lo)):
                            for hf in range(2):
                                mm = pe.matmul(bank(hf), w, moving[:, k, hf * 512:(hf + 1) * 512],
                                               start=(k == 0 and m == 0), stop=(k == KT - 1 and m == 1))
                    mm.then_inc(s_wu, 1)
                else:
                    features(2 * (n % 2), n, before=beside(n)).then_inc(s_wu, 1)
                if n == 3:
                    pe.wait_ge(s_acc, 6)
                    pe.wait_ge(s_bias, NPAIR)
                    for half in range(2):
                        sum_gate(4 + half, GATE_BANKS[half])
                if n == 4:
                    for c in range(4):
                        mm = sum_columns(6 + c, EXT + 16 + 4 * c)
                    mm.then_inc(s_mp, 1)

            def project_out(b, ks):
                u = U_OUT + b
                if ks[0] == 0:
                    pe.wait_ge(s_mh, b + 1)
                    pe.wait_ge(s_ml, b + 1)
                    if 1 <= b < NB - 1:
                        pe.wait_ge(s_mf, b)
                for k in ks:
                    if b == 0:
                        pe.wait_ge(s_wlo, U_OUT + k + 1)
                    cs = slice(k * P, (k + 1) * P)
                    mm = split_products([bank(out_bank(b) + hf) for hf in range(2)],
                                        (ring(w_hi, u)[:, cs], ring(w_lo, u)[:, cs]),
                                        lambda s, j: (a_hi, a_lo)[s][:, k, j * 512:(j + 1) * 512],
                                        k == 0, k == KT - 1)
                    if b == NB - 1 and k < KT - 1:
                        mm.then_inc(s_wr, 1)
                if ks[-1] == KT - 1:
                    mm.then_inc(s_wu, 1)

            def x1_transpose(b):
                pe.wait_ge(s_n2, b + 1)
                for k in range(KT):
                    mm = pe.transpose(bank(4 if b == NB - 1 else 2, 2)[:, k * P:(k + 1) * P],
                                      xn2[:, b % 2, k * P:(k + 1) * P], ident)
                mm.then_inc(s_T2, 1)

            def mixed_transpose(b):
                pe.wait_ge(s_my, b + 1)
                if b >= 2:
                    pe.wait_ge(s_e2, b - 1)
                transpose_four(2, four(Q, b))
                transpose_four(3, four(Z, b)).then_inc(s_mT, 1)

            pe.wait_ge(s_z0, 4)
            for i in range(NB + 1):
                if 1 <= i < NB:
                    rows_and_b(i)
                    cb_and_first_sums(i)
                if i == 1:
                    mixed_transpose(0)
                if 2 <= i < NB:
                    project_out(i - 2, range(6, KT))
                if i < NB:
                    second_sums(i)
                if i == NB:
                    project_out(i - 2, range(4, 6))
                if i >= 2:
                    mixed_transpose(i - 1)
                if i == NB:
                    project_out(i - 2, range(6, KT))
                if i < NB:
                    pe.wait_ge(s_E, 2 * i + 1)
                    if i == 0:
                        pe.wait_ge(s_pc, NB + 1)
                    for g in range(GROUPS):
                        mm = pe.matmul(bank(5)[:, g * 256:(g + 1) * 256], blk(CC + g, i),
                                       state[:, g * 256:(g + 1) * 256], start=True, stop=True)
                    mm.then_inc(s_yo, 1)
                    pe.wait_ge(s_xc, i + 1)
                    pe.wait_ge(s_W, 2 * i + 2)
                    for h in range(H):
                        mm = pe.matmul(bank(6)[:, h * HD:(h + 1) * HD], decay[:, h // 4, (h % 4) * P:(h % 4 + 1) * P],
                                       xc[:, h * HD:(h + 1) * HD], start=True, stop=True)
                    mm.then_inc(s_yd, 1)
                if i >= 1:
                    project_out(i - 1, range(0, 2))
                if i < NB:
                    pe.wait_ge(s_bn, i + 1)
                    for g in range(GROUPS):
                        mm = pe.matmul(bank(7)[:, g * 256:(g + 1) * 256], bn[:, g, :],
                                       xc_end[:, g * 256:(g + 1) * 256], start=True, stop=True)
                    mm.then_inc(s_sn, 1)
                if i >= 1:
                    project_out(i - 1, range(2, 4))
                if i < NB:
                    if i == 0:
                        pe.wait_ge(s_si, len(SILU))
                    pe.wait_ge(s_ya, i + 1)
                    transpose_four(5, four(Z, i)).then_inc(s_zT, 1)
                if 1 <= i < NB - 1:
                    project_out(i - 1, range(4, 6))
                if 2 <= i < NB:
                    x1_transpose(i - 2)
                if i == NB:
                    project_out(i - 1, range(4, 6))
                    x1_transpose(i - 2)
                    project_out(i - 1, range(6, KT))

            def up_tile(i, t):
                pe.wait_ge(s_wlo, i * 4 + (U_UP + t + 1))
                pe.wait_ge(s_u1, i * 4 + (t - 3))
                features(2 * t, U_UP + t).then_inc(s_wu, 1)

            def h2_ready(hf):
                return lambda k: pe.wait_ge(s_h2l, KT * hf + k + 1)

            pe.wait_ge(s_mf, NB - 1)
            pe.wait_ge(s_wlo, U_UP + 1)
            features(0, U_UP, (0,), before=h2_ready(0))
            pe.wait_ge(s_wlo, U_UP + 2)
            pe.wait_ge(s_e2, NB - 1)
            features(2, U_UP + 1, (0,), before=lambda k: x1_transpose(NB - 1) if k == 2 else None)
            features(0, U_UP, (1,), before=h2_ready(1)).then_inc(s_wu, 1)
            features(2, U_UP + 1, (1,)).then_inc(s_wu, 1)
            for t in range(2, 4):
                pe.wait_ge(s_wlo, U_UP + t + 1)
                if t == 2:
                    pe.wait_ge(s_e2, NB)
                else:
                    pe.wait_ge(s_mf, NB)
                features(2 * t, U_UP + t).then_inc(s_wu, 1)
            with pe.Fori(1, FT // 2 - 1) as i:
                for t in range(4):
                    up_tile(i, t)
            for t in range(3):
                up_tile(FT // 2 - 1, t)
            pe.wait_ge(s_wlo, U_DOWN)
            pe.wait_ge(s_u1, 2 * FT - 4)
            features(6, U_DOWN - 1, after=lambda k, mm: mm.then_inc(s_ah, 1) if k < 2 else None).then_inc(s_wu, 1)

            def row_products(u, e, first, last, per_bank=None, done=None):
                ws = slice(e * 512, (e + 1) * 512)
                for b in range(NB):
                    if per_bank:
                        per_bank(b)
                    ts = slice(b * P, (b + 1) * P)
                    mm = split_products([bank(b)], (a_hi[:, e, ts], a_lo[:, e, ts]),
                                        lambda s, j: ring((w_hi, w_lo)[s], u)[:, ws], first, last)
                    if done is not None and b < NB - 1:
                        mm.then_inc(done, 1)
                return mm

            def down_unit(half, kk0, dk):
                u = U_DOWN + DOWN_UNITS * half + kk0
                pe.wait_ge(s_wlo, dk + (u + 1))
                for e in range(2):
                    q = FT * half + 2 * kk0 + e
                    pe.wait_ge(s_fl, dk * 2 + (q + 1))
                    first, last = kk0 == 0 and e == 0, kk0 == DOWN_UNITS - 1 and e == 1
                    bank_ready = None
                    if first and half == 0:
                        def bank_ready(b):
                            pe.wait_ge(s_u1, 2 * FT - 4 + b // 2 + 1)
                    if first and half == 1:
                        def bank_ready(b):
                            pe.wait_ge(s_d0, b + 1)
                    mm = row_products(u, e, first, last, bank_ready, s_dn if last else None)
                    if e == 0:
                        mm.then_inc(s_fu, 1)
                mm.then_inc(s_wu, 1)

            for half in range(2):
                down_unit(half, 0, 0)
                with pe.Fori(0, 4) as i:
                    down_unit(half, 1, i * 2)
                    down_unit(half, 2, i * 2)
                if half == 0:
                    down_unit(half, 9, 0)
                    down_unit(half, 10, 0)

            for b in range(NB):
                ts = slice(b * P, (b + 1) * P)
                for n in range(4):
                    u, ws = U_END - 2 + n // 2, slice((n % 2) * 512, (n % 2 + 1) * 512)
                    if b == 0:
                        pe.wait_ge(s_wlo, u + 1)
                        pe.wait_ge(s_fl, 2 * FT - 3 + n)
                    at = (n + 2) % 4
                    mm = split_products([bank(b)], (a_hi[:, at, ts], a_lo[:, at, ts]),
                                        lambda s, j: ring((w_hi, w_lo)[s], u)[:, ws], False, n == 3)
                    if b == NB - 1 and n % 2:
                        mm.then_inc(s_wu, 1)
                if b < NB - 1:
                    mm.then_inc(s_dn, 1)


_INS = ["x", "c", "rel_bias", "w_ada", "b_ada", "pre_mix_w", "w_in", "attn_sinks", "ssm_conv_w", "ssm_conv_b",
        "ssm_dt_bias", "ssm_a_log", "ssm_d", "ssm_norm_w", "w_out", "post_mix_w", "pre_ffn_w", "w_up",
        "ffn_conv_w", "ffn_conv_b", "w_down", "post_ffn_w"]


def kernel(**inputs):
    import concourse.bacc as _bacc
    from concourse.bass_utils import run_bass_kernel_spmd as _run

    nc = _bacc.Bacc("TRN2", target_bir_lowering=False, num_devices=1)
    arrays, args = {}, []
    named = [(name, np.ascontiguousarray(inputs[name])) for name in _INS]
    named += list(zip(("squares", "hot"), shape_constants()))
    for name, a in named:
        arrays[f"in_{name}_dram"] = a
        args.append(nc.dram_tensor(f"in_{name}_dram", a.shape, mybir.dt.from_np(a.dtype), kind="ExternalInput").ap())
    args.append(nc.dram_tensor("out_dram", (1, T, D), mybir.dt.float32, kind="ExternalOutput").ap())
    hybrid_layer_kernel(nc, *args)
    r = _run(nc, [arrays], core_ids=[0])
    return r.results[0]["out_dram"]
```
